# Optimizing a Trainium2 kernel written in Bass

```python
import jax, jax.numpy as jnp
from jax import lax
import numpy as np
import math
import jax
import jax.numpy as jnp

D_MODEL = 1024
BATCH = 1
SEQ = 512
DEPTH = 2

N_EVEN = (DEPTH + 1) // 2
N_ODD = DEPTH // 2
CHUNK = 64
EPS = 1e-6
RET_HEADS = 4
RET_DV = D_MODEL // 2 // RET_HEADS
RET_DK = RET_DV
ROPE_BASE = 10000.0
GLA_HEADS = 4
GLA_DV = D_MODEL // 2 // GLA_HEADS
GLA_DK = GLA_DV // 2
GLA_RANK = 16
GLA_TAU = 16.0
AB_SIZES = (RET_HEADS * RET_DK, RET_HEADS * RET_DK, RET_HEADS * RET_DV, RET_HEADS * RET_DV,
            GLA_HEADS * GLA_DK, GLA_HEADS * GLA_DK, GLA_HEADS * GLA_DV, GLA_HEADS * GLA_DV,
            GLA_RANK)
AB_IN = sum(AB_SIZES)
HGRN_DK = 128
HGRN_HEADS = D_MODEL // HGRN_DK
HGRN_DV = D_MODEL // HGRN_HEADS
C_IN = 4 * D_MODEL
D_FF = ((8 * D_MODEL // 3 + 255) // 256) * 256
N_EXPERTS = 8
TOP_K = 2
EXPERT_FF = 7 * D_MODEL // 2
OUT_SCALE = (2 * DEPTH) ** -0.5


def rms_norm(x, g):
    xf = x.astype(jnp.float32)
    y = xf * lax.rsqrt(jnp.mean(xf * xf, axis=-1, keepdims=True) + EPS)
    return (y * g.astype(jnp.float32)).astype(x.dtype)

def rotary(x, positions):
    d = x.shape[-1]
    inv_freq = ROPE_BASE ** (-jnp.arange(0, d, 2, dtype=jnp.float32) / d)
    ang = positions.astype(jnp.float32)[..., None, None] * inv_freq
    cos, sin = jnp.cos(ang), jnp.sin(ang)
    xf = x.astype(jnp.float32)
    x1, x2 = xf[..., : d // 2], xf[..., d // 2:]
    return jnp.concatenate([x1 * cos - x2 * sin, x2 * cos + x1 * sin], axis=-1)

def _to_chunks(a):
    b, t, h, d = a.shape
    return a.reshape(b, t // CHUNK, CHUNK, h, d).transpose(1, 0, 3, 2, 4)

def _from_chunks(a):
    nc, b, h, c, d = a.shape
    return a.transpose(1, 0, 3, 2, 4).reshape(b, nc * c, h, d)

def _causal_mask():
    t = jnp.arange(CHUNK)
    return t[:, None] >= t[None, :]

def retention_chunkwise(q, k, v, log_gamma):
    b, _, h, dk = q.shape
    dv = v.shape[-1]
    t = jnp.arange(CHUNK, dtype=jnp.float32)
    lg = log_gamma.astype(jnp.float32)
    rel = t[:, None] - t[None, :]
    intra_decay = jnp.exp(jnp.where(_causal_mask()[None], rel[None] * lg[:, None, None], -jnp.inf))
    q_decay = jnp.exp((t[None, :] + 1.0) * lg[:, None])[..., None]
    k_decay = jnp.exp((CHUNK - 1.0 - t[None, :]) * lg[:, None])[..., None]
    chunk_decay = jnp.exp(CHUNK * lg)[:, None, None]

    def step(state, inp):
        qc, kc, vc = inp
        scores = jnp.einsum('bhid,bhjd->bhij', qc, kc) * intra_decay
        o = (jnp.einsum('bhij,bhjv->bhiv', scores, vc)
             + jnp.einsum('bhid,bhdv->bhiv', qc * q_decay, state))
        state = chunk_decay * state + jnp.einsum('bhjd,bhjv->bhdv', kc * k_decay, vc)
        return state, o

    s0 = jnp.zeros((b, h, dk, dv), jnp.float32)
    _, o = lax.scan(step, s0, (_to_chunks(q), _to_chunks(k), _to_chunks(v)))
    return _from_chunks(o)

def gated_chunkwise(q, k, v, log_f):
    b, _, h, dk = q.shape
    dv = v.shape[-1]
    mask = _causal_mask()[:, :, None]
    g_cum = jnp.cumsum(_to_chunks(log_f), axis=-2)

    def step(state, inp):
        qc, kc, vc, gc = inp
        diff = gc[:, :, :, None, :] - gc[:, :, None, :, :]
        decay = jnp.exp(jnp.where(mask, diff, -jnp.inf))
        scores = jnp.einsum('bhid,bhjd,bhijd->bhij', qc, kc, decay)
        g_last = gc[:, :, -1:, :]
        o = (jnp.einsum('bhij,bhjv->bhiv', scores, vc)
             + jnp.einsum('bhid,bhdv->bhiv', qc * jnp.exp(gc), state))
        state = (jnp.exp(g_last[:, :, 0, :])[..., None] * state
                 + jnp.einsum('bhjd,bhjv->bhdv', kc * jnp.exp(g_last - gc), vc))
        return state, o

    s0 = jnp.zeros((b, h, dk, dv), jnp.float32)
    _, o = lax.scan(step, s0, (_to_chunks(q), _to_chunks(k), _to_chunks(v), g_cum))
    return _from_chunks(o)

def retnet_gla_mixer(h, positions, w_in, w_a2, b_a2, ret_g, gla_g, w_out):
    b, t, _ = h.shape
    z = h @ w_in
    aq, ak, av, ag, bq, bk, bv, bg, ba = jnp.split(z, np.cumsum(AB_SIZES)[:-1], axis=-1)
    f32 = jnp.float32

    def heads(a, n):
        return a.reshape(b, t, n, -1).astype(f32)

    qa = rotary(heads(aq, RET_HEADS), positions)
    ka = rotary(heads(ak, RET_HEADS), positions) * (RET_DK ** -0.5)
    log_gamma = jnp.log1p(-jnp.exp2(-5.0 - jnp.arange(RET_HEADS, dtype=f32)))
    oa = retention_chunkwise(qa, ka, heads(av, RET_HEADS), log_gamma)
    oa = rms_norm(oa, ret_g) * jax.nn.silu(heads(ag, RET_HEADS))
    log_alpha = jax.nn.log_sigmoid((ba @ w_a2 + b_a2).astype(f32)) / GLA_TAU
    ob = gated_chunkwise(heads(bq, GLA_HEADS) * (GLA_DK ** -0.5), heads(bk, GLA_HEADS),
                         heads(bv, GLA_HEADS), heads(log_alpha, GLA_HEADS))
    ob = rms_norm(ob, gla_g) * jax.nn.silu(heads(bg, GLA_HEADS))
    o = jnp.concatenate([oa.reshape(b, t, -1), ob.reshape(b, t, -1)], axis=-1)
    return o.astype(h.dtype) @ w_out

def hgrn2_mixer(h, lb, w_in, norm_g, w_out):
    b, t, d = h.shape
    f32 = jnp.float32
    q, f, i, g = jnp.split(h @ w_in, 4, axis=-1)

    def heads(a):
        return a.reshape(b, t, HGRN_HEADS, -1).astype(f32)

    f = heads(f)
    lb = lb.astype(f32)
    log_f = jnp.logaddexp(jnp.log(lb), jnp.log1p(-lb) + jax.nn.log_sigmoid(f))
    k = (1.0 - lb) * jax.nn.sigmoid(-f)
    qh = jax.nn.silu(heads(q)) * (HGRN_DK ** -0.5)
    o = gated_chunkwise(qh, k, heads(i), log_f)
    o = rms_norm(o, norm_g) * jax.nn.silu(heads(g))
    return o.reshape(b, t, d).astype(h.dtype) @ w_out

def swiglu(h, w_gate, w_up, w_down):
    return (jax.nn.silu(h @ w_gate) * (h @ w_up)) @ w_down

def moe_swiglu(h, w_router, w_gate, w_up, w_down):
    b, t, d = h.shape
    xt = h.reshape(b * t, d)
    logits = (xt @ w_router).astype(jnp.float32)
    top_logits, top_idx = lax.top_k(logits, TOP_K)
    gates = jax.nn.softmax(top_logits, axis=-1)
    flat_e = top_idx.reshape(-1)
    order = jnp.argsort(flat_e)
    group_sizes = jnp.bincount(flat_e, length=N_EXPERTS).astype(jnp.int32)
    xs = xt[order // TOP_K]
    hid = (jax.nn.silu(lax.ragged_dot(xs, w_gate, group_sizes))
           * lax.ragged_dot(xs, w_up, group_sizes))
    ys = lax.ragged_dot(hid, w_down, group_sizes)
    y = jnp.zeros_like(ys).at[order].set(ys).reshape(b * t, TOP_K, d)
    out = jnp.einsum('nk,nkd->nd', gates.astype(y.dtype), y)
    return out.reshape(b, t, d)

def first_inputs(seed: int = 0) -> dict:
    key = jax.random.key(seed)
    ks = jax.random.split(key, 24)
    f32 = jnp.float32

    def nrm(k, shape, scale):
        return jax.random.normal(k, shape, f32) * scale

    def gain(k, shape):
        return 1.0 + 0.02 * jax.random.normal(k, shape, f32)

    ds = D_MODEL ** -0.5
    return {
        "x": nrm(ks[0], (BATCH, SEQ, D_MODEL), 1.0),
        "positions": jnp.broadcast_to(jnp.arange(SEQ, dtype=jnp.int32), (BATCH, SEQ)),
        "norm_mix_g": gain(ks[1], (DEPTH, D_MODEL)),
        "norm_ffn_g": gain(ks[2], (DEPTH, D_MODEL)),
        "final_norm_g": gain(ks[3], (D_MODEL,)),
        "ab_w_in": nrm(ks[4], (N_EVEN, D_MODEL, AB_IN), ds),
        "gla_w_a2": nrm(ks[5], (N_EVEN, GLA_RANK, GLA_HEADS * GLA_DK), GLA_RANK ** -0.5),
        "gla_b_a2": nrm(ks[6], (N_EVEN, GLA_HEADS * GLA_DK), 0.1),
        "ret_norm_g": gain(ks[7], (N_EVEN, RET_DV)),
        "gla_norm_g": gain(ks[8], (N_EVEN, GLA_DV)),
        "ab_w_out": nrm(ks[9], (N_EVEN, D_MODEL, D_MODEL), ds * OUT_SCALE),
        "ffn_w_gate": nrm(ks[10], (N_EVEN, D_MODEL, D_FF), ds),
        "ffn_w_up": nrm(ks[11], (N_EVEN, D_MODEL, D_FF), ds),
        "ffn_w_down": nrm(ks[12], (N_EVEN, D_FF, D_MODEL), D_FF ** -0.5 * OUT_SCALE),
        "hgrn_lb_logits": nrm(ks[13], (DEPTH, HGRN_HEADS * HGRN_DK), 0.1),
        "c_w_in": nrm(ks[14], (N_ODD, D_MODEL, C_IN), ds),
        "hgrn_norm_g": gain(ks[15], (N_ODD, HGRN_DV)),
        "c_w_out": nrm(ks[16], (N_ODD, D_MODEL, D_MODEL), ds * OUT_SCALE),
        "moe_router": nrm(ks[17], (N_ODD, D_MODEL, N_EXPERTS), ds),
        "moe_w_gate": nrm(ks[18], (N_ODD, N_EXPERTS, D_MODEL, EXPERT_FF), ds),
        "moe_w_up": nrm(ks[19], (N_ODD, N_EXPERTS, D_MODEL, EXPERT_FF), ds),
        "moe_w_down": nrm(ks[20], (N_ODD, N_EXPERTS, EXPERT_FF, D_MODEL), EXPERT_FF ** -0.5 * OUT_SCALE),
    }

def first_block(x, positions, norm_mix_g, norm_ffn_g, final_norm_g, ab_w_in, gla_w_a2, gla_b_a2,
              ret_norm_g, gla_norm_g, ab_w_out, ffn_w_gate, ffn_w_up, ffn_w_down,
              hgrn_lb_logits, c_w_in, hgrn_norm_g, c_w_out, moe_router, moe_w_gate,
              moe_w_up, moe_w_down):
    lb_cum = jnp.cumsum(jax.nn.softmax(hgrn_lb_logits.astype(jnp.float32), axis=0), axis=0)
    lower_bounds = lb_cum - lb_cum[0:1]
    h = x
    for l in range(DEPTH):
        e = l // 2
        hn = rms_norm(h, norm_mix_g[l])
        if l % 2 == 0:
            h = h + retnet_gla_mixer(hn, positions, ab_w_in[e], gla_w_a2[e], gla_b_a2[e],
                                     ret_norm_g[e], gla_norm_g[e], ab_w_out[e])
            h = h + swiglu(rms_norm(h, norm_ffn_g[l]), ffn_w_gate[e], ffn_w_up[e], ffn_w_down[e])
        else:
            lb = lower_bounds[l].reshape(HGRN_HEADS, HGRN_DK)
            h = h + hgrn2_mixer(hn, lb, c_w_in[e], hgrn_norm_g[e], c_w_out[e])
            h = h + moe_swiglu(rms_norm(h, norm_ffn_g[l]), moe_router[e], moe_w_gate[e],
                               moe_w_up[e], moe_w_down[e])
    return rms_norm(h, final_norm_g)


DEPTH_2 = 1

N_HEADS_A = 8
HEAD_DIM_A = 64
ROPE_DIM_A = HEAD_DIM_A // 4
NOPE_DIM_A = HEAD_DIM_A - ROPE_DIM_A
KV_RANK = 128
IDX_HEADS = 8
IDX_DIM = 32
IDX_ROPE_DIM = IDX_DIM // 4
TOPK_MAX = 256
N_HEADS_B = 8
HEAD_DIM_B = 64
WIDTH_A = N_HEADS_A * HEAD_DIM_A
WIDTH_B = N_HEADS_B * HEAD_DIM_B
MIX_WIDTH = WIDTH_A + WIDTH_B
Q_BLOCK = 128
ROPE_THETA = 500000.0
PEER_HEADS = 8
N_KEYS = 128
N_EXPERTS_2 = N_KEYS * N_KEYS
PEER_KEY_DIM = 128
PEER_TOPK = 16
PEER_CHUNK = 128
IN_SIZES = (WIDTH_A, KV_RANK, ROPE_DIM_A, IDX_HEADS * IDX_DIM, IDX_DIM, IDX_HEADS,
            WIDTH_B, WIDTH_B, WIDTH_B, N_HEADS_B)
IN_COLS = sum(IN_SIZES)


def rms_norm_2(x, g):
    xf = x.astype(jnp.float32)
    y = xf * lax.rsqrt(jnp.mean(xf * xf, axis=-1, keepdims=True) + EPS)
    return (y * g.astype(jnp.float32)).astype(x.dtype)

def rope_tables(pos, rot_dim):
    inv = ROPE_THETA ** (-jnp.arange(0, rot_dim, 2, dtype=jnp.float32) / rot_dim)
    ang = pos.astype(jnp.float32)[..., None] * inv
    return jnp.cos(ang), jnp.sin(ang)

def apply_partial_rope(x, cos, sin):
    half = cos.shape[-1]
    cos = cos.astype(x.dtype)
    sin = sin.astype(x.dtype)
    x1 = x[..., :half]
    x2 = x[..., half:2 * half]
    return jnp.concatenate([x1 * cos - x2 * sin, x2 * cos + x1 * sin, x[..., 2 * half:]], axis=-1)

def to_blocks(a):
    b, s = a.shape[:2]
    return a.reshape(b, s // Q_BLOCK, Q_BLOCK, *a.shape[2:]).swapaxes(0, 1)

def from_blocks(a):
    nb, b, q = a.shape[:3]
    return a.swapaxes(0, 1).reshape(b, nb * q, *a.shape[3:])

def dsa_attention(q, latent, k_rope, iq, ik, iw, cos_a, sin_a, cos_i, sin_i, w_uk, w_uv):
    b, s = q.shape[:2]
    topk = min(TOPK_MAX, s // 4)
    q = apply_partial_rope(q, cos_a[:, :, None], sin_a[:, :, None])
    q_rope, q_nope = q[..., :ROPE_DIM_A], q[..., ROPE_DIM_A:]
    k_rope = apply_partial_rope(k_rope, cos_a, sin_a)
    q_lat = jnp.einsum('bshn,rhn->bshr', q_nope, w_uk)
    iq = apply_partial_rope(iq, cos_i[:, :, None], sin_i[:, :, None])
    ik = apply_partial_rope(ik, cos_i, sin_i)
    key_pos = jnp.arange(s)
    t_blocks = key_pos.reshape(s // Q_BLOCK, Q_BLOCK)
    gather_rows = jax.vmap(lambda table, ids: table[ids])
    scale = HEAD_DIM_A ** -0.5

    def block(args):
        q_lat_b, q_rope_b, iq_b, iw_b, t_b = args
        dots = jnp.einsum('bqhd,bsd->bqhs', iq_b, ik,
                          preferred_element_type=jnp.float32) * (IDX_DIM ** -0.5)
        w_h = iw_b.astype(jnp.float32) * (IDX_HEADS ** -0.5)
        score = jnp.einsum('bqhs,bqh->bqs', jax.nn.relu(dots), w_h)
        causal = key_pos[None, :] <= t_b[:, None]
        score = jnp.where(causal[None], score, -jnp.inf)
        _, sel = lax.top_k(score, topk)
        valid = sel <= t_b[None, :, None]
        lat_s = gather_rows(latent, sel)
        kr_s = gather_rows(k_rope, sel)
        logits = (jnp.einsum('bqhr,bqkr->bqhk', q_lat_b, lat_s, preferred_element_type=jnp.float32)
                  + jnp.einsum('bqhd,bqkd->bqhk', q_rope_b, kr_s, preferred_element_type=jnp.float32)) * scale
        logits = jnp.where(valid[:, :, None, :], logits, -jnp.inf)
        p = jax.nn.softmax(logits, axis=-1).astype(lat_s.dtype)
        return jnp.einsum('bqhk,bqkr->bqhr', p, lat_s)

    o = lax.map(block, (to_blocks(q_lat), to_blocks(q_rope), to_blocks(iq), to_blocks(iw), t_blocks))
    o = from_blocks(o)
    return jnp.einsum('bshr,rhd->bshd', o, w_uv).reshape(b, s, WIDTH_A)

def forgetting_attention(q, k, v, f_logit):
    b, s = q.shape[:2]
    cum = jnp.cumsum(jax.nn.log_sigmoid(f_logit.astype(jnp.float32)), axis=1)
    cum_k = cum.transpose(0, 2, 1)
    key_pos = jnp.arange(s)
    t_blocks = key_pos.reshape(s // Q_BLOCK, Q_BLOCK)
    scale = HEAD_DIM_B ** -0.5

    def block(args):
        q_b, cum_b, t_b = args
        logits = jnp.einsum('bqhd,bshd->bhqs', q_b, k, preferred_element_type=jnp.float32) * scale
        logits = logits + cum_b.transpose(0, 2, 1)[..., None] - cum_k[:, :, None, :]
        causal = key_pos[None, :] <= t_b[:, None]
        logits = jnp.where(causal, logits, -jnp.inf)
        p = jax.nn.softmax(logits, axis=-1).astype(v.dtype)
        return jnp.einsum('bhqs,bshd->bqhd', p, v)

    o = from_blocks(lax.map(block, (to_blocks(q), to_blocks(cum), t_blocks)))
    return o.reshape(b, s, WIDTH_B)

def peer_ffn(h, w_q, keys1, keys2, u, v):
    b, s, d = h.shape
    half = PEER_KEY_DIM // 2
    k1 = keys1.astype(jnp.float32)
    k2 = keys2.astype(jnp.float32)

    def chunk(hc):
        q = (hc @ w_q).reshape(-1, PEER_HEADS, PEER_KEY_DIM).astype(jnp.float32)
        s1 = jnp.einsum('chd,nd->chn', q[..., :half], k1)
        s2 = jnp.einsum('chd,nd->chn', q[..., half:], k2)
        v1, i1 = lax.top_k(s1, PEER_TOPK)
        v2, i2 = lax.top_k(s2, PEER_TOPK)
        cand_s = (v1[..., :, None] + v2[..., None, :]).reshape(*v1.shape[:-1], PEER_TOPK * PEER_TOPK)
        cand_i = (i1[..., :, None] * N_KEYS + i2[..., None, :]).reshape(*i1.shape[:-1], PEER_TOPK * PEER_TOPK)
        best_s, best_pos = lax.top_k(cand_s, PEER_TOPK)
        expert = jnp.take_along_axis(cand_i, best_pos, axis=-1)
        g = jax.nn.softmax(best_s, axis=-1)
        act = jax.nn.gelu(jnp.einsum('cd,chkd->chk', hc, u[expert],
                                     preferred_element_type=jnp.float32), approximate=False)
        wgt = (g * act).astype(hc.dtype)
        return jnp.einsum('chk,chkd->cd', wgt, v[expert])

    out = lax.map(chunk, h.reshape(-1, PEER_CHUNK, d))
    return out.reshape(b, s, d)

def second_inputs(seed: int = 0) -> dict:
    key = jax.random.key(seed)
    ks = jax.random.split(key, 21)
    f32 = jnp.float32
    L, D = DEPTH_2, D_MODEL

    def nrm(k, shape, sc):
        return jax.random.normal(k, shape, f32) * sc

    def gain(k, shape):
        return 1.0 + 0.05 * jax.random.normal(k, shape, f32)

    x = nrm(ks[0], (BATCH, SEQ, D), 1.0)
    c = nrm(ks[1], (BATCH, D), 1.0)
    positions = (jnp.arange(SEQ, dtype=jnp.int32)[None, :]
                 + jax.random.randint(ks[2], (BATCH, 1), 0, 1024, dtype=jnp.int32))
    w_ada = nrm(ks[3], (L, D, 6 * D), 0.2 * D ** -0.5)
    b_ada = nrm(ks[4], (L, 6 * D), 0.1)
    g_mix = gain(ks[5], (L, D))
    w_in = nrm(ks[6], (L, D, IN_COLS), D ** -0.5)
    g_kv = gain(ks[7], (L, KV_RANK))
    w_uk = nrm(ks[8], (L, KV_RANK, N_HEADS_A, NOPE_DIM_A), KV_RANK ** -0.5)
    w_uv = nrm(ks[9], (L, KV_RANK, N_HEADS_A, HEAD_DIM_A), KV_RANK ** -0.5)
    b_forget = jax.random.uniform(ks[10], (L, N_HEADS_B), f32, 2.0, 6.0)
    g_out_a = gain(ks[11], (L, WIDTH_A))
    g_out_b = gain(ks[12], (L, WIDTH_B))
    w_out = nrm(ks[13], (L, MIX_WIDTH, D), MIX_WIDTH ** -0.5)
    g_ffn = gain(ks[14], (L, D))
    w_peer_q = nrm(ks[15], (L, D, PEER_HEADS * PEER_KEY_DIM), D ** -0.5)
    peer_keys1 = nrm(ks[16], (L, N_KEYS, PEER_KEY_DIM // 2), (PEER_KEY_DIM // 2) ** -0.5)
    peer_keys2 = nrm(ks[17], (L, N_KEYS, PEER_KEY_DIM // 2), (PEER_KEY_DIM // 2) ** -0.5)
    peer_u = nrm(ks[18], (L, N_EXPERTS_2, D), D ** -0.5)
    peer_v = nrm(ks[19], (L, N_EXPERTS_2, D), 0.5)
    g_final = gain(ks[20], (D,))
    return {'x': x, 'c': c, 'positions': positions, 'w_ada': w_ada, 'b_ada': b_ada,
            'g_mix': g_mix, 'w_in': w_in, 'g_kv': g_kv, 'w_uk': w_uk, 'w_uv': w_uv,
            'b_forget': b_forget, 'g_out_a': g_out_a, 'g_out_b': g_out_b, 'w_out': w_out,
            'g_ffn': g_ffn, 'w_peer_q': w_peer_q, 'peer_keys1': peer_keys1,
            'peer_keys2': peer_keys2, 'peer_u': peer_u, 'peer_v': peer_v, 'g_final': g_final}

def second_block(x, c, positions, w_ada, b_ada, g_mix, w_in, g_kv, w_uk, w_uv, b_forget,
              g_out_a, g_out_b, w_out, g_ffn, w_peer_q, peer_keys1, peer_keys2, peer_u,
              peer_v, g_final):
    b, s, d = x.shape
    cos_a, sin_a = rope_tables(positions, ROPE_DIM_A)
    cos_i, sin_i = rope_tables(positions, IDX_ROPE_DIM)
    c_act = jax.nn.silu(c)
    split_at = []
    acc = 0
    for n in IN_SIZES[:-1]:
        acc += n
        split_at.append(acc)
    for l in range(DEPTH_2):
        mod = (c_act @ w_ada[l] + b_ada[l])[:, None, :]
        shift1, scale1, gate1, shift2, scale2, gate2 = jnp.split(mod, 6, axis=-1)
        h = rms_norm_2(x, g_mix[l]) * (1.0 + scale1) + shift1
        proj = h @ w_in[l]
        q_a, lat, k_r, iq, ik, iw, q_b, k_b, v_b, f_b = jnp.split(proj, split_at, axis=-1)
        o_a = dsa_attention(q_a.reshape(b, s, N_HEADS_A, HEAD_DIM_A), rms_norm_2(lat, g_kv[l]), k_r,
                            iq.reshape(b, s, IDX_HEADS, IDX_DIM), ik, iw,
                            cos_a, sin_a, cos_i, sin_i, w_uk[l], w_uv[l])
        o_b = forgetting_attention(q_b.reshape(b, s, N_HEADS_B, HEAD_DIM_B),
                                   k_b.reshape(b, s, N_HEADS_B, HEAD_DIM_B),
                                   v_b.reshape(b, s, N_HEADS_B, HEAD_DIM_B),
                                   f_b + b_forget[l])
        mixed = jnp.concatenate([rms_norm_2(o_a, g_out_a[l]), rms_norm_2(o_b, g_out_b[l])], axis=-1)
        x = x + gate1 * (mixed @ w_out[l])
        h2 = rms_norm_2(x, g_ffn[l]) * (1.0 + scale2) + shift2
        x = x + gate2 * peer_ffn(h2, w_peer_q[l], peer_keys1[l], peer_keys2[l], peer_u[l], peer_v[l])
    return rms_norm_2(x, g_final)


def setup_inputs(seed=0):
    out = dict(first_inputs(seed))
    for name, value in second_inputs(seed + 1).items():
        if name != "x":
            out[name + "_2"] = value
    return out


def reference(
    x, positions, norm_mix_g, norm_ffn_g, final_norm_g, ab_w_in, gla_w_a2, gla_b_a2, ret_norm_g,
    gla_norm_g, ab_w_out, ffn_w_gate, ffn_w_up, ffn_w_down, hgrn_lb_logits, c_w_in, hgrn_norm_g,
    c_w_out, moe_router, moe_w_gate, moe_w_up, moe_w_down, c_2, positions_2, w_ada_2, b_ada_2,
    g_mix_2, w_in_2, g_kv_2, w_uk_2, w_uv_2, b_forget_2, g_out_a_2, g_out_b_2, w_out_2, g_ffn_2,
    w_peer_q_2, peer_keys1_2, peer_keys2_2, peer_u_2, peer_v_2, g_final_2,
):
    x = first_block(
        x, positions, norm_mix_g, norm_ffn_g, final_norm_g, ab_w_in, gla_w_a2, gla_b_a2,
        ret_norm_g, gla_norm_g, ab_w_out, ffn_w_gate, ffn_w_up, ffn_w_down, hgrn_lb_logits,
        c_w_in, hgrn_norm_g, c_w_out, moe_router, moe_w_gate, moe_w_up, moe_w_down,
    )
    return second_block(
        x, c_2, positions_2, w_ada_2, b_ada_2, g_mix_2, w_in_2, g_kv_2, w_uk_2, w_uv_2,
        b_forget_2, g_out_a_2, g_out_b_2, w_out_2, g_ffn_2, w_peer_q_2, peer_keys1_2,
        peer_keys2_2, peer_u_2, peer_v_2, g_final_2,
    )


_drawn_inputs = setup_inputs


def setup_inputs(seed=0):
    import zlib

    import numpy as np

    out = dict(_drawn_inputs(seed))
    spreads = {}
    factors = {'gla_b_a2': 3.263,
     'ret_norm_g': 5.399,
     'gla_norm_g': 6.493,
     'hgrn_lb_logits': 6.296,
     'hgrn_norm_g': 4.775,
     'g_mix_2': 3.223,
     'g_kv_2': 7.817,
     'g_out_a_2': 8.0,
     'g_out_b_2': 8.0,
     'g_ffn_2': 5.864}
    for name, (base, spread) in spreads.items():
        noise = np.random.default_rng([zlib.crc32(name.encode()), seed]).standard_normal(out[name].shape)
        drawn = base * np.exp(spread * noise) if base else spread * noise
        out[name] = jnp.asarray(drawn.astype(out[name].dtype))
    for name, factor in factors.items():
        out[name] = (out[name] * factor).astype(out[name].dtype)
    return out
```

```python
from contextlib import ExitStack

import concourse.bass as bass
from concourse import mybir

F32 = mybir.dt.float32
BF16 = mybir.dt.bfloat16
I32 = mybir.dt.int32
U32 = mybir.dt.uint32
ALU = mybir.AluOpType
ACT = mybir.ActivationFunctionType
AX = mybir.AxisListType

P = 128
T = 512
TT = T // P
D = 1024
KD = D // P
EPS = 1e-6
BANK = 512
D_FF = 2816
E_FF = 3584
N_EXP = 8
SLOTS = 160
GROUP = 256
UNITS_MAX = (2 * T + N_EXP * (SLOTS - 1)) // SLOTS
ROWS_MAX = UNITS_MAX * SLOTS
LEVELS = 7
NEG = -1.0e30
TAKEN = -3.0e38
DSA_TOPK = 128
PEER_HEADS = 8
PEER_K = 16
N_PEER = 16384
PICKS = PEER_HEADS * PEER_K
MAGIC = 1.5 * 2.0 ** 23
TWO_PI_HI = 6.28125
TWO_PI_MID = 0.0019350051879882812
TWO_PI_LO = 3.019916050561733e-07


def const_layout():
    widths = [("ident", P), ("before", P), ("ones", P), ("causal", P), ("swap_ret", P), ("swap_a", P),
              ("swap_i", P), ("freq", 4), ("levels", (LEVELS + 1) * P), ("decay", 4 * T), ("restart", T),
              ("iota16", 16), ("token", TT), ("eye8", P)]
    at, out = 0, {}
    for name, w in widths:
        out[name] = (at, w)
        at += w
    return out, at


def const_values():
    import numpy as np
    where, n = const_layout()
    c = np.zeros((P, n), np.float32)

    def put(name, a):
        at, w = where[name]
        c[:a.shape[0], at:at + a.shape[1]] = a

    i = np.arange(P)
    put("ident", np.eye(P))
    put("before", (i[:, None] < i[None, :]))
    put("ones", np.ones((P, P)))
    put("causal", np.where(i[None, :] <= i[:, None], 0.0, NEG))

    def swap(period, rot):
        m = np.zeros((P, P))
        for d in range(P):
            r = d % period
            if r < rot // 2:
                m[d + rot // 2, d] = -1.0
            elif r < rot:
                m[d - rot // 2, d] = 1.0
        return m

    def freq(period, rot, base):
        inv = base ** (-np.arange(0, rot, 2, dtype=np.float32) / np.float32(rot))
        f = np.zeros(P, np.float32)
        for d in range(P):
            r = d % period
            if r < rot:
                f[d] = inv.astype(np.float32)[r % (rot // 2)]
        return f

    put("swap_ret", swap(128, 128))
    put("swap_a", swap(64, 16))
    put("swap_i", swap(32, 8))
    put("freq", np.stack([freq(128, 128, np.float32(10000.0)), freq(64, 16, np.float32(500000.0)),
                          freq(32, 8, np.float32(500000.0)), np.full(P, np.pi / 2)], 1))
    lev = np.zeros((P, LEVELS + 1, P))
    for l in range(LEVELS):
        b = 64 >> l
        lev[:, l] = ((i[:, None] // (2 * b) == i[None, :] // (2 * b))
                     & (i[:, None] % (2 * b) < b) & (i[None, :] % (2 * b) >= b))
    lev[:, LEVELS] = np.eye(P)
    put("levels", lev.reshape(P, -1))
    gam = np.log1p(-np.exp2(-5.0 - np.arange(4)))
    rel = np.arange(T)[None, :] - i[:, None]
    dec = np.stack([np.where(rel >= 0, np.exp(np.maximum(rel, 0) * g), 0.0) for g in gam], 1)
    put("decay", dec.reshape(P, -1))
    put("restart", np.broadcast_to((np.arange(T) % P != 0), (P, T)))
    put("iota16", np.broadcast_to(np.arange(16), (P, 16)))
    put("token", i[:, None] + P * np.arange(TT)[None, :])
    return c


class Signal:

    def __init__(self, nc, stack, name, pool_dma):
        self.sem = stack.enter_context(nc.semaphore(name))
        self.base = 0
        if not pool_dma:
            nc.sync.sem_inc(self.sem, 1)
            self.base = 1

    def at(self, n):
        return n + self.base


SIGNALS = """
    start n_squares n_inverse n_roots n_normed n_normed_a n_turned n_own n_stored p_loaded0 p_loaded1
    p_loaded2 p_scaled p_summed p_taken_act p_taken_dve a_got a_own a_ready a_sines r_swapped r_own t_scored
    t_decayed t_summed t_taken loads g_made g_own g_logs g_low g_out q_own q_diffs q_decays q_queries q_keys
    q_keys_k q_scored0 q_scored1 q_picked0 q_picked1 q_turned q_turned_sb q_updates q_states q_outs q_taken
    q_absed passed_dve passed_pool m_squares m_own m_inverse m_roots m_ready m_gained m_turned m_taken m_got
    s_loaded0 s_loaded1 s_hidden0 s_hidden1 s_gate_up0 s_gate_up1 s_gated0 s_gated1 s_freed0 s_freed1
    s_y_ready s_y_taken s_y_turned s_emitted s_x_ready s_zeros s_stored passed_pe h_got h_own h_exp h_sig_f
    h_sig_k h_made h_logs h_kept scaled l_got l_squares l_inverse l_roots l_own l_normed l_turned l_copied
    l_made l_cleared i_dots i_relus i_own i_weighed x_ready x_logits x_masked x_scaled x_exps x_turned
    x_copied x_lat_made x_lat_copied x_made x_inverse x_taken x_zeroed x_cum x_got y_h_staged y_fin y_zeroed
    y_activated passed_act stored
""".split()


class Stages:

    def __init__(self, nc, stack):
        self.nc, self.stack = nc, stack
        self.signals = {}
        self.spare = []

    def sb(self, name, shape, dt=F32, stack=None):
        return (stack or self.stack).enter_context(self.nc.sbuf_tensor(name, shape, dt))

    def sig(self, name, pool_dma=False):
        if name not in self.signals:
            self.signals[name] = Signal(self.nc, self.stack, name, True) if pool_dma else self.spare.pop()
        return self.signals[name]

    def retire(self, prefix):
        for name in sorted(x for x in self.signals if x.startswith(prefix)):
            self.spare.append(self.signals.pop(name))

    def const(self, name):
        at, w = self.where[name]
        return self.consts[:, at:at + w]


def settle(eng, passed):
    eng.sem_inc(passed.sem, 1)


class Count:

    def __init__(self, signal):
        self.base, self.n = signal.base, 0

    def up(self):
        self.n += 1
        return 1

    def value(self):
        return self.base + self.n


def norm_stage(S, name, gain, shift=None, xn_dram=None):
    nc, h, xT, ps = S.nc, S.h, S.xT, S.ps
    with ExitStack() as st:
        xn = S.sb(name + "_xn", [P, TT, D], F32, st)
        ss = S.sb(name + "_ss", [P, TT], F32, st)
        rstd = S.sb(name + "_rstd", [P, TT], F32, st)
        squares, inverse, roots, normed, normed_a, turned, own, stored = (
            S.sig(x) for x in ("n_squares", "n_inverse", "n_roots", "n_normed", "n_normed_a", "n_turned", "n_own", "n_stored"))
        ident = S.const("ident")
        with nc.Block(name) as block:
            @block.scalar
            def _(act):
                for t in range(TT):
                    nc.scalar.activation(xn[:, t, :], h[:, t, :], ACT.Square,
                                         accum_out=ss[:, t:t + 1]).then_inc(squares.sem, 1)
                act.wait_ge(inverse.sem, inverse.at(1))
                nc.scalar.activation(rstd[:, :], ss[:, :], ACT.Sqrt).then_inc(roots.sem, 1)
                act.wait_ge(roots.sem, roots.at(1))
                for t in (1, 3):
                    nc.scalar.activation(xn[:, t, :], h[:, t, :], ACT.Copy,
                                         scale=rstd[:, t:t + 1]).then_inc(normed_a.sem, 1)

            @block.vector
            def _(dve):
                o = Count(own)
                dve.wait_ge(squares.sem, squares.at(TT))
                nc.vector.tensor_scalar(ss[:, :], ss[:, :], 1.0 / D, EPS, ALU.mult, ALU.add).then_inc(own.sem, o.up())
                dve.wait_ge(own.sem, o.value())
                nc.vector.reciprocal(ss[:, :], ss[:, :]).then_inc(inverse.sem, 1)
                dve.wait_ge(roots.sem, roots.at(1))
                for t in (0, 2):
                    nc.vector.tensor_scalar(xn[:, t, :], h[:, t, :], rstd[:, t:t + 1], None,
                                            ALU.mult).then_inc(normed.sem, 1)
                for t in range(TT):
                    for half in range(2):
                        dve.wait_ge(turned.sem, turned.at(2 * t + half + 1))
                        dst = xT[:, 4 * half:4 * half + 4, t * P:(t + 1) * P]
                        src = ps[2 * t + half][:, :].rearrange("p (k c) -> p k c", k=4)
                        g = gain[:, 4 * half:4 * half + 4].unsqueeze(2).broadcast_to([P, 4, P])
                        nc.vector.tensor_tensor(dst, src, g, ALU.mult).then_inc(own.sem, o.up())
                if shift is not None:
                    dve.wait_ge(own.sem, o.value())
                    s = shift.unsqueeze(2).broadcast_to([P, KD, T])
                    nc.vector.tensor_tensor(xT[:, :, :], xT[:, :, :], s, ALU.add).then_inc(own.sem, o.up())

            @block.tensor
            def _(pe):
                for t in range(TT):
                    pe.wait_ge((normed_a if t % 2 else normed).sem, (normed_a if t % 2 else normed).at(t // 2 + 1))
                    for half in range(2):
                        for k in range(4):
                            last = nc.tensor.transpose(ps[2 * t + half][:, k * P:(k + 1) * P],
                                                       xn[:, t, (4 * half + k) * P:(4 * half + k + 1) * P], ident)
                        last.then_inc(turned.sem, 1)

            if xn_dram is not None:
                @block.sync
                def _(sp):
                    sp.wait_ge(normed.sem, normed.at(2))
                    sp.wait_ge(normed_a.sem, normed_a.at(2))
                    sp.dma_start(xn_dram.rearrange("(t p) d -> p t d", p=P), xn[:, :, :]).then_inc(stored.sem, 16)
                    sp.wait_ge(stored.sem, stored.at(16))
        for s, n in ((squares, TT), (inverse, 1), (roots, 1), (normed, 2), (normed_a, 2), (turned, 8),
                     (own, 1 + 8 + (shift is not None)), (stored, 16 * (xn_dram is not None))):
            s.base += n


def project_stage(S, name, chunks):
    nc, xT, ps = S.nc, S.xT, S.ps
    NW = 3

    def pieces(w):
        return w if isinstance(w, list) else [w]

    def width_of(w):
        return sum(x.shape[1] for x in pieces(w))

    def loads_to(c):
        return 16 * sum(len(pieces(chunks[x][0])) for x in range(c % NW, c + 1, NW)) if c >= 0 else 0

    groups, ends = [], []
    count = {"act": 0, "dve": 0}
    for c, (w, kind, how, dst) in enumerate(chunks):
        n = width_of(w)
        parts = [(m, min(P, n - m * P)) for m in range((n + P - 1) // P)] if kind == "T" else [(t, P) for t in range(TT)]
        for i, (m, width) in enumerate(parts):
            who = "act" if len(groups) % 2 else "dve"
            if isinstance(how, str):
                who = {"silu": "act", "add": "dve"}.get(how, who)
            if isinstance(how, float):
                who = "act"
            elif not isinstance(how, str):
                who = "dve"
            groups.append((c, m, width, who, count[who], i == len(parts) - 1))
            count[who] += 1
        ends.append(len(groups))
    with ExitStack() as st:
        wring = S.sb(name + "_w", [P, NW, KD, BANK], F32, st)
        loaded = [S.sig(f"p_loaded{b}") for b in range(NW)]
        tmp = S.sb(name + "_tmp", [P, BANK], F32, st)
        scaled, n_scaled = S.sig("p_scaled"), 0
        summed = S.sig("p_summed")
        taken = {"act": S.sig("p_taken_act"), "dve": S.sig("p_taken_dve")}

        def out_of(g):
            c, m, width, who, _, _ = g
            n = width_of(chunks[c][0])
            b = ps[groups.index(g) % 8]
            return b[0:width, :] if chunks[c][1] == "T" else b[:, 0:n]

        with nc.Block(name) as block:
            @block.sync
            def _(sp):
                for c, (w, kind, how, dst) in enumerate(chunks):
                    if c >= NW:
                        sp.wait_ge(summed.sem, summed.at(ends[c - NW]))
                    at = 0
                    for part in pieces(w):
                        n = part.shape[1]
                        sp.dma_start(wring[:, c % NW, :, at:at + n],
                                     part.rearrange("(k p) n -> p k n", p=P)).then_inc(loaded[c % NW].sem, 16)
                        at += n

            @block.tensor
            def _(pe):
                for i, g in enumerate(groups):
                    c, m, width, who, _, final = g
                    w, kind, how, dst = chunks[c]
                    n = width_of(w)
                    if i == 0 or groups[i - 1][0] != c:
                        pe.wait_ge(loaded[c % NW].sem, loaded[c % NW].at(loads_to(c)))
                    if i >= 8:
                        pe.wait_ge(taken[groups[i - 8][3]].sem, taken[groups[i - 8][3]].at(groups[i - 8][4] + 1))
                    for k in range(KD):
                        wk = wring[:, c % NW, k, :]
                        if kind == "T":
                            last = nc.tensor.matmul(out_of(g), wk[:, m * P:m * P + width], xT[:, k, :],
                                                    start=(k == 0), stop=(k == KD - 1))
                        else:
                            last = nc.tensor.matmul(out_of(g), xT[:, k, m * P:(m + 1) * P], wk[:, 0:n],
                                                    start=(k == 0), stop=(k == KD - 1))
                    last.then_inc(summed.sem, 1)

            def evacuate(eng, me):
                for i, g in enumerate(groups):
                    c, m, width, who, _, _ = g
                    if who != me:
                        continue
                    how, dst = chunks[c][2], chunks[c][3]
                    eng.wait_ge(summed.sem, summed.at(i + 1))
                    if not isinstance(how, (str, float)):
                        nonlocal n_scaled
                        if me == "dve" and n_scaled >= 1:
                            eng.wait_ge(taken[me].sem, taken[me].at(g[4]))
                        nc.vector.tensor_tensor(tmp[:, 0:how.shape[1]], out_of(g), how, ALU.mult).then_inc(scaled.sem, 1)
                        n_scaled += 1
                        eng.wait_ge(scaled.sem, scaled.at(n_scaled))
                        ins = nc.vector.tensor_tensor(dst(m), dst(m), tmp[:, 0:how.shape[1]], ALU.add)
                    elif isinstance(how, str) and how == "add":
                        ins = nc.vector.tensor_tensor(dst(m), dst(m), out_of(g), ALU.add)
                    elif isinstance(how, str) and how == "silu":
                        ins = nc.scalar.activation(dst(m), out_of(g), ACT.Silu)
                    elif isinstance(how, float):
                        ins = nc.scalar.activation(dst(m), out_of(g), ACT.Copy, scale=how)
                    elif me == "act":
                        ins = nc.scalar.activation(dst(m), out_of(g), ACT.Copy)
                    else:
                        ins = nc.vector.tensor_copy(dst(m), out_of(g))
                    ins.then_inc(taken[me].sem, 1)

            @block.scalar
            def _(act):
                evacuate(act, "act")

            @block.vector
            def _(dve):
                evacuate(dve, "dve")
        for b in range(NW):
            loaded[b].base += loads_to(max([c for c in range(len(chunks)) if c % NW == b], default=-1))
        scaled.base += n_scaled
        summed.base += len(groups)
        for who in count:
            taken[who].base += count[who]


def angle_stage(S, name, positions, freqs, tables):
    nc = S.nc
    got, own, ready, sines = S.sig("a_got"), S.sig("a_own"), S.sig("a_ready"), S.sig("a_sines")
    with ExitStack() as st:
        pos_i = S.sb(name + "_pi", [P, T], I32, st)
        pos = S.sb(name + "_pf", [P, T], F32, st)
        turns = S.sb(name + "_turns", [P, T], F32, st)
        steps = 0
        with nc.Block(name) as block:
            @block.sync
            def _(sp):
                sp.dma_start(pos_i[:, :], positions.partition_broadcast(P)).then_inc(got.sem, 16)

            @block.vector
            def _(dve):
                nonlocal steps
                o = Count(own)
                dve.wait_ge(got.sem, got.at(16))
                nc.vector.tensor_copy(pos[:, :], pos_i[:, :]).then_inc(own.sem, o.up())
                dve.wait_ge(own.sem, o.value())
                for f, (cos, sin) in zip(freqs, tables):
                    nc.vector.tensor_scalar(sin, pos[:, :], f, None, ALU.mult).then_inc(own.sem, o.up())
                    dve.wait_ge(own.sem, o.value())
                    nc.vector.tensor_scalar(turns[:, :], sin, 0.15915494309189535, MAGIC, ALU.mult, ALU.add).then_inc(own.sem, o.up())
                    dve.wait_ge(own.sem, o.value())
                    nc.vector.tensor_scalar(turns[:, :], turns[:, :], MAGIC, None, ALU.subtract).then_inc(own.sem, o.up())
                    dve.wait_ge(own.sem, o.value())
                    for part in (TWO_PI_HI, TWO_PI_MID, TWO_PI_LO):
                        nc.vector.scalar_tensor_tensor(sin, turns[:, :], -part, sin, ALU.mult, ALU.add).then_inc(own.sem, o.up())
                        dve.wait_ge(own.sem, o.value())
                    nc.vector.tensor_scalar(sin, sin, 3.1415925, -3.1415925, ALU.min, ALU.max).then_inc(own.sem, o.up())
                    dve.wait_ge(own.sem, o.value())
                    nc.vector.scalar_tensor_tensor(cos, sin, -1.0, sin, ALU.mult, ALU.max).then_inc(ready.sem, 1)
                steps = o.n

            @block.scalar
            def _(act):
                for n, (cos, sin) in enumerate(tables):
                    act.wait_ge(ready.sem, ready.at(n + 1))
                    half_pi = S.const("freq")[:, 3:4]
                    nc.scalar.activation(cos, cos, ACT.Sin, bias=half_pi, scale=-1.0).then_inc(sines.sem, 1)
                    nc.scalar.activation(sin, sin, ACT.Sin).then_inc(sines.sem, 1)
        got.base += 16
        own.base += steps
        ready.base += len(tables)
        sines.base += 2 * len(tables)


def rotate_stage(S, name, tiles):
    nc, ps = S.nc, S.ps
    swapped, own = S.sig("r_swapped"), S.sig("r_own")
    with ExitStack() as st:
        scaled = S.sb(name + "_c", [P, 2, T], F32, st)
        with nc.Block(name) as block:
            @block.tensor
            def _(pe):
                for n, (x, swap, cos, sin) in enumerate(tiles):
                    if n >= 8:
                        pe.wait_ge(own.sem, own.at(3 * (n - 8) + 2))
                    rows = x.shape[0]
                    nc.tensor.matmul(ps[n % 8][0:rows, :], swap[0:rows, 0:rows], x, start=True,
                                     stop=True).then_inc(swapped.sem, 1)

            @block.vector
            def _(dve):
                o = Count(own)
                for n, (x, swap, cos, sin) in enumerate(tiles):
                    rows = x.shape[0]
                    dve.wait_ge(swapped.sem, swapped.at(n + 1))
                    nc.vector.tensor_tensor(x, x, cos[0:rows, :], ALU.mult).then_inc(own.sem, o.up())
                    nc.vector.tensor_tensor(scaled[0:rows, n % 2, :], ps[n % 8][0:rows, :], sin[0:rows, :], ALU.mult).then_inc(own.sem, o.up())
                    dve.wait_ge(own.sem, o.value())
                    nc.vector.tensor_tensor(x, x, scaled[0:rows, n % 2, :], ALU.add).then_inc(own.sem, o.up())
        swapped.base += len(tiles)
        own.base += 3 * len(tiles)


def retention_stage(S, q, k, v, mix):
    nc, ps = S.nc, S.ps
    NH = 4
    scored, decayed, summed, taken = S.sig("t_scored"), S.sig("t_decayed"), S.sig("t_summed"), S.sig("t_taken")
    decay = S.const("decay").rearrange("p (h t) -> p h t", h=NH)
    with ExitStack() as st:
        probs = S.sb("ret_probs", [P, 2, TT, T], F32, st)
        with nc.Block("retention") as block:
            @block.tensor
            def _(pe):
                def scores(h):
                    for j in range(TT):
                        if h:
                            pe.wait_ge(decayed.sem, decayed.at(TT * (h - 1) + j + 1))
                        nc.tensor.matmul(ps[j][:, 0:T - j * P], k[:, h, j * P:(j + 1) * P], q[:, h, j * P:T],
                                         start=True, stop=True).then_inc(scored.sem, 1)

                def outputs(h):
                    pe.wait_ge(decayed.sem, decayed.at(TT * (h + 1)))
                    if h >= 2:
                        pe.wait_ge(taken.sem, taken.at(h - 1))
                    for i in range(TT):
                        for j in range(i + 1):
                            last = nc.tensor.matmul(ps[4 + h % 2][:, i * P:(i + 1) * P],
                                                    probs[:, h % 2, j, (i - j) * P:(i - j + 1) * P],
                                                    v[:, j, h * P:(h + 1) * P], start=(j == 0), stop=(j == i))
                    last.then_inc(summed.sem, 1)

                scores(0)
                for h in range(1, NH):
                    scores(h)
                    outputs(h - 1)
                outputs(NH - 1)

            @block.vector
            def _(dve):
                for h in range(NH):
                    if h >= 2:
                        dve.wait_ge(summed.sem, summed.at(h - 1))
                    for j in range(TT):
                        n = T - j * P
                        dve.wait_ge(scored.sem, scored.at(TT * h + j + 1))
                        nc.vector.tensor_tensor(probs[:, h % 2, j, 0:n], ps[j][:, 0:n], decay[:, h, 0:n],
                                                ALU.mult).then_inc(decayed.sem, 1)

            @block.scalar
            def _(act):
                for h in range(NH):
                    act.wait_ge(summed.sem, summed.at(h + 1))
                    nc.scalar.activation(mix[:, :, h, :], ps[4 + h % 2][:, :].rearrange("p (t d) -> p t d", t=TT),
                                         ACT.Copy).then_inc(taken.sem, 1)
        scored.base += 16
        decayed.base += 16
        summed.base += NH
        taken.base += NH


def log_gate_stage(S, name, tiles, factor):
    nc, ps = S.nc, S.ps
    made, own, logs, low, out = (S.sig("g_" + x) for x in ("made", "own", "logs", "low", "out"))
    n_act = 0
    with ExitStack() as st:
        y = S.sb(name + "_y", [P, len(tiles), T], F32, st)
        e = S.sb(name + "_e", [P, len(tiles), T], F32, st)
        with nc.Block(name) as block:
            @block.tensor
            def _(pe):
                for n, (lhsT, rhs, bias, dst) in enumerate(tiles):
                    rows = dst.shape[0]
                    nc.tensor.matmul(ps[n][0:rows, :], lhsT, rhs, start=True, stop=True).then_inc(made.sem, 1)

            @block.scalar
            def _(act):
                nonlocal n_act
                o = Count(own)
                for n, (lhsT, rhs, bias, dst) in enumerate(tiles):
                    r = dst.shape[0]
                    act.wait_ge(made.sem, made.at(n + 1))
                    nc.scalar.activation(y[0:r, n, :], ps[n][0:r, :], ACT.Identity, bias=bias).then_inc(low.sem, 1)
                    act.wait_ge(low.sem, low.at(n + 1))
                    nc.scalar.activation(e[0:r, n, :], y[0:r, n, :], ACT.Abs).then_inc(own.sem, o.up())
                    act.wait_ge(own.sem, o.value())
                    nc.scalar.activation(e[0:r, n, :], e[0:r, n, :], ACT.Exp, scale=-1.0).then_inc(own.sem, o.up())
                    act.wait_ge(own.sem, o.value())
                    nc.scalar.activation(e[0:r, n, :], e[0:r, n, :], ACT.Ln, bias=1.0).then_inc(logs.sem, 1)
                n_act = o.n

            @block.vector
            def _(dve):
                for n, (lhsT, rhs, bias, dst) in enumerate(tiles):
                    r = dst.shape[0]
                    dve.wait_ge(logs.sem, logs.at(n + 1))
                    nc.vector.scalar_tensor_tensor(dst, y[0:r, n, :], 0.0, e[0:r, n, :], ALU.min,
                                                   ALU.subtract).then_inc(out.sem, 1)
                    dve.wait_ge(out.sem, out.at(2 * n + 1))
                    nc.vector.tensor_scalar(dst, dst, factor, None, ALU.mult).then_inc(out.sem, 1)
        made.base += len(tiles)
        own.base += n_act
        low.base += len(tiles)
        logs.base += len(tiles)
        out.base += 2 * len(tiles)


def gated_stage(S, name, n_packs, heads, q, k, logf, v, mix, head0):
    nc, ps = S.nc, S.ps
    W = P // heads
    L = LEVELS
    sig = S.sig
    g_own, diffs, decays, queries = sig("q_own"), sig("q_diffs"), sig("q_decays"), sig("q_queries")
    keys, keys_k = sig("q_keys"), sig("q_keys_k")
    scored = [sig("q_scored0"), sig("q_scored1")]
    picked = [sig("q_picked0"), sig("q_picked1")]
    turned, turned_sb, updates, states, outs, taken, absed = (
        sig(x) for x in ("q_turned", "q_turned_sb", "q_updates", "q_states", "q_outs", "q_taken", "q_absed"))
    restart = S.const("restart")
    masks = S.const("levels").bitcast(U32).rearrange("p (l i) -> p l i", l=L + 1)
    ident = S.const("ident")
    with ExitStack() as st:
        g = S.sb(name + "_g", [P, T], F32, st)
        diff = S.sb(name + "_diff", [P, L + 2, T], F32, st)
        qE = S.sb(name + "_qe", [P, 2, T], F32, st)
        kE = S.sb(name + "_ke", [P, 2, T], F32, st)
        qd = S.sb(name + "_qd", [P, T], F32, st)
        kd = S.sb(name + "_kd", [P, T], F32, st)
        kdt = S.sb(name + "_kdt", [P, TT, P], F32, st)
        sT = S.sb(name + "_st", [P, heads, TT, P], F32, st)
        state = S.sb(name + "_state", [P, 3, P], F32, st)

        def loop(eng, body):
            if n_packs <= 2:
                for p in range(n_packs):
                    body(p)
            else:
                with eng.Fori(0, n_packs) as p:
                    body(p)

        with nc.Block(name) as block:
            @block.vector
            def _(dve):
                nc.vector.memset(sT[:, :, :, :], 0.0).then_inc(g_own.sem, 1)

                def body(p):
                    dve.wait_ge(keys.sem, keys.at((L + 1) * p))
                    dve.wait_ge(keys_k.sem, keys_k.at(p))
                    nc.vector.tensor_tensor_scan(g[:, :], restart, logf(p), 0.0, ALU.mult, ALU.add).then_inc(g_own.sem, 1)
                    dve.wait_ge(g_own.sem, g_own.at(p + 2))
                    for l in range(L):
                        b = 64 >> l
                        gv = g[:, :].rearrange("p (n w) -> p n w", w=2 * b)
                        dv = diff[:, l, :].rearrange("p (n w) -> p n w", w=2 * b)
                        nc.vector.tensor_tensor(dv, gv, gv[:, :, b - 1:b].broadcast_to([P, T // (2 * b), 2 * b]),
                                                ALU.subtract).then_inc(diffs.sem, 1)
                    gv = g[:, :].rearrange("p (n w) -> p n w", w=P)
                    dv = diff[:, L, :].rearrange("p (n w) -> p n w", w=P)
                    nc.vector.tensor_tensor(dv, gv, gv[:, :, P - 1:P].broadcast_to([P, TT, P]),
                                            ALU.subtract).then_inc(diffs.sem, 1)
                    dve.wait_ge(outs.sem, outs.at(heads * p))

                    def query(l):
                        dve.wait_ge(scored[l % 2].sem, scored[l % 2].at(_half(p, L + 1, l)))
                        if l < L:
                            dve.wait_ge(decays.sem, decays.at(p * (L + 2) + l + 1))
                            nc.vector.tensor_tensor(qE[:, l % 2, :], q(p), diff[:, l, :], ALU.mult).then_inc(queries.sem, 1)
                        else:
                            settle(dve, S.sig("passed_dve"))
                            nc.vector.tensor_copy(qE[:, l % 2, :], q(p)).then_inc(queries.sem, 1)

                    def pick(l):
                        dve.wait_ge(scored[l % 2].sem, scored[l % 2].at(_half(p, L + 1, l) + 1))
                        settle(dve, S.sig("passed_dve"))
                        for hd in range(heads):
                            ins = nc.vector.copy_predicated(
                                sT[:, hd, :, :], masks[:, l:l + 1, :].broadcast_to([P, TT, P]),
                                ps[2 * (l % 2) + hd][:, :].rearrange("p (c i) -> p c i", c=TT))
                            if hd == heads - 1:
                                ins.then_inc(picked[l % 2].sem, 1)

                    for l in range(L + 1):
                        query(l)
                        if l:
                            if l > 1:
                                dve.wait_ge(picked[l % 2].sem, picked[l % 2].at(_half(p, L + 1, l - 2) + 1))
                            pick(l - 1)
                    dve.wait_ge(picked[(L - 1) % 2].sem, picked[(L - 1) % 2].at(_half(p, L + 1, L - 1) + 1))
                    pick(L)
                    dve.wait_ge(decays.sem, decays.at(p * (L + 2) + L + 1))
                    nc.vector.tensor_tensor(qd[:, :], q(p), diff[:, L + 1, :], ALU.mult).then_inc(queries.sem, 1)
                    dve.wait_ge(updates.sem, updates.at(p + 1))
                    nc.vector.tensor_copy(state[:, 0, :], ps[5][:, 0:P]).then_inc(states.sem, 1)
                    for c in (1, 2):
                        dve.wait_ge(states.sem, states.at(3 * p + c))
                        nc.vector.scalar_tensor_tensor(state[:, c, :], state[:, c - 1, :],
                                                       diff[:, L + 1, c * P + P - 1:c * P + P],
                                                       ps[5][:, c * P:(c + 1) * P], ALU.mult,
                                                       ALU.add).then_inc(states.sem, 1)
                loop(dve, body)

            @block.scalar
            def _(act):
                def body(p):
                    for l in range(L):
                        act.wait_ge(diffs.sem, diffs.at(p * (L + 1) + l + 1))
                        nc.scalar.activation(diff[:, l, :], diff[:, l, :], ACT.Abs).then_inc(absed.sem, 1)
                        act.wait_ge(absed.sem, absed.at(p * L + l + 1))
                        nc.scalar.activation(diff[:, l, :], diff[:, l, :], ACT.Exp, scale=-1.0).then_inc(decays.sem, 1)
                    nc.scalar.activation(diff[:, L + 1, :], g[:, :], ACT.Exp).then_inc(decays.sem, 1)
                    act.wait_ge(diffs.sem, diffs.at((p + 1) * (L + 1)))
                    nc.scalar.activation(diff[:, L, :], diff[:, L, :], ACT.Exp, scale=-1.0).then_inc(decays.sem, 1)
                    act.wait_ge(turned.sem, turned.at(p + 1))
                    nc.scalar.activation(kdt[:, :, :], ps[4][:, :].rearrange("p (c d) -> p c d", c=TT),
                                         ACT.Copy).then_inc(turned_sb.sem, 1)
                    for hd in range(heads):
                        act.wait_ge(outs.sem, outs.at(heads * p + hd + 1))
                        nc.scalar.activation(mix(p * heads + hd), ps[6 + hd][:, :].rearrange("p (c d) -> p c d", c=TT),
                                             ACT.Copy).then_inc(taken.sem, 1)
                loop(act, body)

            @block.gpsimd
            def _(pool):
                def body(p):
                    for l in range(L + 1):
                        pool.wait_ge(scored[l % 2].sem, scored[l % 2].at(_half(p, L + 1, l)))
                        if l < L:
                            pool.wait_ge(decays.sem, decays.at(p * (L + 2) + l + 1))
                            settle(pool, S.sig("passed_pool"))
                            nc.gpsimd.tensor_tensor(kE[:, l % 2, :], k(p), diff[:, l, :], ALU.mult).then_inc(keys.sem, 1)
                        else:
                            settle(pool, S.sig("passed_pool"))
                            nc.gpsimd.tensor_copy(kE[:, l % 2, :], k(p)).then_inc(keys.sem, 1)
                    pool.wait_ge(decays.sem, decays.at((p + 1) * (L + 2)))
                    pool.wait_ge(turned.sem, turned.at(p))
                    settle(pool, S.sig("passed_pool"))
                    nc.gpsimd.tensor_tensor(kd[:, :], k(p), diff[:, L, :], ALU.mult).then_inc(keys_k.sem, 1)
                loop(pool, body)

            @block.tensor
            def _(pe):
                def body(p):
                    for l in range(L + 1):
                        pe.wait_ge(queries.sem, queries.at(p * (L + 2) + l + 1))
                        pe.wait_ge(keys.sem, keys.at(p * (L + 1) + l + 1))
                        pe.wait_ge(picked[l % 2].sem, picked[l % 2].at(_half(p, L + 1, l)))
                        for hd in range(heads):
                            r = slice(hd * W, (hd + 1) * W)
                            for c in range(TT):
                                cc = slice(c * P, (c + 1) * P)
                                last = nc.tensor.matmul(ps[2 * (l % 2) + hd][:, cc], kE[r, l % 2, cc], qE[r, l % 2, cc],
                                                        start=True, stop=True)
                        last.then_inc(scored[l % 2].sem, 1)
                    pe.wait_ge(keys_k.sem, keys_k.at(p + 1))
                    pe.wait_ge(turned_sb.sem, turned_sb.at(p))
                    for c in range(TT):
                        last = nc.tensor.transpose(ps[4][:, c * P:(c + 1) * P], kd[:, c * P:(c + 1) * P], ident)
                    last.then_inc(turned.sem, 1)
                    pe.wait_ge(turned_sb.sem, turned_sb.at(p + 1))
                    pe.wait_ge(states.sem, states.at(3 * p))
                    for c in range(3):
                        for hd in range(heads):
                            last = nc.tensor.matmul(ps[5][hd * W:(hd + 1) * W, c * P:(c + 1) * P],
                                                    kdt[:, c, hd * W:(hd + 1) * W], v(p * heads + hd, c),
                                                    start=True, stop=True)
                    last.then_inc(updates.sem, 1)
                    pe.wait_ge(picked[0].sem, picked[0].at((L + 1) // 2 * (p + 1)))
                    pe.wait_ge(picked[1].sem, picked[1].at((L + 1) // 2 * (p + 1)))
                    pe.wait_ge(queries.sem, queries.at((p + 1) * (L + 2)))
                    pe.wait_ge(states.sem, states.at(3 * (p + 1)))
                    pe.wait_ge(taken.sem, taken.at(heads * p))
                    for hd in range(heads):
                        r = slice(hd * W, (hd + 1) * W)
                        for c in range(TT):
                            cc = slice(c * P, (c + 1) * P)
                            last = nc.tensor.matmul(ps[6 + hd][:, cc], sT[:, hd, c, :], v(p * heads + hd, c),
                                                    start=True, stop=(c == 0))
                            if c:
                                last = nc.tensor.matmul(ps[6 + hd][:, cc], qd[r, cc], state[r, c - 1, :],
                                                        start=False, stop=True)
                        last.then_inc(outs.sem, 1)
                loop(pe, body)
        for s, n in ((g_own, 1 + n_packs), (diffs, (L + 1) * n_packs), (decays, (L + 2) * n_packs),
                     (queries, (L + 2) * n_packs), (keys, (L + 1) * n_packs), (keys_k, n_packs),
                     (scored[0], (L + 1) // 2 * n_packs), (scored[1], (L + 1) // 2 * n_packs),
                     (picked[0], (L + 1) // 2 * n_packs), (picked[1], (L + 1) // 2 * n_packs),
                     (turned, n_packs), (turned_sb, n_packs), (updates, n_packs), (states, 3 * n_packs),
                     (outs, heads * n_packs), (taken, heads * n_packs), (absed, L * n_packs)):
            s.base += n


def _half(p, per_pack, l):
    return p * (per_pack // 2) + l // 2


def head_norm_stage(S, name, mix, width, gain_row, gate):
    nc, ps, xT = S.nc, S.ps, S.xT
    NH = D // width
    squares, own, inverse, roots, ready, gained, turned, taken, got = (
        S.sig("m_" + x) for x in ("squares", "own", "inverse", "roots", "ready", "gained", "turned", "taken", "got"))
    n_own = 0
    with ExitStack() as st:
        sq = S.sb(name + "_sq", [P, 2, D], F32, st)
        gains = S.sb(name + "_gains", [P, D], F32, st)
        ss = S.sb(name + "_ss", [P, TT, NH], F32, st)
        r = S.sb(name + "_r", [P, TT, NH], F32, st)
        with nc.Block(name) as block:
            @block.sync
            def _(sp):
                for at, src in gain_row:
                    n = src.shape[0]
                    sp.dma_start(gains[:, at:at + n], src.partition_broadcast(P)).then_inc(got.sem, 16)

            @block.gpsimd
            def _(pool):
                pool.wait_ge(got.sem, got.at(16 * len(gain_row)))
                for t in range(TT):
                    m = gate[:, t, :] if gate is not None else None
                    if m is not None:
                        nc.gpsimd.tensor_tensor(m, m, gains[:, :], ALU.mult).then_inc(gained.sem, 1)

            @block.scalar
            def _(act):
                for t in range(TT):
                    if t >= 2:
                        act.wait_ge(own.sem, own.at(t - 1))
                    nc.scalar.activation(sq[:, t % 2, :], mix[:, t, :], ACT.Square).then_inc(squares.sem, 1)
                act.wait_ge(inverse.sem, inverse.at(1))
                nc.scalar.activation(r[:, :, :], ss[:, :, :], ACT.Sqrt).then_inc(roots.sem, 1)
                for t in range(TT):
                    for half in range(2):
                        act.wait_ge(turned.sem, turned.at(2 * t + half + 1))
                        nc.scalar.activation(xT[:, 4 * half:4 * half + 4, t * P:(t + 1) * P],
                                             ps[2 * t + half][:, :].rearrange("p (k c) -> p k c", k=4),
                                             ACT.Copy).then_inc(taken.sem, 1)

            @block.vector
            def _(dve):
                nonlocal n_own
                o = Count(own)
                for t in range(TT):
                    dve.wait_ge(squares.sem, squares.at(t + 1))
                    nc.vector.tensor_reduce(ss[:, t, :], sq[:, t % 2, :].rearrange("p (h w) -> p h w", h=NH),
                                                   AX.X, ALU.add).then_inc(own.sem, o.up())
                dve.wait_ge(own.sem, o.value())
                nc.vector.tensor_scalar(ss[:, :, :], ss[:, :, :], 1.0 / width, EPS, ALU.mult, ALU.add).then_inc(own.sem, o.up())
                dve.wait_ge(own.sem, o.value())
                nc.vector.reciprocal(ss[:, :, :], ss[:, :, :]).then_inc(inverse.sem, 1)
                dve.wait_ge(roots.sem, roots.at(1))
                for t in range(TT):
                    m = mix[:, t, :].rearrange("p (h w) -> p h w", h=NH)
                    nc.vector.tensor_tensor(m, m, r[:, t, :].unsqueeze(2).broadcast_to([P, NH, width]), ALU.mult).then_inc(own.sem, o.up())
                    dve.wait_ge(own.sem, o.value())
                    if gate is not None:
                        dve.wait_ge(gained.sem, gained.at(t + 1))
                        by = gate[:, t, :]
                    else:
                        dve.wait_ge(got.sem, got.at(16 * len(gain_row)))
                        by = gains[:, :]
                    nc.vector.tensor_tensor(mix[:, t, :], mix[:, t, :], by, ALU.mult).then_inc(ready.sem, 1)
                n_own = o.n

            @block.tensor
            def _(pe):
                for t in range(TT):
                    pe.wait_ge(ready.sem, ready.at(t + 1))
                    for half in range(2):
                        for kk in range(4):
                            c = 4 * half + kk
                            last = nc.tensor.transpose(ps[2 * t + half][:, kk * P:(kk + 1) * P],
                                                       mix[:, t, c * P:(c + 1) * P], S.const("ident"))
                        last.then_inc(turned.sem, 1)
        for s, n in ((squares, TT), (own, n_own), (inverse, 1), (roots, 1), (ready, TT), (turned, 8), (taken, 8),
                     (gained, TT * (gate is not None)), (got, 16 * len(gain_row))):
            s.base += n


def swiglu_stage(S, name, rows, hidden, units, weights, x_of, gather, emit):
    nc, ps = S.nc, S.ps
    n_groups = hidden // GROUP
    per = ((n_groups + 1) // 2, n_groups // 2)
    subs = [(0, P), (P, rows - P)]
    sig = S.sig
    loaded = [sig("s_loaded0"), sig("s_loaded1")]
    hidden_ready = [sig("s_hidden0"), sig("s_hidden1")]
    gate_up, gated = [sig("s_gate_up0"), sig("s_gate_up1")], [sig("s_gated0"), sig("s_gated1")]
    freed = [sig("s_freed0"), sig("s_freed1")]
    y_ready, y_taken, y_turned, emitted, x_ready, zeros_ready, stored = (
        sig("s_" + x) for x in ("y_ready", "y_taken", "y_turned", "emitted", "x_ready", "zeros", "stored"))
    with ExitStack() as st:
        wg = S.sb(name + "_wg", [P, 2, KD, GROUP], F32, st)
        wu = S.sb(name + "_wu", [P, 2, KD, GROUP], F32, st)
        wd = S.sb(name + "_wd", [P, 2, 2, D], F32, st)
        gated_sb = S.sb(name + "_gs", [P, 2, rows], F32, st)
        hid = S.sb(name + "_hid", [P, 2, rows], F32, st)
        yT = S.sb(name + "_yt", [P, KD, rows], F32, st)
        zero = S.sb(name + "_zero", [P, BANK], BF16, st)

        def groups(eng, u, body):
            with eng.Fori(0, n_groups // 2) as i:
                for b in range(2):
                    body(i, b)
            if n_groups % 2:
                body(n_groups // 2, 0)

        with nc.Block(name) as block:
            @block.sync
            def _(sp):
                with sp.Fori(0, units(sp)) as u:
                    g, up, dn = weights(sp, u)

                    def body(i, b):
                        sp.wait_ge(freed[b].sem, freed[b].at(u * per[b] + i))
                        f = (i * 2 + b) * GROUP
                        gv = g[:, bass.ds(f, GROUP)].rearrange("(k p) f -> p k f", p=P)
                        uv = up[:, bass.ds(f, GROUP)].rearrange("(k p) f -> p k f", p=P)
                        dv = dn[bass.ds(f, GROUP), :].rearrange("(j p) d -> p j d", p=P)
                        sp.dma_start(wg[:, b, :, :], gv).then_inc(loaded[b].sem, 16)
                        sp.dma_start(wu[:, b, :, :], uv).then_inc(loaded[b].sem, 16)
                        sp.dma_start(wd[:, b, :, :], dv).then_inc(loaded[b].sem, 16)
                    groups(sp, u, body)

            @block.tensor
            def _(pe):
                pe.wait_ge(zeros_ready.sem, zeros_ready.at(1))
                with pe.Fori(0, units(pe)) as u:
                    if gather is not None:
                        gather.turn(pe, u)
                    pe.wait_ge(y_taken.sem, y_taken.at(u))
                    for b in range(4):
                        nc.tensor.matmul(ps[b][:, :], zero[:, 0:P], zero[:, :], start=True, stop=False,
                                         skip_group_check=True)
                    if gather is None:
                        pe.wait_ge(emitted.sem, emitted.at(4 * u))
                    else:
                        pe.wait_ge(x_ready.sem, x_ready.at(4 * (u + 1)))

                    settle(pe, S.sig("passed_pe"))

                    def body(i, b):
                        pe.wait_ge(loaded[b].sem, loaded[b].at((u * per[b] + i + 1) * 48))
                        n = u * n_groups + i * 2 + b
                        for j in range(2):
                            pe.wait_ge(hidden_ready[j].sem, hidden_ready[j].at(n))
                            for w, bank in ((wg, 4 + j), (wu, 6 + j)):
                                for k in range(KD):
                                    last = nc.tensor.matmul(ps[bank][:, 0:rows], w[:, b, k, j * P:(j + 1) * P], x_of(k, u),
                                                            start=(k == 0), stop=(k == KD - 1))
                            last.then_inc(gate_up[j].sem, 1)
                        for j in range(2):
                            pe.wait_ge(hidden_ready[j].sem, hidden_ready[j].at(n + 1))
                            for d in range(KD):
                                at = (d % 2) * rows
                                last = nc.tensor.matmul(ps[d // 2][:, at:at + rows], wd[:, b, j, d * P:(d + 1) * P],
                                                        hid[:, j, :], start=False, stop=False, skip_group_check=True)
                        last.then_inc(freed[b].sem, 1)
                    groups(pe, u, body)
                    nc.tensor.matmul(ps[3][0:32, 0:2], zero[:, 0:32], zero[:, 0:2], start=False, stop=True,
                                     skip_group_check=True).then_inc(y_ready.sem, 1)
                    pe.wait_ge(y_taken.sem, y_taken.at(u + 1))
                    pe.wait_ge(hidden_ready[0].sem, hidden_ready[0].at((u + 1) * n_groups))
                    pe.wait_ge(hidden_ready[1].sem, hidden_ready[1].at((u + 1) * n_groups))
                    for s, (r0, n) in enumerate(subs):
                        for half in range(2):
                            for kk in range(4):
                                last = nc.tensor.transpose(ps[4 + 2 * s + half][0:n, kk * P:(kk + 1) * P],
                                                           yT[:, 4 * half + kk, r0:r0 + n], S.const("ident"))
                            last.then_inc(y_turned.sem, 1)

            @block.scalar
            def _(act):
                with act.Fori(0, units(act)) as u:
                    def body(i, b):
                        n = u * n_groups + i * 2 + b
                        for j in range(2):
                            act.wait_ge(gate_up[j].sem, gate_up[j].at(n + 1))
                            act.wait_ge(hidden_ready[j].sem, hidden_ready[j].at(n))
                            nc.scalar.activation(gated_sb[:, j, :], ps[4 + j][:, 0:rows], ACT.Silu).then_inc(gated[j].sem, 1)
                    groups(act, u, body)
                    if gather is not None:
                        gather.store(act, u)

            @block.vector
            def _(dve):
                nc.vector.memset(zero[:, :], 0.0).then_inc(zeros_ready.sem, 1)
                with dve.Fori(0, units(dve)) as u:
                    if gather is not None:
                        gather.place(dve, u)

                    def body(i, b):
                        n = u * n_groups + i * 2 + b
                        for j in range(2):
                            dve.wait_ge(gated[j].sem, gated[j].at(n + 1))
                            nc.vector.tensor_tensor(hid[:, j, :], gated_sb[:, j, :], ps[6 + j][:, 0:rows],
                                                    ALU.mult).then_inc(hidden_ready[j].sem, 1)
                    groups(dve, u, body)
                    dve.wait_ge(y_ready.sem, y_ready.at(u + 1))
                    dve.wait_ge(y_turned.sem, y_turned.at(4 * u))
                    for b in range(4):
                        ins = nc.vector.tensor_copy(yT[:, 2 * b:2 * b + 2, :],
                                                    ps[b][:, 0:2 * rows].rearrange("p (d r) -> p d r", d=2))
                    ins.then_inc(y_taken.sem, 1)
                    if gather is not None:
                        gather.before_emit(dve, u)
                    for s, (r0, n) in enumerate(subs):
                        for half in range(2):
                            dve.wait_ge(y_turned.sem, y_turned.at(4 * u + 2 * s + half + 1))
                            emit(u, s, half, ps[4 + 2 * s + half][0:n, :]).then_inc(emitted.sem, 1)

            if gather is not None:
                @block.gpsimd
                def _(pool):
                    with pool.Fori(0, units(pool)) as u:
                        gather.fetch(pool, u)


def ffn_swiglu(S):
    a, rows = S.a, T // 2

    def emit(u, s, half, src):
        dst = S.h[:, bass.ds(u * 2 + s, 1), half * 512:(half + 1) * 512].rearrange("p o c -> p (o c)")
        return S.nc.vector.tensor_tensor(dst, dst, src, ALU.add)

    swiglu_stage(S, "ffn", rows, D_FF, lambda eng: 2,
                 lambda eng, u: (a["ffn_w_gate"][0], a["ffn_w_up"][0], a["ffn_w_down"][0]),
                 lambda k, u: S.xT[:, k, bass.ds(u * rows, rows)], None, emit)
    n = D_FF // GROUP
    for b, per in ((0, (n + 1) // 2), (1, n // 2)):
        S.sig(f"s_loaded{b}").base += 48 * 2 * per
        S.sig(f"s_freed{b}").base += 2 * per
    for j in range(2):
        for x in ("s_hidden", "s_gate_up", "s_gated"):
            S.sig(f"{x}{j}").base += 2 * n
    for x, c in (("y_ready", 2), ("y_taken", 2), ("y_turned", 8), ("emitted", 8), ("zeros", 1)):
        S.sig("s_" + x).base += c


def hgrn_gate_stage(S, z, logf, keys):
    nc, a = S.nc, S.a
    got, own, lb_exp, sig_f, sig_k, made, logs, kept = (
        S.sig("h_" + x) for x in ("got", "own", "exp", "sig_f", "sig_k", "made", "logs", "kept"))
    n_own = 0
    with ExitStack() as st:
        lg = S.sb("lb_logits", [P, 2, KD], F32, st)
        e = S.sb("lb_e", [P, 2, KD], F32, st)
        m = S.sb("lb_m", [P, KD], F32, st)
        lb = S.sb("lb_v", [P, KD], F32, st)
        rest = S.sb("lb_rest", [P, KD], F32, st)
        with nc.Block("hgrn_gates") as block:
            @block.sync
            def _(sp):
                with nc.allow_non_contiguous_dma(reason="8 KB of logits"):
                    for l in range(2):
                        sp.dma_start(lg[:, l, :], a["hgrn_lb_logits"][l].rearrange("(k p) -> p k", p=P)).then_inc(got.sem, 16)

            @block.vector
            def _(dve):
                nonlocal n_own
                o = Count(own)
                dve.wait_ge(got.sem, got.at(32))
                nc.vector.tensor_tensor(m[:, :], lg[:, 0, :], lg[:, 1, :], ALU.max).then_inc(own.sem, o.up())
                dve.wait_ge(own.sem, o.value())
                nc.vector.tensor_tensor(e[:, :, :], lg[:, :, :], m[:, :].unsqueeze(1).broadcast_to([P, 2, KD]),
                                               ALU.subtract).then_inc(own.sem, o.up())
                dve.wait_ge(own.sem, o.value())
                dve.wait_ge(lb_exp.sem, lb_exp.at(1))
                nc.vector.tensor_tensor(m[:, :], e[:, 0, :], e[:, 1, :], ALU.add).then_inc(own.sem, o.up())
                dve.wait_ge(own.sem, o.value())
                nc.vector.reciprocal(m[:, :], m[:, :]).then_inc(own.sem, o.up())
                dve.wait_ge(own.sem, o.value())
                nc.vector.tensor_tensor(lb[:, :], e[:, 1, :], m[:, :], ALU.mult).then_inc(own.sem, o.up())
                dve.wait_ge(own.sem, o.value())
                nc.vector.tensor_scalar(rest[:, :], lb[:, :], -1.0, 1.0, ALU.mult, ALU.add).then_inc(own.sem, o.up())
                dve.wait_ge(own.sem, o.value())
                for k in range(KD):
                    dve.wait_ge(sig_f.sem, sig_f.at(k + 1))
                    nc.vector.tensor_scalar(logf[:, k, :], logf[:, k, :], rest[:, k:k + 1], lb[:, k:k + 1],
                                                   ALU.mult, ALU.add).then_inc(own.sem, o.up())
                    dve.wait_ge(own.sem, o.value())
                    nc.vector.tensor_scalar(logf[:, k, :], logf[:, k, :], 2.0e-38, None, ALU.max).then_inc(made.sem, 1)
                    dve.wait_ge(sig_k.sem, sig_k.at(k + 1))
                    nc.vector.tensor_scalar(keys[:, k, :], keys[:, k, :], rest[:, k:k + 1], None, ALU.mult).then_inc(kept.sem, 1)
                n_own = o.n

            @block.scalar
            def _(act):
                act.wait_ge(own.sem, own.at(2))
                nc.scalar.activation(e[:, :, :], e[:, :, :], ACT.Exp).then_inc(lb_exp.sem, 1)
                for k in range(KD):
                    nc.scalar.activation(keys[:, k, :], z[:, k, :], ACT.Sigmoid, scale=-1.0).then_inc(sig_k.sem, 1)
                    if z is logf:
                        act.wait_ge(sig_k.sem, sig_k.at(k + 1))
                    nc.scalar.activation(logf[:, k, :], z[:, k, :], ACT.Sigmoid).then_inc(sig_f.sem, 1)
                for k in range(KD):
                    act.wait_ge(made.sem, made.at(k + 1))
                    nc.scalar.activation(logf[:, k, :], logf[:, k, :], ACT.Ln).then_inc(logs.sem, 1)
        for s, n in ((got, 32), (own, n_own), (lb_exp, 1), (sig_f, KD), (sig_k, KD), (made, KD), (logs, KD), (kept, KD)):
            s.base += n


def mixer1(S):
    a = S.a
    norm_stage(S, "norm2", S.gains[:, 2, :])
    w = a["c_w_in"][0]
    with ExitStack() as st:
        mix = S.sb("mix1", [P, TT, D], F32, st)
        gate = S.sb("gate1", [P, TT, D], F32, st)
        heads = mix[:, :, :].rearrange("p t (h d) -> p t h d", h=8)
        with ExitStack() as st2:
            v = S.sb("v1", [P, TT, D], F32, st2)
            q = S.sb("q1", [P, KD, T], F32, st2)
            z = S.sb("z1", [P, KD, T], F32, st2)
            keys = S.sb("k1", [P, KD, T], F32, st2)
            project_stage(S, "proj1", [
                (w[:, c * 512:(c + 1) * 512], "T", "silu", lambda m, c=c: q[:, 4 * c + m, :]) for c in range(2)] + [
                (w[:, (2 + c) * 512:(3 + c) * 512], "T", "copy", lambda m, c=c: z[:, 4 * c + m, :]) for c in range(2)] + [
                (w[:, (4 + c) * 512:(5 + c) * 512], "tok", "copy", lambda t, c=c: v[:, t, c * 512:(c + 1) * 512]) for c in range(2)] + [
                (w[:, (6 + c) * 512:(7 + c) * 512], "tok", "silu", lambda t, c=c: gate[:, t, c * 512:(c + 1) * 512]) for c in range(2)])
            hgrn_gate_stage(S, z, z, keys)
            scale_stage(S, q[:, :, :], P ** -0.5)
            row = lambda x, p: x[:, bass.ds(p, 1), :].rearrange("p o t -> p (o t)")
            gated_stage(S, "hgrn", 8, 1, lambda p: row(q, p), lambda p: row(keys, p), lambda p: row(z, p),
                        lambda hd, c: v[:, c, bass.ds(hd * P, P)],
                        lambda hd: mix[:, :, bass.ds(hd * P, P)], 0)
        head_norm_stage(S, "headnorm1", mix, 128, [(i * P, a["hgrn_norm_g"][0]) for i in range(8)], gate)
        add_projection(S, "out1", a["c_w_out"][0])


def scale_stage(S, x, by):
    nc = S.nc
    done = S.sig("scaled")
    with nc.Block(f"scale{done.base}") as block:
        @block.vector
        def _(dve):
            nc.vector.tensor_scalar(x, x, by, None, ALU.mult).then_inc(done.sem, 1)
    done.base += 1


def route_stage(S, R):
    nc, a, ps, xT = S.nc, S.a, S.ps, S.xT
    S_ = S.sig
    got, logits, own, gates_in, gates_e, chosen, placed, zeroed, ids, blanked = (
        S_("o_" + x) for x in ("got", "logits", "own", "gates_in", "gates_e", "chosen", "placed", "zeroed", "ids", "blanked"))
    cleared, scattered = S_("o_cleared", pool_dma=True), S_("o_scattered", pool_dma=True)
    n_own = 0
    with ExitStack() as st:
        wr = S.sb("router_w", [P, KD, N_EXP], F32, st)
        lg = S.sb("router_lg", [P, TT, N_EXP], F32, st)
        top = S.sb("router_top", [P, TT, 8], F32, st)
        top_i = S.sb("router_ti", [P, TT, 8], U32, st)
        top_f = S.sb("router_tf", [P, TT, 8], F32, st)
        hot = S.sb("router_hot", [P, TT, 2, N_EXP], F32, st)
        both = S.sb("router_both", [P, TT, N_EXP], F32, st)
        e2 = S.sb("router_e2", [P, TT, 1], F32, st)
        total = S.sb("router_total", [P, TT, 1], F32, st)
        count = S.sb("router_count", [P, N_EXP], F32, st)
        need = S.sb("router_need", [P, N_EXP], F32, st)
        more = S.sb("router_more", [P, N_EXP], F32, st)
        upto = S.sb("router_upto", [P, N_EXP], F32, st)
        first = S.sb("router_first", [P, N_EXP], F32, st)
        pos = S.sb("router_pos", [P, TT, N_EXP], F32, st)
        prod = S.sb("router_prod", [P, TT, 2, N_EXP], F32, st)
        row = S.sb("router_row", [P, TT, 2], F32, st)
        past = S.sb("router_past", [P, 16, N_EXP], F32, st)
        owner = S.sb("router_owner", [P, 16], F32, st)
        token_i = S.sb("router_token", [P, TT], I32, st)
        zero_rows = S.sb("router_zero", [1, ROWS_MAX], I32, st)
        blank = S.sb("router_blank", [SLOTS // 2, D], F32, st)
        with nc.Block("route") as block:
            @block.sync
            def _(sp):
                with nc.allow_non_contiguous_dma(reason="32 KB of router weights"):
                    sp.dma_start(wr[:, :, :], a["moe_router"][0].rearrange("(k p) e -> p k e", p=P)).then_inc(got.sem, 16)

            @block.tensor
            def _(pe):
                pe.wait_ge(got.sem, got.at(16))
                for t in range(TT):
                    for k in range(KD):
                        last = nc.tensor.matmul(ps[t][:, 0:N_EXP], xT[:, k, t * P:(t + 1) * P], wr[:, k, :],
                                                start=(k == 0), stop=(k == KD - 1))
                    last.then_inc(logits.sem, 1)
                pe.wait_ge(chosen.sem, chosen.at(1))
                for t in range(TT):
                    for u in range(t + 1):
                        nc.tensor.matmul(ps[4 + t % 2][:, t * 8:t * 8 + 8], S.const("before") if u == t else S.const("ones"),
                                         both[:, u, :], start=(u == 0), stop=(u == t))
                for u in range(TT):
                    last = nc.tensor.matmul(ps[6][:, 0:8], S.const("ones"), both[:, u, :], start=(u == 0), stop=(u == TT - 1))
                last.then_inc(placed.sem, 1)

            @block.scalar
            def _(act):
                act.wait_ge(zeroed.sem, zeroed.at(2))
                act.dma_start(R.y.rearrange("(a p) d -> p a d", p=SLOTS // 2),
                              blank[:, :].unsqueeze(1).broadcast_to([SLOTS // 2, ROWS_MAX // (SLOTS // 2), D])).then_inc(blanked.sem, 16)
                act.wait_ge(gates_in.sem, gates_in.at(1))
                nc.scalar.activation(e2[:, :, :], e2[:, :, :], ACT.Exp).then_inc(gates_e.sem, 1)
                act.wait_ge(blanked.sem, blanked.at(16))

            @block.vector
            def _(dve):
                nonlocal n_own
                o = Count(own)
                iota8 = S.const("iota16")[:, 0:8]
                for t in range(TT):
                    dve.wait_ge(logits.sem, logits.at(t + 1))
                    nc.vector.tensor_copy(lg[:, t, :], ps[t][:, 0:N_EXP]).then_inc(own.sem, o.up())
                dve.wait_ge(own.sem, o.value())
                for t in range(TT):
                    nc.vector.max(top[:, t, :], lg[:, t, :]).then_inc(own.sem, o.up())
                dve.wait_ge(own.sem, o.value())
                for t in range(TT):
                    nc.vector.max_index(top_i[:, t, :], top[:, t, :], lg[:, t, :]).then_inc(own.sem, o.up())
                nc.vector.tensor_tensor(e2[:, :, :], top[:, :, 1:2], top[:, :, 0:1], ALU.subtract).then_inc(gates_in.sem, 1)
                dve.wait_ge(own.sem, o.value())
                nc.vector.tensor_copy(top_f[:, :, :], top_i[:, :, :]).then_inc(own.sem, o.up())
                dve.wait_ge(own.sem, o.value())
                for c in range(2):
                    nc.vector.tensor_tensor(hot[:, :, c, :], iota8.unsqueeze(1).broadcast_to([P, TT, 8]),
                                                   top_f[:, :, c:c + 1].broadcast_to([P, TT, 8]), ALU.is_equal).then_inc(own.sem, o.up())
                dve.wait_ge(own.sem, o.value())
                nc.vector.tensor_tensor(both[:, :, :], hot[:, :, 0, :], hot[:, :, 1, :], ALU.add).then_inc(chosen.sem, 1)
                dve.wait_ge(gates_e.sem, gates_e.at(1))
                nc.vector.tensor_scalar(total[:, :, :], e2[:, :, :], 1.0, None, ALU.add).then_inc(own.sem, o.up())
                dve.wait_ge(own.sem, o.value())
                nc.vector.reciprocal(R.gates[:, :, 0:1], total[:, :, :]).then_inc(own.sem, o.up())
                dve.wait_ge(own.sem, o.value())
                nc.vector.tensor_tensor(R.gates[:, :, 1:2], R.gates[:, :, 0:1], e2[:, :, :], ALU.mult).then_inc(own.sem, o.up())
                dve.wait_ge(placed.sem, placed.at(1))
                for t in range(TT):
                    nc.vector.tensor_copy(pos[:, t, :], ps[4 + t % 2][:, t * 8:t * 8 + 8]).then_inc(own.sem, o.up())
                nc.vector.tensor_copy(count[:, :], ps[6][:, 0:8]).then_inc(own.sem, o.up())
                dve.wait_ge(own.sem, o.value())
                nc.vector.tensor_scalar(need[:, :], count[:, :], 0.0, None, ALU.is_gt).then_inc(own.sem, o.up())
                dve.wait_ge(own.sem, o.value())
                for m in range(1, (T + SLOTS - 1) // SLOTS):
                    nc.vector.tensor_scalar(more[:, :], count[:, :], float(m * SLOTS), None, ALU.is_gt).then_inc(own.sem, o.up())
                    dve.wait_ge(own.sem, o.value())
                    nc.vector.tensor_tensor(need[:, :], need[:, :], more[:, :], ALU.add).then_inc(own.sem, o.up())
                    dve.wait_ge(own.sem, o.value())
                nc.vector.tensor_tensor_scan(upto[:, :], S.const("ones")[:, 0:8], need[:, :], 0.0, ALU.mult, ALU.add).then_inc(own.sem, o.up())
                dve.wait_ge(own.sem, o.value())
                nc.vector.tensor_tensor(first[:, :], upto[:, :], need[:, :], ALU.subtract).then_inc(own.sem, o.up())
                dve.wait_ge(own.sem, o.value())
                nc.vector.tensor_scalar(first[:, :], first[:, :], float(SLOTS), None, ALU.mult).then_inc(own.sem, o.up())
                dve.wait_ge(own.sem, o.value())
                nc.vector.tensor_tensor(pos[:, :, :], pos[:, :, :], first[:, :].unsqueeze(1).broadcast_to([P, TT, 8]),
                                               ALU.add).then_inc(own.sem, o.up())
                dve.wait_ge(own.sem, o.value())
                for c in range(2):
                    nc.vector.tensor_tensor(prod[:, :, c, :], hot[:, :, c, :], pos[:, :, :], ALU.mult).then_inc(own.sem, o.up())
                dve.wait_ge(own.sem, o.value())
                nc.vector.tensor_reduce(row[:, :, :], prod[:, :, :, :], AX.X, ALU.add).then_inc(own.sem, o.up())
                dve.wait_ge(own.sem, o.value())
                nc.vector.tensor_copy(R.row[:, :, :], row[:, :, :]).then_inc(ids.sem, 1)
                nc.vector.tensor_copy(token_i[:, :], S.const("token")).then_inc(ids.sem, 1)
                nc.vector.tensor_tensor(past[:, :, :], S.const("iota16").unsqueeze(2).broadcast_to([P, 16, 8]),
                                               upto[:, :].unsqueeze(1).broadcast_to([P, 16, 8]), ALU.is_ge).then_inc(own.sem, o.up())
                dve.wait_ge(own.sem, o.value())
                nc.vector.tensor_reduce(owner[:, :], past[:, :, :], AX.X, ALU.add).then_inc(own.sem, o.up())
                dve.wait_ge(own.sem, o.value())
                nc.vector.tensor_scalar(owner[:, :], owner[:, :], float(N_EXP - 1), None, ALU.min).then_inc(own.sem, o.up())
                dve.wait_ge(own.sem, o.value())
                nc.vector.tensor_copy(R.expert[:, :], owner[:, :]).then_inc(own.sem, o.up())
                nc.vector.tensor_copy(R.units[:, :], upto[:, N_EXP - 1:N_EXP]).then_inc(own.sem, o.up())
                n_own = o.n

            @block.gpsimd
            def _(pool):
                nc.gpsimd.memset(zero_rows[:, :], 0).then_inc(zeroed.sem, 1)
                nc.gpsimd.memset(blank[:, :], 0.0).then_inc(zeroed.sem, 1)
                pool.wait_ge(zeroed.sem, zeroed.at(2))
                pool.dma_start(R.token_of_row.rearrange("r o -> o r"), zero_rows[:, :]).then_inc(cleared.sem, 16)
                pool.wait_ge(cleared.sem, cleared.at(16))
                pool.wait_ge(ids.sem, ids.at(2))
                for t in range(TT):
                    for c in range(2):
                        pool.indirect_dma_start(
                            out=R.token_of_row, out_offset=bass.IndirectOffsetOnAxis(ap=R.row[:, t, c:c + 1], axis=0),
                            in_=token_i[:, t:t + 1], in_offset=None).then_inc(scattered.sem, 16)
                pool.wait_ge(scattered.sem, scattered.at(16 * 2 * TT))
        for s, n in ((got, 16), (logits, TT), (own, n_own), (gates_in, 1), (gates_e, 1), (chosen, 1), (placed, 1),
                     (zeroed, 2), (cleared, 16), (blanked, 16), (scattered, 32 * TT), (ids, 2)):
            s.base += n


class ExpertRows:

    def __init__(self, S, R, st):
        self.S, self.R = S, R
        self.xg = S.sb("rows_x", [P, 2, D], F32, st)
        self.xu = S.sb("rows_xt", [P, KD, SLOTS], F32, st)
        self.yrow = S.sb("rows_y", [P, 2, D], F32, st)
        self.index = S.sb("rows_index", [P, 2], I32, st)
        self.subs = [(0, P), (P, SLOTS - P)]
        self.indexed, self.gathered = (S.sig("e_" + x, pool_dma=True) for x in ("indexed", "gathered"))
        self.turned, self.stored = (S.sig("e_" + x) for x in ("turned", "stored"))

    def fetch(self, pool, u):
        S, nc, R = self.S, self.S.nc, self.R
        pool.wait_ge(self.turned.sem, self.turned.at(4 * u))
        settle(pool, S.sig("passed_pool"))
        for s, (r0, n) in enumerate(self.subs):
            pool.dma_start(self.index[0:n, s:s + 1], R.token_of_row[bass.ds(u * SLOTS + r0, n), :]).then_inc(self.indexed.sem, 16)
        pool.wait_ge(self.indexed.sem, self.indexed.at(32 * (u + 1)))
        settle(pool, S.sig("passed_pool"))
        for s, (r0, n) in enumerate(self.subs):
            pool.indirect_dma_start(out=self.xg[0:n, s, :], out_offset=None, in_=R.xn,
                                    in_offset=bass.IndirectOffsetOnAxis(ap=self.index[0:n, s:s + 1], axis=0),
                                    ).then_inc(self.gathered.sem, 16)

    def turn(self, pe, u):
        S, nc = self.S, self.S.nc
        pe.wait_ge(self.gathered.sem, self.gathered.at(32 * (u + 1)))
        pe.wait_ge(S.sig("s_emitted").sem, S.sig("s_emitted").at(4 * u))
        settle(pe, S.sig("passed_pe"))
        for s, (r0, n) in enumerate(self.subs):
            for half in range(2):
                for kk in range(4):
                    c = (4 * half + kk) * P
                    last = nc.tensor.transpose(S.ps[4 + 2 * s + half][:, kk * P:kk * P + n], self.xg[0:n, s, c:c + P],
                                               S.const("ident")[0:n, 0:n])
                last.then_inc(self.turned.sem, 1)

    def place(self, dve, u):
        S, nc = self.S, self.S.nc
        for s, (r0, n) in enumerate(self.subs):
            for half in range(2):
                dve.wait_ge(self.turned.sem, self.turned.at(4 * u + 2 * s + half + 1))
                src = S.ps[4 + 2 * s + half][:, :].rearrange("p (k r) -> p k r", k=4)[:, :, 0:n]
                g = S.gains[:, 3, 4 * half:4 * half + 4].unsqueeze(2).broadcast_to([P, 4, n])
                nc.vector.tensor_tensor(self.xu[:, 4 * half:4 * half + 4, r0:r0 + n], src, g,
                                        ALU.mult).then_inc(S.sig("s_x_ready").sem, 1)

    def before_emit(self, dve, u):
        dve.wait_ge(self.stored.sem, self.stored.at(32 * u))

    def emit(self, u, s, half, src):
        n = self.subs[s][1]
        return self.S.nc.vector.tensor_copy(self.yrow[0:n, s, half * 512:(half + 1) * 512], src)

    def store(self, act, u):
        for s, (r0, n) in enumerate(self.subs):
            act.wait_ge(self.S.sig("s_emitted").sem, self.S.sig("s_emitted").at(4 * u + 2 * s + 2))
            act.dma_start(self.R.y[bass.ds(u * SLOTS + r0, n), :], self.yrow[0:n, s, :]).then_inc(self.stored.sem, 16)
        act.wait_ge(self.stored.sem, self.stored.at(32 * (u + 1)))


class Routing:
    pass


def expert_values(eng, tile, lo, hi):
    return eng.value_load(tile, min_val=lo, max_val=hi)


def moe1(S):
    nc, a = S.nc, S.a
    with ExitStack() as st:
        R = Routing()
        R.gates = S.sb("gates", [P, TT, 2], F32, st)
        R.row = S.sb("row_of", [P, TT, 2], I32, st)
        R.expert = S.sb("expert_of", [P, 16], I32, st)
        R.units = S.sb("n_units", [P, 1], I32, st)
        R.xn = nc.dram_tensor("xn_rows", (T, D), F32, kind="Internal").ap()
        R.y = nc.dram_tensor("y_rows", (ROWS_MAX, D), F32, kind="Internal").ap()
        R.token_of_row = nc.dram_tensor("token_of_row", (ROWS_MAX, 1), I32, kind="Internal").ap()
        norm_stage(S, "norm3", S.gains[:, 3, :], xn_dram=R.xn)
        route_stage(S, R)
        with ExitStack() as st2:
            rows = ExpertRows(S, R, st2)

            def weights(eng, u):
                e = expert_values(eng, R.expert[0:1, bass.ds(u, 1)], 0, N_EXP - 1)
                one = lambda w: w[0][bass.ds(e, 1)].rearrange("o a b -> (o a) b")
                return one(a["moe_w_gate"]), one(a["moe_w_up"]), one(a["moe_w_down"])

            swiglu_stage(S, "experts", SLOTS, E_FF,
                         lambda eng: expert_values(eng, R.units[0:1, 0:1], 1, UNITS_MAX), weights,
                         lambda k, u: rows.xu[:, k, :], rows, rows.emit)
        combine_stage(S, R)


def combine_stage(S, R):
    nc = S.nc
    got, own = S.sig("c_got", pool_dma=True), S.sig("c_own")
    with ExitStack() as st:
        yg = S.sb("combine_y", [P, TT, 2, D], F32, st)
        with nc.Block("combine") as block:
            @block.gpsimd
            def _(pool):
                for t in range(TT):
                    for c in range(2):
                        pool.indirect_dma_start(out=yg[:, t, c, :], out_offset=None, in_=R.y,
                                                in_offset=bass.IndirectOffsetOnAxis(ap=R.row[:, t, c:c + 1], axis=0),
                                                ).then_inc(got.sem, 16)

            @block.vector
            def _(dve):
                o = Count(own)
                dve.wait_ge(got.sem, got.at(16 * 2 * TT))
                for c in range(2):
                    for t in range(TT):
                        nc.vector.scalar_tensor_tensor(S.h[:, t, :], yg[:, t, c, :], R.gates[:, t, c:c + 1],
                                                              S.h[:, t, :], ALU.mult, ALU.add).then_inc(own.sem, o.up())
                    dve.wait_ge(own.sem, o.value())
        got.base += 32 * TT
        own.base += 8


def row_norm_stage(S, name, gain):
    nc, h = S.nc, S.h
    got, squares, own, inverse, roots, ready = (S.sig("w_" + x) for x in ("got", "squares", "own", "inverse", "roots", "ready"))
    with ExitStack() as st:
        junk = S.sb(name + "_sq", [P, TT, D], F32, st)
        g = S.sb(name + "_g", [P, D], F32, st)
        ss = S.sb(name + "_ss", [P, TT], F32, st)
        r = S.sb(name + "_r", [P, TT], F32, st)
        with nc.Block(name) as block:
            @block.sync
            def _(sp):
                sp.dma_start(g[:, :], gain.partition_broadcast(P)).then_inc(got.sem, 16)

            @block.scalar
            def _(act):
                for t in range(TT):
                    nc.scalar.activation(junk[:, t, :], h[:, t, :], ACT.Square, accum_out=ss[:, t:t + 1]).then_inc(squares.sem, 1)
                act.wait_ge(inverse.sem, inverse.at(1))
                nc.scalar.activation(r[:, :], ss[:, :], ACT.Sqrt).then_inc(roots.sem, 1)

            @block.vector
            def _(dve):
                o = Count(own)
                dve.wait_ge(squares.sem, squares.at(TT))
                nc.vector.tensor_scalar(ss[:, :], ss[:, :], 1.0 / D, EPS, ALU.mult, ALU.add).then_inc(own.sem, o.up())
                dve.wait_ge(own.sem, o.value())
                nc.vector.reciprocal(ss[:, :], ss[:, :]).then_inc(inverse.sem, 1)
                dve.wait_ge(roots.sem, roots.at(1))
                dve.wait_ge(got.sem, got.at(16))
                for t in range(TT):
                    nc.vector.scalar_tensor_tensor(h[:, t, :], h[:, t, :], r[:, t:t + 1], g[:, :], ALU.mult,
                                                   ALU.mult).then_inc(ready.sem, 1)
        for s, n in ((got, 16), (squares, TT), (own, 1), (inverse, 1), (roots, 1), (ready, TT)):
            s.base += n


def ada_stage(S, M):
    nc, a, ps = S.nc, S.a, S.ps
    NW, NC = 3, 6 * D // 512
    got, c_ready, summed, turned, own, rows_made, biased = (
        S.sig("d_" + x) for x in ("got", "c", "summed", "turned", "own", "rows", "biased"))
    loaded = [S.sig(f"d_loaded{b}") for b in range(NW)]
    n_own = 0
    with ExitStack() as st:
        wring = S.sb("ada_w", [P, NW, KD, 512], F32, st)
        small = S.sb("ada_small", [6 * KD + KD, P], F32, st)
        cT = S.sb("ada_c", [P, KD], F32, st)
        with nc.Block("ada") as block:
            @block.sync
            def _(sp):
                sp.dma_start(small[0:48, :], a["b_ada_2"][0].rearrange("(m p) -> m p", p=P)).then_inc(got.sem, 16)
                sp.dma_start(small[48:56, :], a["c_2"][0].rearrange("(m p) -> m p", p=P)).then_inc(got.sem, 16)
                for c in range(NC):
                    if c >= NW:
                        sp.wait_ge(summed.sem, summed.at(c - NW + 1))
                    sp.dma_start(wring[:, c % NW, :, :], a["w_ada_2"][0][:, c * 512:(c + 1) * 512].rearrange(
                        "(k p) n -> p k n", p=P)).then_inc(loaded[c % NW].sem, 16)

            @block.tensor
            def _(pe):
                pe.wait_ge(got.sem, got.at(32))
                nc.tensor.transpose(ps[1][:, 0:56], small[:, :], S.const("ident")[0:56, 0:56]).then_inc(turned.sem, 1)
                pe.wait_ge(c_ready.sem, c_ready.at(1))
                for c in range(NC):
                    pe.wait_ge(loaded[c % NW].sem, loaded[c % NW].at(16 * (c // NW + 1)))
                    for m in range(4):
                        col = 4 * c + m
                        for k in range(KD):
                            last = nc.tensor.matmul(ps[0][:, col:col + 1], wring[:, c % NW, k, m * P:(m + 1) * P],
                                                    cT[:, k:k + 1], start=(k == 0), stop=(k == KD - 1))
                    last.then_inc(summed.sem, 1)
                pe.wait_ge(own.sem, own.at(1))
                for g, part in enumerate((2, 5)):
                    for m in range(KD):
                        col = M.col[:, part * KD + m:part * KD + m + 1].broadcast_to([P, P])
                        last = nc.tensor.matmul(ps[2 + 2 * g + m // 4][:, (m % 4) * P:(m % 4 + 1) * P], col,
                                                S.const("ident"), start=True, stop=True)
                last.then_inc(rows_made.sem, 1)

            @block.scalar
            def _(act):
                act.wait_ge(turned.sem, turned.at(1))
                nc.scalar.activation(cT[:, :], ps[1][:, 48:56], ACT.Silu).then_inc(c_ready.sem, 1)

            @block.vector
            def _(dve):
                nonlocal n_own
                o = Count(own)
                dve.wait_ge(summed.sem, summed.at(NC))
                dve.wait_ge(turned.sem, turned.at(1))
                nc.vector.tensor_copy(M.bias[:, :], ps[1][:, 0:48]).then_inc(biased.sem, 1)
                dve.wait_ge(biased.sem, biased.at(1))
                nc.vector.tensor_tensor(M.col[:, :], ps[0][:, 0:48], M.bias[:, :], ALU.add).then_inc(own.sem, o.up())
                dve.wait_ge(own.sem, o.value())
                for gain, part, g in ((M.gain1, 1, 4), (M.gain2, 4, 5)):
                    nc.vector.scalar_tensor_tensor(gain[:, :], M.col[:, part * KD:(part + 1) * KD], 1.0,
                                                          S.gains[:, g, :], ALU.add, ALU.mult).then_inc(own.sem, o.up())
                dve.wait_ge(rows_made.sem, rows_made.at(1))
                for g in range(2):
                    for half in range(2):
                        nc.vector.tensor_copy(M.rows[:, g, half * 512:(half + 1) * 512], ps[2 + 2 * g + half][:, :]).then_inc(own.sem, o.up())
                n_own = o.n
        for s, n in ((got, 32), (c_ready, 1), (summed, NC), (turned, 1), (own, n_own), (rows_made, 1), (biased, 1),
                     *((loaded[b], 16 * (NC // NW)) for b in range(NW))):
            s.base += n


def latent_stage(S, lat, latT, qa, q_lat, w_uk_T, gain):
    nc, a, ps = S.nc, S.a, S.ps
    got, squares, inverse, roots, own, normed, turned, copied, made, cleared = (
        S.sig("l_" + x) for x in ("got", "squares", "inverse", "roots", "own", "normed", "turned", "copied", "made", "cleared"))
    with ExitStack() as st:
        uk = S.sb("w_uk_sb", [P, 8, 64], F32, st)
        g = S.sb("g_kv_row", [P, P], F32, st)
        sq = S.sb("lat_sq", [P, TT, P], F32, st)
        ss = S.sb("lat_ss", [P, TT], F32, st)
        r = S.sb("lat_r", [P, TT], F32, st)
        n_own = 0
        with nc.Block("latent") as block:
            @block.gpsimd
            def _(pool):
                nc.gpsimd.memset(uk[:, :, 0:16], 0.0).then_inc(cleared.sem, 1)

            @block.sync
            def _(sp):
                sp.dma_start(uk[:, :, 16:64], a["w_uk_2"][0]).then_inc(got.sem, 16)
                sp.dma_start(g[:, :], a["g_kv_2"][0].partition_broadcast(P)).then_inc(got.sem, 16)

            @block.scalar
            def _(act):
                for t in range(TT):
                    nc.scalar.activation(sq[:, t, :], lat[:, t, :], ACT.Square, accum_out=ss[:, t:t + 1]).then_inc(squares.sem, 1)
                act.wait_ge(inverse.sem, inverse.at(1))
                nc.scalar.activation(r[:, :], ss[:, :], ACT.Sqrt).then_inc(roots.sem, 1)
                for h in range(8):
                    act.wait_ge(made.sem, made.at(h + 1))
                    nc.scalar.activation(q_lat[:, h, :], ps[h][:, :], ACT.Copy).then_inc(copied.sem, 1)

            @block.vector
            def _(dve):
                nonlocal n_own
                o = Count(own)
                dve.wait_ge(squares.sem, squares.at(TT))
                nc.vector.tensor_scalar(ss[:, :], ss[:, :], 1.0 / P, EPS, ALU.mult, ALU.add).then_inc(own.sem, o.up())
                dve.wait_ge(own.sem, o.value())
                nc.vector.reciprocal(ss[:, :], ss[:, :]).then_inc(inverse.sem, 1)
                dve.wait_ge(roots.sem, roots.at(1))
                dve.wait_ge(got.sem, got.at(32))
                for t in range(TT):
                    nc.vector.scalar_tensor_tensor(lat[:, t, :], lat[:, t, :], r[:, t:t + 1], g[:, :], ALU.mult,
                                                   ALU.mult).then_inc(normed.sem, 1)
                dve.wait_ge(turned.sem, turned.at(1))
                nc.vector.tensor_copy(w_uk_T[:, :, :], ps[0][:, :].rearrange("p (m r) -> p m r", m=4)).then_inc(own.sem, o.up())
                dve.wait_ge(turned.sem, turned.at(2))
                nc.vector.tensor_copy(latT[:, :], ps[1][:, :]).then_inc(own.sem, o.up())
                n_own = o.n

            @block.tensor
            def _(pe):
                pe.wait_ge(got.sem, got.at(32))
                pe.wait_ge(cleared.sem, cleared.at(1))
                for m in range(4):
                    last = nc.tensor.transpose(ps[0][:, m * P:(m + 1) * P], uk[:, 2 * m:2 * m + 2, :].rearrange("p h n -> p (h n)"),
                                               S.const("ident"))
                last.then_inc(turned.sem, 1)
                pe.wait_ge(normed.sem, normed.at(TT))
                for t in range(TT):
                    last = nc.tensor.transpose(ps[1][:, t * P:(t + 1) * P], lat[:, t, :], S.const("ident"))
                last.then_inc(turned.sem, 1)
                pe.wait_ge(own.sem, own.at(3))
                for h in range(8):
                    b = 64 * (h % 2)
                    nc.tensor.matmul(ps[h][:, :], w_uk_T[b:b + 64, h // 2, :], qa[b:b + 64, h // 2, :], start=True,
                                     stop=True).then_inc(made.sem, 1)
        for s, n in ((got, 32), (squares, TT), (inverse, 1), (roots, 1), (own, n_own), (normed, TT), (turned, 2), (copied, 8),
                     (made, 8), (cleared, 1)):
            s.base += n


def index_stage(S, iq, ik, iw, bias):
    nc, ps = S.nc, S.ps
    H = 8
    dots, relus, own, weighed = (S.sig("i_" + x) for x in ("dots", "relus", "own", "weighed"))
    n_own = 0
    with ExitStack() as st:
        work = S.sb("index_work", [P, TT - 1, T], F32, st)
        r = S.sb("index_relu", [P, 4, T], F32, st)
        best = S.sb("index_best", [P, TT - 1, 8], F32, st)
        w = S.sb("index_w", [P, TT, H], F32, st)
        with nc.Block("indexer") as block:
            @block.tensor
            def _(pe):
                for t in range(1, TT):
                    K = (t + 1) * P
                    for h in range(H):
                        n = (t - 1) * H + h
                        b = 32 * (h % 4)
                        if n >= 8:
                            pe.wait_ge(relus.sem, relus.at(n - 7))
                        nc.tensor.matmul(ps[n % 8][:, 0:K], iq[b:b + 32, h // 4, t * P:(t + 1) * P], ik[b:b + 32, 0:K],
                                         start=True, stop=True).then_inc(dots.sem, 1)

            @block.scalar
            def _(act):
                for t in range(1, TT):
                    for h in range(H):
                        n = (t - 1) * H + h
                        act.wait_ge(dots.sem, dots.at(n + 1))
                        if n >= 4:
                            act.wait_ge(weighed.sem, weighed.at(n - 3))
                        K = (t + 1) * P
                        nc.scalar.activation(r[:, n % 4, 0:K], ps[n % 8][:, 0:K], ACT.Relu, scale=32 ** -0.5).then_inc(relus.sem, 1)

            @block.vector
            def _(dve):
                nonlocal n_own
                o = Count(own)
                nc.vector.tensor_scalar(w[:, :, :], iw[:, :, :], 8 ** -0.5, None, ALU.mult).then_inc(own.sem, o.up())
                dve.wait_ge(own.sem, o.value())
                for t in range(1, TT):
                    K = (t + 1) * P
                    s = work[:, t - 1, 0:K]
                    for h in range(H):
                        n = (t - 1) * H + h
                        dve.wait_ge(relus.sem, relus.at(n + 1))
                        wt = w[:, t, h:h + 1]
                        if h == 0:
                            ins = nc.vector.tensor_scalar(s, r[:, n % 4, 0:K], wt, None, ALU.mult)
                        else:
                            dve.wait_ge(weighed.sem, weighed.at(n))
                            ins = nc.vector.scalar_tensor_tensor(s, r[:, n % 4, 0:K], wt, s, ALU.mult, ALU.add)
                        ins.then_inc(weighed.sem, 1)
                    dve.wait_ge(weighed.sem, weighed.at(H * t))
                    d = work[:, t - 1, t * P:K]
                    nc.vector.tensor_tensor(d, d, S.const("causal"), ALU.add).then_inc(own.sem, o.up())
                for i in range(DSA_TOPK // 8):
                    dve.wait_ge(own.sem, o.value())
                    for t in range(1, TT):
                        nc.vector.max(best[:, t - 1, :], work[:, t - 1, 0:(t + 1) * P]).then_inc(own.sem, o.up())
                    dve.wait_ge(own.sem, o.value())
                    for t in range(1, TT):
                        s = work[:, t - 1, 0:(t + 1) * P]
                        nc.vector.match_replace(s, best[:, t - 1, :], s, TAKEN).then_inc(own.sem, o.up())
                dve.wait_ge(own.sem, o.value())
                for t in range(1, TT):
                    K = (t + 1) * P
                    nc.vector.tensor_scalar(bias[:, t - 1, 0:K], work[:, t - 1, 0:K], -2.0e38, -NEG, ALU.is_le, ALU.mult).then_inc(own.sem, o.up())
                dve.wait_ge(own.sem, o.value())
                for t in range(1, TT):
                    K = (t + 1) * P
                    nc.vector.tensor_scalar(bias[:, t - 1, 0:K], bias[:, t - 1, 0:K], NEG, None, ALU.add).then_inc(own.sem, o.up())
                n_own = o.n


def attention_stage(S, A, mix):
    nc, ps = S.nc, S.ps
    items = [(t, h, kind) for t in range(TT) for h in range(8) for kind in "ab"]
    N = len(items)
    n_a = [sum(1 for x in items[:i] if x[2] == "a") for i in range(N + 1)]
    s_ = lambda x: S.sig("x_" + x)
    ready, logits, masked, scaled, exps, turned, copied, lat_made, lat_copied, made, inverse, taken, zeroed, cum_own = (
        s_(x) for x in ("ready", "logits", "masked", "scaled", "exps", "turned", "copied", "lat_made", "lat_copied", "made",
                        "inverse", "taken", "zeroed", "cum"))
    got = s_("got")
    ident = S.const("ident")
    with ExitStack() as st:
        cum = S.sb("cum", [8, T], F32, st)
        ncum = S.sb("ncum", [8, T], F32, st)
        past = S.sb("past_bias", [P, T], F32, st)
        uv = S.sb("w_uv_sb", [P, 8, 64], F32, st)
        lg = S.sb("logits_sb", [P, 3, T], F32, st)
        pT = S.sb("probs_t", [P, 2, T], F32, st)
        olT = S.sb("o_lat", [P, 2, P], F32, st)
        top = S.sb("row_max", [P, N], F32, st)
        rsum = S.sb("row_sum", [P, N], F32, st)
        rinv = S.sb("row_inv", [P, N], F32, st)

        def bias_of(t, kind):
            K = (t + 1) * P
            if kind == "b" or t == 0:
                return past[:, T - K:T]
            return A.bias[:, t - 1, 0:K]

        with nc.Block("attention") as block:
            @block.sync
            def _(sp):
                sp.dma_start(uv[:, :, :], A.w_uv).then_inc(got.sem, 16)

            @block.vector
            def _(dve):
                nc.vector.memset(past[:, 0:T - P], 0.0).then_inc(zeroed.sem, 1)
                nc.vector.tensor_copy(past[:, T - P:T], S.const("causal")).then_inc(zeroed.sem, 1)
                nc.vector.tensor_tensor_scan(cum[:, :], A.ones8, A.logf[:, :], 0.0, ALU.mult, ALU.add).then_inc(cum_own.sem, 1)
                dve.wait_ge(cum_own.sem, cum_own.at(1))
                nc.vector.tensor_scalar(ncum[:, :], cum[:, :], -1.0, None, ALU.mult).then_inc(cum_own.sem, 1)
                dve.wait_ge(zeroed.sem, zeroed.at(2))
                for i in range(N + 4):
                    if i < N:
                        t, h, kind = items[i]
                        K = (t + 1) * P
                        dve.wait_ge(logits.sem, logits.at(i + 1))
                        if i >= 3:
                            dve.wait_ge(turned.sem, turned.at(i - 2))
                        nc.vector.tensor_tensor_reduce(out=lg[:, i % 3, 0:K], in0=ps[i % 3][:, 0:K], in1=bias_of(t, kind),
                                                       scale=1.0, scalar=-3.0e38, op0=ALU.add, op1=ALU.max,
                                                       accum_out=top[:, i:i + 1]).then_inc(masked.sem, 1)
                        dve.wait_ge(masked.sem, masked.at(i + 1))
                        nc.vector.tensor_scalar(top[:, i:i + 1], top[:, i:i + 1], -0.125 if kind == "a" else -1.0, None,
                                                ALU.mult).then_inc(scaled.sem, 1)
                    j = i - 2
                    if 0 <= j < N:
                        t, h, kind = items[j]
                        K = (t + 1) * P
                        dve.wait_ge(turned.sem, turned.at(j + 1))
                        if j >= 2:
                            if items[j - 2][2] == "a":
                                dve.wait_ge(lat_made.sem, lat_made.at(n_a[j - 1]))
                            else:
                                dve.wait_ge(made.sem, made.at(j - 1))
                        nc.vector.tensor_copy(pT[:, j % 2, 0:K], ps[3 + j % 2][:, 0:K]).then_inc(copied.sem, 1)
                        dve.wait_ge(exps.sem, exps.at(j + 1))
                        nc.vector.reciprocal(rinv[:, j:j + 1], rsum[:, j:j + 1]).then_inc(inverse.sem, 1)
                    j = i - 4
                    if 0 <= j < N:
                        t, h, kind = items[j]
                        dve.wait_ge(made.sem, made.at(j + 1))
                        dve.wait_ge(inverse.sem, inverse.at(j + 1))
                        at = (0 if kind == "a" else 512) + h * 64
                        nc.vector.tensor_scalar(mix[:, t, at:at + 64], ps[6 + j % 2][:, 0:64], rinv[:, j:j + 1], None,
                                                ALU.mult).then_inc(taken.sem, 1)

            @block.scalar
            def _(act):
                for i in range(N + 3):
                    if i < N:
                        t, h, kind = items[i]
                        K = (t + 1) * P
                        act.wait_ge(scaled.sem, scaled.at(i + 1))
                        nc.scalar.activation(lg[:, i % 3, 0:K], lg[:, i % 3, 0:K], ACT.Exp, bias=top[:, i:i + 1],
                                             scale=0.125 if kind == "a" else 1.0,
                                             accum_out=rsum[:, i:i + 1]).then_inc(exps.sem, 1)
                    j = i - 3
                    if 0 <= j < N and items[j][2] == "a":
                        act.wait_ge(lat_made.sem, lat_made.at(n_a[j] + 1))
                        if n_a[j] >= 2:
                            act.wait_ge(made.sem, made.at([x for x in range(N) if items[x][2] == "a"][n_a[j] - 2] + 1))
                        nc.scalar.activation(olT[:, n_a[j] % 2, :], ps[5][:, 0:P], ACT.Copy).then_inc(lat_copied.sem, 1)

            @block.tensor
            def _(pe):
                pe.wait_ge(got.sem, got.at(16))
                pe.wait_ge(cum_own.sem, cum_own.at(2))
                for i in range(N + 4):
                    if i < N:
                        t, h, kind = items[i]
                        K = (t + 1) * P
                        q = slice(t * P, (t + 1) * P)
                        b = 64 * (h % 2)
                        if i >= 3:
                            pe.wait_ge(masked.sem, masked.at(i - 2))
                        out = ps[i % 3][:, 0:K]
                        if kind == "a":
                            nc.tensor.matmul(out, A.q_lat[:, h, q], A.latT[:, 0:K], start=True, stop=False)
                            last = nc.tensor.matmul(out, A.qa[b:b + 16, h // 2, q], A.kr[b:b + 16, 0:K], start=False, stop=True)
                        else:
                            nc.tensor.matmul(out, A.qb[b:b + 64, h // 2, q], A.kb[b:b + 64, h // 2, 0:K], start=True, stop=False)
                            nc.tensor.matmul(out, cum[:, q], ident[0:8, h:h + 1].broadcast_to([8, K]), start=False, stop=False)
                            last = nc.tensor.matmul(out, ident[0:8, h:h + 1].broadcast_to([8, P]), ncum[:, 0:K], start=False,
                                                    stop=True)
                        last.then_inc(logits.sem, 1)
                    j = i - 2
                    if 0 <= j < N:
                        pe.wait_ge(exps.sem, exps.at(j + 1))
                        if j >= 2:
                            pe.wait_ge(copied.sem, copied.at(j - 1))
                        for kt in range(items[j][0] + 1):
                            last = nc.tensor.transpose(ps[3 + j % 2][:, kt * P:(kt + 1) * P], lg[:, j % 3, kt * P:(kt + 1) * P], ident)
                        last.then_inc(turned.sem, 1)
                    j = i - 3
                    if 0 <= j < N:
                        t, h, kind = items[j]
                        pe.wait_ge(copied.sem, copied.at(j + 1))
                        if kind == "a":
                            if n_a[j] >= 1:
                                pe.wait_ge(lat_copied.sem, lat_copied.at(n_a[j]))
                            for kt in range(t + 1):
                                last = nc.tensor.matmul(ps[5][:, 0:P], A.lat[:, kt, :], pT[:, j % 2, kt * P:(kt + 1) * P],
                                                        start=(kt == 0), stop=(kt == t))
                            last.then_inc(lat_made.sem, 1)
                    j = i - 4
                    if 0 <= j < N and items[j][2] == "a":
                        t, h, kind = items[j]
                        pe.wait_ge(lat_copied.sem, lat_copied.at(n_a[j] + 1))
                        if j >= 2:
                            pe.wait_ge(taken.sem, taken.at(j - 1))
                        nc.tensor.matmul(ps[6 + j % 2][:, 0:64], olT[:, n_a[j] % 2, :], uv[:, h, :], start=True,
                                         stop=True).then_inc(made.sem, 1)
                    j = i - 3
                    if 0 <= j < N and items[j][2] == "b":
                        t, h, kind = items[j]
                        if j >= 2:
                            pe.wait_ge(taken.sem, taken.at(j - 1))
                        for kt in range(t + 1):
                            last = nc.tensor.matmul(ps[6 + j % 2][:, 0:64], pT[:, j % 2, kt * P:(kt + 1) * P],
                                                    A.v[:, kt, h * 64:(h + 1) * 64], start=(kt == 0), stop=(kt == t))
                        last.then_inc(made.sem, 1)


def attention2(S, M):
    nc, a = S.nc, S.a
    w = a["w_in_2"][0]
    norm_stage(S, "norm4", M.gain1[:, :], shift=M.col[:, 0:KD])
    A = Routing()
    with ExitStack() as st:
        mix = S.sb("mix2", [P, TT, D], F32, st)
        with ExitStack() as st2:
            A.qa = S.sb("qa2", [P, 4, T], F32, st2)
            A.qb = S.sb("qb2", [P, 4, T], F32, st2)
            A.kb = S.sb("kb2", [P, 4, T], F32, st2)
            A.v = S.sb("vb2", [P, TT, 512], F32, st2)
            A.lat = S.sb("lat2", [P, TT, P], F32, st2)
            A.latT = S.sb("lat2T", [P, T], F32, st2)
            A.kr = S.sb("kr2", [P, T], F32, st2)
            A.q_lat = S.sb("q_lat", [P, 8, T], F32, st2)
            A.bias = S.sb("dsa_bias", [P, TT - 1, T], F32, st2)
            A.logf = S.sb("logf2", [8, T], F32, st2)
            A.ones8 = S.const("ones")[0:8, 0:1].broadcast_to([8, T])
            A.w_uv = a["w_uv_2"][0]
            iq = S.sb("iq2", [P, 2, T], F32, st2)
            ik = S.sb("ik2", [P, T], F32, st2)
            iw = S.sb("iw2", [P, TT, 8], F32, st2)
            f = S.sb("f2", [8, T], F32, st2)
            project_stage(S, "proj2", [
                (w[:, 0:512], "T", "copy", lambda m: A.qa[:, m, :]),
                (w[:, 512:640], "tok", "copy", lambda t: A.lat[:, t, :]),
                ([w[:, 640:704], w[:, 640:704]], "T", "copy", lambda m: A.kr[:, :]),
                (w[:, 656:912], "T", "copy", lambda m: iq[:, m, :]),
                ([w[:, 912:944]] * 4, "T", "copy", lambda m: ik[:, :]),
                (w[:, 944:952], "tok", "copy", lambda t: iw[:, t, :]),
                (w[:, 2488:2496], "T", "copy", lambda m: f[:, :]),
                (w[:, 952:1464], "T", 64 ** -0.5, lambda m: A.qb[:, m, :]),
                (w[:, 1464:1976], "T", "copy", lambda m: A.kb[:, m, :]),
                (w[:, 1976:2488], "tok", "copy", lambda t: A.v[:, t, :])])
            with ExitStack() as st3:
                ca, sa, ci, si = (S.sb(x, [P, T], F32, st3) for x in ("cos_a", "sin_a", "cos_i", "sin_i"))
                angle_stage(S, "angles2", a["positions_2"][0], [S.const("freq")[:, 1:2], S.const("freq")[:, 2:3]],
                            [(ca[:, :], sa[:, :]), (ci[:, :], si[:, :])])
                rotate_stage(S, "rotary2", [(A.qa[:, m, :], S.const("swap_a"), ca, sa) for m in range(4)]
                             + [(A.kr[:, :], S.const("swap_a"), ca, sa)]
                             + [(iq[:, m, :], S.const("swap_i"), ci, si) for m in range(2)]
                             + [(ik[:, :], S.const("swap_i"), ci, si)])
            with ExitStack() as st3:
                ukT = S.sb("w_uk_T", [P, 4, P], F32, st3)
                bf = S.sb("b_forget", [8, 1], F32, st3)
                load_stage(S, "load_bf", [(bf[:, :], a["b_forget_2"][0].rearrange("(h o) -> h o", o=1))])
                latent_stage(S, A.lat, A.latT, A.qa, A.q_lat, ukT, None)
                log_gate_stage(S, "log_forget", [(S.const("ident")[0:8, 0:8], f[:, :], bf[:, :], A.logf[:, :])], 1.0)
            index_stage(S, iq, ik, iw, A.bias)
            attention_stage(S, A, mix)
        head_norm_stage(S, "headnorm2", mix, 512, [(0, a["g_out_a_2"][0]), (512, a["g_out_b_2"][0])], None)
        w_out = a["w_out_2"][0]
        project_stage(S, "out2", [(w_out[:, c * 512:(c + 1) * 512], "tok", M.rows[:, 0, c * 512:(c + 1) * 512],
                                   lambda t, c=c: S.h[:, t, c * 512:(c + 1) * 512]) for c in range(2)])


def modulation(S, stack):
    M = Routing()
    M.col = S.sb("mod_col", [P, 48], F32, stack)
    M.bias = S.sb("mod_bias", [P, 48], F32, stack)
    M.gain1 = S.sb("mod_gain1", [P, KD], F32, stack)
    M.gain2 = S.sb("mod_gain2", [P, KD], F32, stack)
    M.rows = S.sb("mod_rows", [P, 2, D], F32, stack)
    ada_stage(S, M)
    return M


def peer_route_stage(S, G, qT, keysT):
    nc, ps = S.nc, S.ps
    NK, H = PEER_K, PEER_HEADS
    scored, copied, own, exps_in, exps, own_p = (S.sig("u_" + x) for x in ("scored", "copied", "own", "exps_in", "exps", "own_p"))
    iota = S.const("iota16")
    with ExitStack() as st:
        s = S.sb("peer_s", [P, 2, H, 2, P], F32, st)
        v = S.sb("peer_v16", [P, H, 2, NK], F32, st)
        vi = S.sb("peer_i16", [P, H, 2, NK], U32, st)
        vf = S.sb("peer_f16", [P, H, 2, NK], F32, st)
        cand = S.sb("peer_cand", [P, H, NK, NK], F32, st)
        best = S.sb("peer_best", [P, H, NK], F32, st)
        at = S.sb("peer_at", [P, H, NK], U32, st)
        half = S.sb("peer_half", [P, 2, H, NK], U32, st)
        half_f = S.sb("peer_halff", [P, 2, H, NK], F32, st)
        hit = S.sb("peer_hit", [P, 2, H, NK, NK], F32, st)
        key = S.sb("peer_key", [P, 2, H, NK], F32, st)
        total = S.sb("peer_total", [P, H, 1], F32, st)
        with nc.Block("peer_route") as block:
            @block.tensor
            def _(pe):
                for t in range(TT):
                    for h in range(H):
                        if t >= 2:
                            pe.wait_ge(copied.sem, copied.at(4 * (t - 2) + 2 * (h // 4) + 2))
                        for side in range(2):
                            b = 64 * side
                            last = nc.tensor.matmul(ps[(t % 2) * 4 + 2 * side + h // 4][:, (h % 4) * P:(h % 4 + 1) * P],
                                                    qT[b:b + 64, h, t * P:(t + 1) * P], keysT[b:b + 64, :], start=True, stop=True)
                            last.then_inc(scored.sem, 1)

            def softmax_exp(act, t):
                act.wait_ge(exps_in.sem, exps_in.at(t + 1))
                g = G.gate[:, t, :].rearrange("p (h k) -> p h k", h=H)
                nc.scalar.activation(g, g, ACT.Exp).then_inc(exps.sem, 1)

            @block.scalar
            def _(act):
                for t in range(TT):
                    for hh in range(2):
                        act.wait_ge(scored.sem, scored.at(2 * (t * H + 4 * hh + 4)))
                        if t >= 2:
                            act.wait_ge(exps_in.sem, exps_in.at(t - 1))
                        for side in range(2):
                            nc.scalar.activation(s[:, t % 2, 4 * hh:4 * hh + 4, side, :],
                                                 ps[(t % 2) * 4 + 2 * side + hh][:, :].rearrange("p (h n) -> p h n", h=4),
                                                 ACT.Copy).then_inc(copied.sem, 1)
                    if t:
                        softmax_exp(act, t - 1)
                softmax_exp(act, TT - 1)

            @block.vector
            def _(dve):
                o = Count(own)
                for t in range(TT):
                    dve.wait_ge(copied.sem, copied.at(4 * (t + 1)))
                    rows = [(h, side) for h in range(H) for side in range(2)]
                    for r in range(2):
                        sl = slice(8 * r, 8 * r + 8)
                        for h, side in rows:
                            nc.vector.max(v[:, h, side, sl], s[:, t % 2, h, side, :]).then_inc(own.sem, o.up())
                        dve.wait_ge(own.sem, o.value())
                        for h, side in rows:
                            nc.vector.max_index(vi[:, h, side, sl], v[:, h, side, sl], s[:, t % 2, h, side, :]).then_inc(own.sem, o.up())
                        dve.wait_ge(own.sem, o.value())
                        if r == 0:
                            for h, side in rows:
                                x = s[:, t % 2, h, side, :]
                                nc.vector.match_replace(x, v[:, h, side, sl], x, TAKEN).then_inc(own.sem, o.up())
                            dve.wait_ge(own.sem, o.value())
                    nc.vector.tensor_copy(vf[:, :, :, :], vi[:, :, :, :]).then_inc(own.sem, o.up())
                    nc.vector.tensor_tensor(cand[:, :, :, :], v[:, :, 0, :].unsqueeze(3).broadcast_to([P, H, NK, NK]),
                                                   v[:, :, 1, :].unsqueeze(2).broadcast_to([P, H, NK, NK]), ALU.add).then_inc(own.sem, o.up())
                    dve.wait_ge(own.sem, o.value())
                    for r in range(2):
                        sl = slice(8 * r, 8 * r + 8)
                        for h in range(H):
                            nc.vector.max(best[:, h, sl], cand[:, h, :, :].rearrange("p a b -> p (a b)")).then_inc(own.sem, o.up())
                        dve.wait_ge(own.sem, o.value())
                        for h in range(H):
                            nc.vector.max_index(at[:, h, sl], best[:, h, sl], cand[:, h, :, :].rearrange("p a b -> p (a b)")).then_inc(own.sem, o.up())
                        dve.wait_ge(own.sem, o.value())
                        if r == 0:
                            for h in range(H):
                                x = cand[:, h, :, :].rearrange("p a b -> p (a b)")
                                nc.vector.match_replace(x, best[:, h, sl], x, TAKEN).then_inc(own.sem, o.up())
                            dve.wait_ge(own.sem, o.value())
                    g = G.gate[:, t, :].rearrange("p (h k) -> p h k", h=H)
                    nc.vector.tensor_tensor(g, best[:, :, :], best[:, :, 0:1].broadcast_to([P, H, NK]),
                                            ALU.subtract).then_inc(exps_in.sem, 1)
                    nc.vector.tensor_scalar(half[:, 0, :, :], at[:, :, :], 4, None, ALU.logical_shift_right).then_inc(own.sem, o.up())
                    nc.vector.tensor_scalar(half[:, 1, :, :], at[:, :, :], 15, None, ALU.bitwise_and).then_inc(own.sem, o.up())
                    dve.wait_ge(own.sem, o.value())
                    nc.vector.tensor_copy(half_f[:, :, :, :], half[:, :, :, :]).then_inc(own.sem, o.up())
                    dve.wait_ge(own.sem, o.value())
                    for side in range(2):
                        nc.vector.tensor_tensor(hit[:, side, :, :, :],
                                                       half_f[:, side, :, :].unsqueeze(3).broadcast_to([P, H, NK, NK]),
                                                       iota.unsqueeze(1).unsqueeze(1).broadcast_to([P, H, NK, NK]), ALU.is_equal).then_inc(own.sem, o.up())
                    dve.wait_ge(own.sem, o.value())
                    for side in range(2):
                        nc.vector.tensor_tensor(hit[:, side, :, :, :], hit[:, side, :, :, :],
                                                       vf[:, :, side, :].unsqueeze(2).broadcast_to([P, H, NK, NK]), ALU.mult).then_inc(own.sem, o.up())
                    dve.wait_ge(own.sem, o.value())
                    for side in range(2):
                        nc.vector.tensor_reduce(key[:, side, :, :], hit[:, side, :, :, :], AX.X, ALU.add).then_inc(own.sem, o.up())
                    dve.wait_ge(own.sem, o.value())
                    nc.vector.scalar_tensor_tensor(key[:, 0, :, :], key[:, 0, :, :], float(P), key[:, 1, :, :], ALU.mult, ALU.add).then_inc(own.sem, o.up())
                    dve.wait_ge(own.sem, o.value())
                    nc.vector.tensor_copy(G.expert[:, t, :].rearrange("p (h k) -> p h k", h=H), key[:, 0, :, :]).then_inc(own.sem, o.up())
                    dve.wait_ge(exps.sem, exps.at(t + 1))
                    nc.vector.tensor_reduce(total[:, :, :], g, AX.X, ALU.add).then_inc(own.sem, o.up())
                    dve.wait_ge(own.sem, o.value())
                    nc.vector.reciprocal(total[:, :, :], total[:, :, :]).then_inc(own.sem, o.up())
                    dve.wait_ge(own.sem, o.value())
                    nc.vector.tensor_tensor(g, g, total[:, :, :].broadcast_to([P, H, NK]), ALU.mult).then_inc(own.sem, o.up())
                    dve.wait_ge(own.sem, o.value())


def peer_experts_stage(S, G, h2, M):
    nc, a, ps, h = S.nc, S.a, S.ps, S.h
    B = 8
    NG = PICKS // B
    s_ = lambda x: S.sig("y_" + x)
    u_in = [S.sig(f"y_u_in{b}", pool_dma=True) for b in range(B)]
    v_in = [S.sig(f"y_v_in{b}", pool_dma=True) for b in range(B)]
    staged, staged_v, dotted, dots_out, acted, diags, pe_done, weighed, w_staged, h_staged, fin, zeroed, activated = (
        s_(x) for x in ("staged", "staged_v", "dotted", "dots_out", "acted", "diags", "pe_done", "weighed", "w_staged",
                        "h_staged", "fin", "zeroed", "activated"))
    table_u, table_v = a["peer_u_2"][0], a["peer_v_2"][0]
    with ExitStack() as st:
        ring = S.sb("peer_ring", [P, B, D], F32, st)
        index = S.sb("peer_index", [P, B], I32, st)
        h2t = S.sb("peer_h2t", [P, D], F32, st)
        dots = S.sb("peer_dots", [P, B], F32, st)
        act_all = S.sb("peer_act", [P, PICKS], F32, st)
        wgt = S.sb("peer_wgt", [P, PICKS], F32, st)
        diag = S.sb("peer_diag", [P, B, P], F32, st)
        acc = S.sb("peer_acc", [P, D], F32, st)
        zero = S.sb("peer_zero", [P, BANK], BF16, st)
        with nc.Block("peer_experts") as block:
            @block.gpsimd
            def _(pool):
                with pool.Fori(0, TT) as t:
                    with pool.Fori(0, NG) as i:
                        n = t * NG + i
                        pool.wait_ge(dotted.sem, dotted.at(B * n))
                        settle(pool, S.sig("passed_pool"))
                        nc.gpsimd.tensor_copy(index[:, :], G.expert[:, bass.ds(t, 1), bass.ds(i * B, B)].rearrange(
                            "p o k -> p (o k)")).then_inc(staged.sem, 1)
                        pool.wait_ge(staged.sem, staged.at(n + 1))
                        settle(pool, S.sig("passed_pool"))
                        for b in range(B):
                            pool.indirect_dma_start(out=ring[:, b, :], out_offset=None, in_=table_u,
                                                    in_offset=bass.IndirectOffsetOnAxis(ap=index[:, b:b + 1], axis=0),
                                                    ).then_inc(u_in[b].sem, 16)
                    for b in range(B):
                        pool.wait_ge(u_in[b].sem, u_in[b].at(16 * NG * (t + 1)))
                    pool.wait_ge(dotted.sem, dotted.at(PICKS * (t + 1)))
                    settle(pool, S.sig("passed_pool"))
                    with pool.Fori(0, NG) as i:
                        n = t * NG + i
                        pool.wait_ge(pe_done.sem, pe_done.at((B // 2) * n))
                        pool.wait_ge(weighed.sem, weighed.at((B // 2) * n))
                        settle(pool, S.sig("passed_pool"))
                        nc.gpsimd.tensor_copy(index[:, :], G.expert[:, bass.ds(t, 1), bass.ds(i * B, B)].rearrange(
                            "p o k -> p (o k)")).then_inc(staged_v.sem, 1)
                        pool.wait_ge(staged_v.sem, staged_v.at(n + 1))
                        settle(pool, S.sig("passed_pool"))
                        for b in range(B):
                            pool.indirect_dma_start(out=ring[:, b, :], out_offset=None, in_=table_v,
                                                    in_offset=bass.IndirectOffsetOnAxis(ap=index[:, b:b + 1], axis=0),
                                                    ).then_inc(v_in[b].sem, 16)
                    pool.wait_ge(pe_done.sem, pe_done.at(PICKS // 2 * (t + 1)))
                    pool.wait_ge(weighed.sem, weighed.at(PICKS // 2 * (t + 1)))
                    for b in range(B):
                        pool.wait_ge(v_in[b].sem, v_in[b].at(16 * NG * (t + 1)))
                    settle(pool, S.sig("passed_pool"))

            @block.vector
            def _(dve):
                nc.vector.memset(zero[:, :], 0.0).then_inc(zeroed.sem, 1)
                with dve.Fori(0, TT) as t:
                    nc.vector.tensor_copy(h2t[:, :], h2[:, bass.ds(t, 1), :].rearrange("p o d -> p (o d)")).then_inc(h_staged.sem, 1)
                    dve.wait_ge(h_staged.sem, h_staged.at(t + 1))
                    settle(dve, S.sig("passed_dve"))
                    with dve.Fori(0, NG) as i:
                        n = t * NG + i
                        dve.wait_ge(dots_out.sem, dots_out.at(n))
                        for b in range(B):
                            dve.wait_ge(u_in[b].sem, u_in[b].at(16 * (n + 1)))
                            nc.vector.scalar_tensor_tensor(ring[:, b, :], ring[:, b, :], 1.0, h2t[:, :], ALU.mult, ALU.mult,
                                                           accum_out=dots[:, b:b + 1]).then_inc(dotted.sem, 1)
                        dve.wait_ge(dotted.sem, dotted.at(B * (n + 1)))
                        settle(dve, S.sig("passed_dve"))
                        nc.vector.tensor_copy(act_all[:, bass.ds(i * B, B)], dots[:, :]).then_inc(dots_out.sem, 1)
                    dve.wait_ge(acted.sem, acted.at(t + 1))
                    nc.vector.tensor_tensor(wgt[:, :], act_all[:, :], G.gate[:, bass.ds(t, 1), :].rearrange("p o k -> p (o k)"),
                                            ALU.mult).then_inc(w_staged.sem, 1)
                    nc.vector.memset(acc[:, :], 0.0).then_inc(activated.sem, 1)
                    dve.wait_ge(w_staged.sem, w_staged.at(t + 1))
                    dve.wait_ge(activated.sem, activated.at(t + 1))
                    settle(dve, S.sig("passed_dve"))
                    with dve.Fori(0, NG) as i:
                        n = t * NG + i
                        for b in range(0, B, 2):
                            dve.wait_ge(v_in[b].sem, v_in[b].at(16 * (n + 1)))
                            dve.wait_ge(weighed.sem, weighed.at((B // 2) * n + b // 2))
                            nc.vector.scalar_tensor_tensor(acc[:, :], ring[:, b, :], wgt[:, bass.ds(i * B + b, 1)], acc[:, :],
                                                           ALU.mult, ALU.add).then_inc(weighed.sem, 1)
                    dve.wait_ge(pe_done.sem, pe_done.at(PICKS // 2 * (t + 1)))
                    dve.wait_ge(weighed.sem, weighed.at(PICKS // 2 * (t + 1)))
                    ht = h[:, bass.ds(t, 1), :].rearrange("p o d -> p (o d)")
                    for half in range(2):
                        sl = slice(half * 512, (half + 1) * 512)
                        nc.vector.tensor_tensor(acc[:, sl], acc[:, sl], ps[half][:, :], ALU.add).then_inc(fin.sem, 1)
                    dve.wait_ge(fin.sem, fin.at(4 * t + 2))
                    nc.vector.tensor_tensor(acc[:, :], acc[:, :], M.rows[:, 1, :], ALU.mult).then_inc(fin.sem, 1)
                    dve.wait_ge(fin.sem, fin.at(4 * t + 3))
                    nc.vector.tensor_tensor(ht, ht, acc[:, :], ALU.add).then_inc(fin.sem, 1)
                    dve.wait_ge(fin.sem, fin.at(4 * t + 4))

            @block.scalar
            def _(act):
                with act.Fori(0, TT) as t:
                    act.wait_ge(dots_out.sem, dots_out.at(NG * (t + 1)))
                    nc.scalar.activation(act_all[:, :], act_all[:, :], ACT.Gelu).then_inc(acted.sem, 1)
                    act.wait_ge(w_staged.sem, w_staged.at(t + 1))
                    settle(act, S.sig("passed_act"))
                    with act.Fori(0, NG) as i:
                        n = t * NG + i
                        act.wait_ge(pe_done.sem, pe_done.at((B // 2) * n))
                        for b in range(1, B, 2):
                            nc.scalar.activation(diag[:, b, :], S.const("ident"), ACT.Copy,
                                                 scale=wgt[:, bass.ds(i * B + b, 1)]).then_inc(diags.sem, 1)

            @block.tensor
            def _(pe):
                pe.wait_ge(zeroed.sem, zeroed.at(1))
                with pe.Fori(0, TT) as t:
                    pe.wait_ge(fin.sem, fin.at(4 * t))
                    for half in range(2):
                        nc.tensor.matmul(ps[half][:, :], zero[:, 0:P], zero[:, :], start=True, stop=False, skip_group_check=True)
                    with pe.Fori(0, NG) as i:
                        n = t * NG + i
                        for b in range(1, B, 2):
                            pe.wait_ge(v_in[b].sem, v_in[b].at(16 * (n + 1)))
                            pe.wait_ge(diags.sem, diags.at((B // 2) * n + b // 2 + 1))
                            for half in range(2):
                                last = nc.tensor.matmul(ps[half][:, :], diag[:, b, :], ring[:, b, half * 512:(half + 1) * 512],
                                                        start=False, stop=(b == B - 1), skip_group_check=True)
                            last.then_inc(pe_done.sem, 1)


def rows_stage(S, name, dst):
    nc, ps, xT = S.nc, S.ps, S.xT
    turned, copied = S.sig("b_turned"), S.sig("b_copied")
    with nc.Block(name) as block:
        @block.tensor
        def _(pe):
            for t in range(TT):
                for half in range(2):
                    for kk in range(4):
                        last = nc.tensor.transpose(ps[2 * t + half][:, kk * P:(kk + 1) * P],
                                                   xT[:, 4 * half + kk, t * P:(t + 1) * P], S.const("ident"))
                    last.then_inc(turned.sem, 1)

        @block.vector
        def _(dve):
            for t in range(TT):
                for half in range(2):
                    dve.wait_ge(turned.sem, turned.at(2 * t + half + 1))
                    nc.vector.tensor_copy(dst[:, t, half * 512:(half + 1) * 512], ps[2 * t + half][:, :]).then_inc(copied.sem, 1)
    turned.base += 8
    copied.base += 8


def keys_stage(S, keysT):
    nc, a, ps = S.nc, S.a, S.ps
    got, turned, copied = S.sig("k_got"), S.sig("k_turned"), S.sig("k_copied")
    with ExitStack() as st:
        keys = S.sb("peer_keys", [P, P], F32, st)
        with nc.Block("peer_keys") as block:
            @block.sync
            def _(sp):
                sp.dma_start(keys[:, 0:64], a["peer_keys1_2"][0]).then_inc(got.sem, 16)
                sp.dma_start(keys[:, 64:128], a["peer_keys2_2"][0]).then_inc(got.sem, 16)

            @block.tensor
            def _(pe):
                pe.wait_ge(got.sem, got.at(32))
                nc.tensor.transpose(ps[0][:, 0:P], keys[:, :], S.const("ident")).then_inc(turned.sem, 1)

            @block.vector
            def _(dve):
                dve.wait_ge(turned.sem, turned.at(1))
                nc.vector.tensor_copy(keysT[:, :], ps[0][:, 0:P]).then_inc(copied.sem, 1)


def peer(S, M):
    w = S.a["w_peer_q_2"][0]
    norm_stage(S, "norm5", M.gain2[:, :], shift=M.col[:, 3 * KD:4 * KD])
    G = Routing()
    with ExitStack() as st:
        h2 = S.sb("h2_rows", [P, TT, D], F32, st)
        G.expert = S.sb("peer_expert", [P, TT, PICKS], I32, st)
        G.gate = S.sb("peer_gate", [P, TT, PICKS], F32, st)
        rows_stage(S, "h2_rows_back", h2)
        with ExitStack() as st2:
            qT = S.sb("peer_q", [P, KD, T], F32, st2)
            keysT = S.sb("peer_kt", [P, P], F32, st2)
            keys_stage(S, keysT)
            project_stage(S, "proj3", [(w[:, c * 512:(c + 1) * 512], "T", "copy", lambda m, c=c: qT[:, 4 * c + m, :])
                                       for c in range(2)])
            peer_route_stage(S, G, qT, keysT)
        peer_experts_stage(S, G, h2, M)


def start_stage(S):
    nc, a = S.nc, S.a
    got = S.sig("start")
    with nc.Block("start") as block:
        @block.sync
        def _(sp):
            sp.dma_start(S.h[:, :, :], a["x"][0].rearrange("(t p) d -> p t d", p=P)).then_inc(got.sem, 16)
            with nc.allow_non_contiguous_dma(reason="gains by feature, a few KB"):
                for i, v in enumerate((a["norm_mix_g"][0], a["norm_ffn_g"][0], a["norm_mix_g"][1], a["norm_ffn_g"][1],
                                       a["g_mix_2"][0], a["g_ffn_2"][0])):
                    sp.dma_start(S.gains[:, i, :], v.rearrange("(k p) -> p k", p=P)).then_inc(got.sem, 16)
            sp.wait_ge(got.sem, got.at(16 * 8))

        @block.scalar
        def _(act):
            act.dma_start(S.consts[:, :], a["consts"]).then_inc(got.sem, 16)
    got.base += 16 * 8


def store_stage(S, dst, src):
    nc = S.nc
    done = S.sig("stored")
    with nc.Block(f"store{done.base}") as block:
        @block.sync
        def _(sp):
            sp.dma_start(dst, src).then_inc(done.sem, 16)
            sp.wait_ge(done.sem, done.at(16))
    done.base += 16


def mixer0(S):
    nc, a = S.nc, S.a
    norm_stage(S, "norm0", S.gains[:, 0, :])
    w = a["ab_w_in"][0]
    with ExitStack() as st:
        mix = S.sb("mix0", [P, TT, D], F32, st)
        gate = S.sb("gate0", [P, TT, D], F32, st)
        heads = mix[:, :, :].rearrange("p t (h d) -> p t h d", h=8)
        va = S.sb("va", [P, TT, 512], F32, st)
        vb = S.sb("vb", [P, TT, 512], F32, st)
        with ExitStack() as st2:
            qa = S.sb("qa", [P, 4, T], F32, st2)
            ka = S.sb("ka", [P, 4, T], F32, st2)
            qkb = S.sb("qkb", [P, 4, T], F32, st2)
            ba = S.sb("ba", [16, T], F32, st2)
            project_stage(S, "proj0", [
                (w[:, 0:512], "T", "copy", lambda m: qa[:, m, :]),
                (w[:, 512:1024], "T", P ** -0.5, lambda m: ka[:, m, :]),
                (w[:, 3584:3600], "T", "copy", lambda m: ba[:, :]),
                (w[:, 2048:2304], "T", 64 ** -0.5, lambda m: qkb[:, m, :]),
                (w[:, 2304:2560], "T", "copy", lambda m: qkb[:, 2 + m, :]),
                (w[:, 1024:1536], "tok", "copy", lambda t: va[:, t, :]),
                (w[:, 2560:3072], "tok", "copy", lambda t: vb[:, t, :]),
                (w[:, 1536:2048], "tok", "silu", lambda t: gate[:, t, 0:512]),
                (w[:, 3072:3584], "tok", "silu", lambda t: gate[:, t, 512:1024])])
            with ExitStack() as st3:
                cos = S.sb("cos_r", [P, T], F32, st3)
                sin = S.sb("sin_r", [P, T], F32, st3)
                angle_stage(S, "angles0", a["positions"][0], [S.const("freq")[:, 0:1]], [(cos[:, :], sin[:, :])])
                rotate_stage(S, "rotary0", [(x[:, m, :], S.const("swap_ret"), cos, sin) for x in (qa, ka) for m in range(4)])
                retention_stage(S, qa, ka, va, heads)
            with ExitStack() as st3:
                logf = S.sb("logf0", [P, 2, T], F32, st3)
                wa = S.sb("wa", [16, 256], F32, st3)
                bias = S.sb("ba2", [P, 2], F32, st3)
                load_stage(S, "load_gla", [(wa[:, :], a["gla_w_a2"][0]),
                                           (bias[:, :], a["gla_b_a2"][0].rearrange("(k p) -> p k", p=P))])
                log_gate_stage(S, "log_alpha", [(wa[:, m * P:(m + 1) * P], ba[:, :], bias[:, m:m + 1], logf[:, m, :])
                                                for m in range(2)], 1.0 / 16.0)
                gated_stage(S, "gla", 2, 2, lambda p: qkb[:, p, :], lambda p: qkb[:, 2 + p, :],
                            lambda p: logf[:, p, :], lambda hd, c: vb[:, c, hd * P:(hd + 1) * P],
                            lambda hd: heads[:, :, 4 + hd, :], 4)
        head_norm_stage(S, "headnorm0", mix, 128,
                        [(i * P, a["ret_norm_g"][0] if i < 4 else a["gla_norm_g"][0]) for i in range(8)], gate)
        add_projection(S, "out0", a["ab_w_out"][0])


def load_stage(S, name, pairs):
    nc = S.nc
    got = S.sig("loads")
    with nc.Block(name) as block:
        @block.sync
        def _(sp):
            with nc.allow_non_contiguous_dma(reason="a few KB of vectors"):
                for dst, src in pairs:
                    sp.dma_start(dst, src).then_inc(got.sem, 16)
            sp.wait_ge(got.sem, got.at(16 * len(pairs)))
    got.base += 16 * len(pairs)


def add_projection(S, name, w):
    project_stage(S, name, [(w[:, c * 512:(c + 1) * 512], "tok", "add", lambda t, c=c: S.h[:, t, c * 512:(c + 1) * 512])
                            for c in range(2)])


def run_stages(S, out):
    S.gains = S.sb("gains", [P, 6, KD])
    start_stage(S)
    mixer0(S)
    norm_stage(S, "norm1", S.gains[:, 1, :])
    ffn_swiglu(S)
    mixer1(S)
    for prefix in ("t_", "h_", "q_"):
        S.retire(prefix)
    moe1(S)
    row_norm_stage(S, "final1", S.a["final_norm_g"])
    M = modulation(S, S.stack)
    attention2(S, M)
    for prefix in ("d_", "l_"):
        S.retire(prefix)
    peer(S, M)
    row_norm_stage(S, "final2", S.a["g_final_2"])
    store_stage(S, out[0].rearrange("(t p) d -> p t d", p=P), S.h[:, :, :])


def program(nc, a, out):
    with ExitStack() as stack:
        S = Stages(nc, stack)
        S.where, n_const = const_layout()
        S.consts = S.sb("consts", [P, n_const])
        S.h = S.sb("h", [P, TT, D])
        S.xT = S.sb("xT", [P, KD, T])
        S.ps = [stack.enter_context(nc.psum_tensor(f"bank{b}", [P, BANK], F32)) for b in range(8)]
        S.a = a
        for name in SIGNALS:
            S.signals[name] = Signal(nc, stack, name, False)
        nc.all_engine_barrier()
        run_stages(S, out)


_INS = ['x', 'positions', 'norm_mix_g', 'norm_ffn_g', 'final_norm_g', 'ab_w_in', 'gla_w_a2', 'gla_b_a2',
        'ret_norm_g', 'gla_norm_g', 'ab_w_out', 'ffn_w_gate', 'ffn_w_up', 'ffn_w_down', 'hgrn_lb_logits',
        'c_w_in', 'hgrn_norm_g', 'c_w_out', 'moe_router', 'moe_w_gate', 'moe_w_up', 'moe_w_down', 'c_2',
        'positions_2', 'w_ada_2', 'b_ada_2', 'g_mix_2', 'w_in_2', 'g_kv_2', 'w_uk_2', 'w_uv_2', 'b_forget_2',
        'g_out_a_2', 'g_out_b_2', 'w_out_2', 'g_ffn_2', 'w_peer_q_2', 'peer_keys1_2', 'peer_keys2_2',
        'peer_u_2', 'peer_v_2', 'g_final_2']


def kernel(**inputs):
    import numpy as _np
    import concourse.bacc as _bacc
    from concourse import mybir as _mybir
    from concourse.bass_utils import run_bass_kernel_spmd as _run

    nc = _bacc.Bacc("TRN2", target_bir_lowering=False, num_devices=1)
    arrays, args = {}, {}
    for name in _INS:
        a = _np.ascontiguousarray(inputs[name])
        arrays[f"in_{name}_dram"] = a
        args[name] = nc.dram_tensor(f"in_{name}_dram", a.shape, _mybir.dt.from_np(a.dtype), kind="ExternalInput").ap()
    consts = const_values()
    arrays["in_consts_dram"] = consts
    args["consts"] = nc.dram_tensor("in_consts_dram", consts.shape, _mybir.dt.from_np(consts.dtype), kind="ExternalInput").ap()
    out = nc.dram_tensor("out_0_dram", (1, T, D), _mybir.dt.from_np(_np.dtype("float32")), kind="ExternalOutput").ap()
    program(nc, args, out)
    r = _run(nc, [arrays], core_ids=[0])
    return r.results[0]["out_0_dram"]
```

```python
from contextlib import ExitStack

import concourse.bass as bass
from concourse import mybir

F32 = mybir.dt.float32
BF16 = mybir.dt.bfloat16
I32 = mybir.dt.int32
U32 = mybir.dt.uint32
ALU = mybir.AluOpType
ACT = mybir.ActivationFunctionType
AX = mybir.AxisListType

P = 128
T = 512
TT = T // P
D = 1024
KD = D // P
EPS = 1e-6
BANK = 512
D_FF = 2816
E_FF = 3584
N_EXP = 8
UNIT_ROWS = (P, 152)
GROUP = 256
UNITS_MAX = (N_EXP, (2 * T + (N_EXP - 1) * (UNIT_ROWS[1] - 1)) // UNIT_ROWS[1])
FIRST_ROW = (0, UNITS_MAX[0] * UNIT_ROWS[0])
ROWS_MAX = (FIRST_ROW[1] + UNITS_MAX[1] * UNIT_ROWS[1] + P - 1) // P * P
LEVELS = 7
NEG = -1.0e30
TAKEN = -3.0e38
DSA_TOPK = 128
PEER_HEADS = 8
PEER_K = 16
N_PEER = 16384
PICKS = PEER_HEADS * PEER_K
MAGIC = 1.5 * 2.0 ** 23
TWO_PI_HI = 6.28125
TWO_PI_MID = 0.0019350051879882812
TWO_PI_LO = 3.019916050561733e-07


def const_layout():
    widths = [("ident", P), ("before", P), ("ones", P), ("causal", P), ("swap_ret", P), ("swap_a", P),
              ("swap_i", P), ("freq", 4), ("levels", (LEVELS + 1) * P), ("decay", 4 * T), ("restart", T),
              ("iota16", 16), ("token", TT), ("eye8", P)]
    at, out = 0, {}
    for name, w in widths:
        out[name] = (at, w)
        at += w
    return out, at


def const_values():
    import numpy as np
    where, n = const_layout()
    c = np.zeros((P, n), np.float32)

    def put(name, a):
        at, w = where[name]
        c[:a.shape[0], at:at + a.shape[1]] = a

    i = np.arange(P)
    put("ident", np.eye(P))
    put("before", (i[:, None] < i[None, :]))
    put("ones", np.ones((P, P)))
    put("causal", np.where(i[None, :] <= i[:, None], 0.0, NEG))

    def swap(period, rot):
        m = np.zeros((P, P))
        for d in range(P):
            r = d % period
            if r < rot // 2:
                m[d + rot // 2, d] = -1.0
            elif r < rot:
                m[d - rot // 2, d] = 1.0
        return m

    def freq(period, rot, base):
        inv = base ** (-np.arange(0, rot, 2, dtype=np.float32) / np.float32(rot))
        f = np.zeros(P, np.float32)
        for d in range(P):
            r = d % period
            if r < rot:
                f[d] = inv.astype(np.float32)[r % (rot // 2)]
        return f

    put("swap_ret", swap(128, 128))
    put("swap_a", swap(64, 16))
    put("swap_i", swap(32, 8))
    put("freq", np.stack([freq(128, 128, np.float32(10000.0)), freq(64, 16, np.float32(500000.0)),
                          freq(32, 8, np.float32(500000.0)), np.full(P, np.pi / 2)], 1))
    lev = np.zeros((P, LEVELS + 1, P))
    for l in range(LEVELS):
        b = 64 >> l
        lev[:, l] = ((i[:, None] // (2 * b) == i[None, :] // (2 * b))
                     & (i[:, None] % (2 * b) < b) & (i[None, :] % (2 * b) >= b))
    lev[:, LEVELS] = np.eye(P)
    put("levels", lev.reshape(P, -1))
    gam = np.log1p(-np.exp2(-5.0 - np.arange(4)))
    rel = np.arange(T)[None, :] - i[:, None]
    dec = np.stack([np.where(rel >= 0, np.exp(np.maximum(rel, 0) * g), 0.0) for g in gam], 1)
    put("decay", dec.reshape(P, -1))
    put("restart", np.broadcast_to((np.arange(T) % P != 0), (P, T)))
    put("iota16", np.broadcast_to(np.arange(16), (P, 16)))
    put("token", i[:, None] + P * np.arange(TT)[None, :])
    return c


class Signal:

    def __init__(self, nc, stack, name, pool_dma):
        self.sem = stack.enter_context(nc.semaphore(name))
        self.base = 0
        if not pool_dma:
            nc.sync.sem_inc(self.sem, 1)
            self.base = 1

    def at(self, n):
        return n + self.base


SIGNALS = """
    start n_squares n_inverse n_roots n_normed n_normed_a n_turned n_own n_stored p_loaded0 p_loaded1
    p_loaded2 p_scaled p_summed p_taken_act p_taken_dve a_got a_own a_ready a_sines r_swapped r_own t_scored
    t_decayed t_summed t_taken loads g_made g_own g_logs g_low g_out q_own q_diffs q_decays q_queries q_keys
    q_keys_k q_scored0 q_scored1 q_picked0 q_picked1 q_turned q_turned_sb q_updates q_states q_outs q_taken
    q_absed passed_dve passed_pool m_squares m_own m_inverse m_roots m_ready m_gained m_turned m_taken m_got
    s_loaded0 s_loaded1 s_hidden0 s_hidden1 s_gate_up0 s_gate_up1 s_gated0 s_gated1 s_freed0 s_freed1
    s_y_ready s_y_taken s_y_turned s_emitted s_zeros passed_pe h_got h_own h_exp h_sig_f h_sig_k h_made h_logs
    h_kept scaled s1_y_turned s1_zeros c_own w_got w_squares w_own w_inverse w_roots w_ready d_got d_c
    d_summed d_turned d_own d_rows d_biased d_row_summed d_row_out d_loaded0 d_loaded1 d_loaded2 l_got
    l_squares l_inverse l_roots l_own l_normed l_turned l_copied l_made l_cleared i_dots i_relus i_own
    i_weighed x_ready x_logits x_masked x_scaled x_exps x_turned x_copied x_lat_made x_lat_copied x_made
    x_inverse x_taken x_zeroed x_cum x_got y_dotted3 y_added0 y_added1 y_added2 y_added3 y_weighed0 y_weighed1
    y_weighed2 y_weighed3 stored
""".split()


class Stages:

    def __init__(self, nc, stack):
        self.nc, self.stack = nc, stack
        self.signals = {}
        self.spare = []

    def sb(self, name, shape, dt=F32, stack=None):
        return (stack or self.stack).enter_context(self.nc.sbuf_tensor(name, shape, dt))

    def sig(self, name, pool_dma=False):
        if name not in self.signals:
            self.signals[name] = Signal(self.nc, self.stack, name, True) if pool_dma else self.spare.pop()
        return self.signals[name]

    def retire(self, prefix):
        for name in sorted(x for x in self.signals if x.startswith(prefix)):
            self.spare.append(self.signals.pop(name))

    def const(self, name):
        at, w = self.where[name]
        return self.consts[:, at:at + w]


def settle(eng, passed):
    eng.sem_inc(passed.sem, 1)


class Count:

    def __init__(self, signal):
        self.base, self.n = signal.base, 0

    def up(self):
        self.n += 1
        return 1

    def value(self):
        return self.base + self.n


def norm_stage(S, name, gain, shift=None, xn_dram=None):
    nc, h, xT, ps = S.nc, S.h, S.xT, S.ps
    with ExitStack() as st:
        xn = S.sb(name + "_xn", [P, TT, D], F32, st)
        ss = S.sb(name + "_ss", [P, TT], F32, st)
        rstd = S.sb(name + "_rstd", [P, TT], F32, st)
        squares, inverse, roots, normed, normed_a, turned, own, stored = (
            S.sig(x) for x in ("n_squares", "n_inverse", "n_roots", "n_normed", "n_normed_a", "n_turned", "n_own", "n_stored"))
        ident = S.const("ident")
        with nc.Block(name) as block:
            @block.scalar
            def _(act):
                for t in range(TT):
                    nc.scalar.activation(xn[:, t, :], h[:, t, :], ACT.Square,
                                         accum_out=ss[:, t:t + 1]).then_inc(squares.sem, 1)
                act.wait_ge(inverse.sem, inverse.at(1))
                nc.scalar.activation(rstd[:, :], ss[:, :], ACT.Sqrt).then_inc(roots.sem, 1)
                act.wait_ge(roots.sem, roots.at(1))
                for t in (1, 3):
                    nc.scalar.activation(xn[:, t, :], h[:, t, :], ACT.Copy,
                                         scale=rstd[:, t:t + 1]).then_inc(normed_a.sem, 1)

            @block.vector
            def _(dve):
                o = Count(own)
                dve.wait_ge(squares.sem, squares.at(TT))
                nc.vector.tensor_scalar(ss[:, :], ss[:, :], 1.0 / D, EPS, ALU.mult, ALU.add).then_inc(own.sem, o.up())
                dve.wait_ge(own.sem, o.value())
                nc.vector.reciprocal(ss[:, :], ss[:, :]).then_inc(inverse.sem, 1)
                dve.wait_ge(roots.sem, roots.at(1))
                for t in (0, 2):
                    nc.vector.tensor_scalar(xn[:, t, :], h[:, t, :], rstd[:, t:t + 1], None,
                                            ALU.mult).then_inc(normed.sem, 1)
                for t in range(TT):
                    for half in range(2):
                        dve.wait_ge(turned.sem, turned.at(2 * t + half + 1))
                        dst = xT[:, 4 * half:4 * half + 4, t * P:(t + 1) * P]
                        src = ps[2 * t + half][:, :].rearrange("p (k c) -> p k c", k=4)
                        g = gain[:, 4 * half:4 * half + 4].unsqueeze(2).broadcast_to([P, 4, P])
                        nc.vector.tensor_tensor(dst, src, g, ALU.mult).then_inc(own.sem, o.up())
                if shift is not None:
                    dve.wait_ge(own.sem, o.value())
                    s = shift.unsqueeze(2).broadcast_to([P, KD, T])
                    nc.vector.tensor_tensor(xT[:, :, :], xT[:, :, :], s, ALU.add).then_inc(own.sem, o.up())

            @block.tensor
            def _(pe):
                for t in range(TT):
                    pe.wait_ge((normed_a if t % 2 else normed).sem, (normed_a if t % 2 else normed).at(t // 2 + 1))
                    for half in range(2):
                        for k in range(4):
                            last = nc.tensor.transpose(ps[2 * t + half][:, k * P:(k + 1) * P],
                                                       xn[:, t, (4 * half + k) * P:(4 * half + k + 1) * P], ident)
                        last.then_inc(turned.sem, 1)

            if xn_dram is not None:
                @block.sync
                def _(sp):
                    sp.wait_ge(normed.sem, normed.at(2))
                    sp.wait_ge(normed_a.sem, normed_a.at(2))
                    sp.dma_start(xn_dram.rearrange("(t p) d -> p t d", p=P), xn[:, :, :]).then_inc(stored.sem, 16)
                    sp.wait_ge(stored.sem, stored.at(16))
        for s, n in ((squares, TT), (inverse, 1), (roots, 1), (normed, 2), (normed_a, 2), (turned, 8),
                     (own, 1 + 8 + (shift is not None)), (stored, 16 * (xn_dram is not None))):
            s.base += n


def project_stage(S, name, chunks):
    nc, xT, ps = S.nc, S.xT, S.ps
    NW = 3

    def pieces(w):
        return w if isinstance(w, list) else [w]

    def width_of(w):
        return sum(x.shape[1] for x in pieces(w))

    def loads_to(c):
        return 16 * sum(len(pieces(chunks[x][0])) for x in range(c % NW, c + 1, NW)) if c >= 0 else 0

    groups, ends = [], []
    count = {"act": 0, "dve": 0}
    for c, (w, kind, how, dst) in enumerate(chunks):
        n = width_of(w)
        parts = [(m, min(P, n - m * P)) for m in range((n + P - 1) // P)] if kind == "T" else [(t, P) for t in range(TT)]
        for i, (m, width) in enumerate(parts):
            who = "act" if len(groups) % 2 else "dve"
            if isinstance(how, str):
                who = {"silu": "act", "add": "dve"}.get(how, who)
            if isinstance(how, float):
                who = "act"
            elif not isinstance(how, str):
                who = "dve"
            groups.append((c, m, width, who, count[who], i == len(parts) - 1))
            count[who] += 1
        ends.append(len(groups))
    with ExitStack() as st:
        wring = S.sb(name + "_w", [P, NW, KD, BANK], F32, st)
        loaded = [S.sig(f"p_loaded{b}") for b in range(NW)]
        tmp = S.sb(name + "_tmp", [P, BANK], F32, st)
        scaled, n_scaled = S.sig("p_scaled"), 0
        summed = S.sig("p_summed")
        taken = {"act": S.sig("p_taken_act"), "dve": S.sig("p_taken_dve")}

        def out_of(g):
            c, m, width, who, _, _ = g
            n = width_of(chunks[c][0])
            b = ps[groups.index(g) % 8]
            return b[0:width, :] if chunks[c][1] == "T" else b[:, 0:n]

        with nc.Block(name) as block:
            @block.sync
            def _(sp):
                for c, (w, kind, how, dst) in enumerate(chunks):
                    if c >= NW:
                        sp.wait_ge(summed.sem, summed.at(ends[c - NW]))
                    at = 0
                    for part in pieces(w):
                        n = part.shape[1]
                        sp.dma_start(wring[:, c % NW, :, at:at + n],
                                     part.rearrange("(k p) n -> p k n", p=P)).then_inc(loaded[c % NW].sem, 16)
                        at += n

            @block.tensor
            def _(pe):
                for i, g in enumerate(groups):
                    c, m, width, who, _, final = g
                    w, kind, how, dst = chunks[c]
                    n = width_of(w)
                    if i == 0 or groups[i - 1][0] != c:
                        pe.wait_ge(loaded[c % NW].sem, loaded[c % NW].at(loads_to(c)))
                    if i >= 8:
                        pe.wait_ge(taken[groups[i - 8][3]].sem, taken[groups[i - 8][3]].at(groups[i - 8][4] + 1))
                    for k in range(KD):
                        wk = wring[:, c % NW, k, :]
                        if kind == "T":
                            last = nc.tensor.matmul(out_of(g), wk[:, m * P:m * P + width], xT[:, k, :],
                                                    start=(k == 0), stop=(k == KD - 1))
                        else:
                            last = nc.tensor.matmul(out_of(g), xT[:, k, m * P:(m + 1) * P], wk[:, 0:n],
                                                    start=(k == 0), stop=(k == KD - 1))
                    last.then_inc(summed.sem, 1)

            def evacuate(eng, me):
                for i, g in enumerate(groups):
                    c, m, width, who, _, _ = g
                    if who != me:
                        continue
                    how, dst = chunks[c][2], chunks[c][3]
                    eng.wait_ge(summed.sem, summed.at(i + 1))
                    if not isinstance(how, (str, float)):
                        nonlocal n_scaled
                        if me == "dve" and n_scaled >= 1:
                            eng.wait_ge(taken[me].sem, taken[me].at(g[4]))
                        nc.vector.tensor_tensor(tmp[:, 0:how.shape[1]], out_of(g), how, ALU.mult).then_inc(scaled.sem, 1)
                        n_scaled += 1
                        eng.wait_ge(scaled.sem, scaled.at(n_scaled))
                        ins = nc.vector.tensor_tensor(dst(m), dst(m), tmp[:, 0:how.shape[1]], ALU.add)
                    elif isinstance(how, str) and how == "add":
                        ins = nc.vector.tensor_tensor(dst(m), dst(m), out_of(g), ALU.add)
                    elif isinstance(how, str) and how == "silu":
                        ins = nc.scalar.activation(dst(m), out_of(g), ACT.Silu)
                    elif isinstance(how, float):
                        ins = nc.scalar.activation(dst(m), out_of(g), ACT.Copy, scale=how)
                    elif me == "act":
                        ins = nc.scalar.activation(dst(m), out_of(g), ACT.Copy)
                    else:
                        ins = nc.vector.tensor_copy(dst(m), out_of(g))
                    ins.then_inc(taken[me].sem, 1)

            @block.scalar
            def _(act):
                evacuate(act, "act")

            @block.vector
            def _(dve):
                evacuate(dve, "dve")
        for b in range(NW):
            loaded[b].base += loads_to(max([c for c in range(len(chunks)) if c % NW == b], default=-1))
        scaled.base += n_scaled
        summed.base += len(groups)
        for who in count:
            taken[who].base += count[who]


def angle_stage(S, name, positions, freqs, tables):
    nc = S.nc
    got, own, ready, sines = S.sig("a_got"), S.sig("a_own"), S.sig("a_ready"), S.sig("a_sines")
    with ExitStack() as st:
        pos_i = S.sb(name + "_pi", [P, T], I32, st)
        pos = S.sb(name + "_pf", [P, T], F32, st)
        turns = S.sb(name + "_turns", [P, T], F32, st)
        steps = 0
        with nc.Block(name) as block:
            @block.sync
            def _(sp):
                sp.dma_start(pos_i[:, :], positions.partition_broadcast(P)).then_inc(got.sem, 16)

            @block.vector
            def _(dve):
                nonlocal steps
                o = Count(own)
                dve.wait_ge(got.sem, got.at(16))
                nc.vector.tensor_copy(pos[:, :], pos_i[:, :]).then_inc(own.sem, o.up())
                dve.wait_ge(own.sem, o.value())
                for f, (cos, sin) in zip(freqs, tables):
                    nc.vector.tensor_scalar(sin, pos[:, :], f, None, ALU.mult).then_inc(own.sem, o.up())
                    dve.wait_ge(own.sem, o.value())
                    nc.vector.tensor_scalar(turns[:, :], sin, 0.15915494309189535, MAGIC, ALU.mult, ALU.add).then_inc(own.sem, o.up())
                    dve.wait_ge(own.sem, o.value())
                    nc.vector.tensor_scalar(turns[:, :], turns[:, :], MAGIC, None, ALU.subtract).then_inc(own.sem, o.up())
                    dve.wait_ge(own.sem, o.value())
                    for part in (TWO_PI_HI, TWO_PI_MID, TWO_PI_LO):
                        nc.vector.scalar_tensor_tensor(sin, turns[:, :], -part, sin, ALU.mult, ALU.add).then_inc(own.sem, o.up())
                        dve.wait_ge(own.sem, o.value())
                    nc.vector.tensor_scalar(sin, sin, 3.1415925, -3.1415925, ALU.min, ALU.max).then_inc(own.sem, o.up())
                    dve.wait_ge(own.sem, o.value())
                    nc.vector.scalar_tensor_tensor(cos, sin, -1.0, sin, ALU.mult, ALU.max).then_inc(ready.sem, 1)
                steps = o.n

            @block.scalar
            def _(act):
                for n, (cos, sin) in enumerate(tables):
                    act.wait_ge(ready.sem, ready.at(n + 1))
                    half_pi = S.const("freq")[:, 3:4]
                    nc.scalar.activation(cos, cos, ACT.Sin, bias=half_pi, scale=-1.0).then_inc(sines.sem, 1)
                    nc.scalar.activation(sin, sin, ACT.Sin).then_inc(sines.sem, 1)
        got.base += 16
        own.base += steps
        ready.base += len(tables)
        sines.base += 2 * len(tables)


def rotate_stage(S, name, tiles):
    nc, ps = S.nc, S.ps
    swapped, own = S.sig("r_swapped"), S.sig("r_own")
    with ExitStack() as st:
        scaled = S.sb(name + "_c", [P, 2, T], F32, st)
        with nc.Block(name) as block:
            @block.tensor
            def _(pe):
                for n, (x, swap, cos, sin) in enumerate(tiles):
                    if n >= 8:
                        pe.wait_ge(own.sem, own.at(3 * (n - 8) + 2))
                    rows = x.shape[0]
                    nc.tensor.matmul(ps[n % 8][0:rows, :], swap[0:rows, 0:rows], x, start=True,
                                     stop=True).then_inc(swapped.sem, 1)

            @block.vector
            def _(dve):
                o = Count(own)
                for n, (x, swap, cos, sin) in enumerate(tiles):
                    rows = x.shape[0]
                    dve.wait_ge(swapped.sem, swapped.at(n + 1))
                    nc.vector.tensor_tensor(x, x, cos[0:rows, :], ALU.mult).then_inc(own.sem, o.up())
                    nc.vector.tensor_tensor(scaled[0:rows, n % 2, :], ps[n % 8][0:rows, :], sin[0:rows, :], ALU.mult).then_inc(own.sem, o.up())
                    dve.wait_ge(own.sem, o.value())
                    nc.vector.tensor_tensor(x, x, scaled[0:rows, n % 2, :], ALU.add).then_inc(own.sem, o.up())
        swapped.base += len(tiles)
        own.base += 3 * len(tiles)


def retention_stage(S, q, k, v, mix):
    nc, ps = S.nc, S.ps
    NH = 4
    scored, decayed, summed, taken = S.sig("t_scored"), S.sig("t_decayed"), S.sig("t_summed"), S.sig("t_taken")
    decay = S.const("decay").rearrange("p (h t) -> p h t", h=NH)
    with ExitStack() as st:
        probs = S.sb("ret_probs", [P, 2, TT, T], F32, st)
        with nc.Block("retention") as block:
            @block.tensor
            def _(pe):
                def scores(h):
                    for j in range(TT):
                        if h:
                            pe.wait_ge(decayed.sem, decayed.at(TT * (h - 1) + j + 1))
                        nc.tensor.matmul(ps[j][:, 0:T - j * P], k[:, h, j * P:(j + 1) * P], q[:, h, j * P:T],
                                         start=True, stop=True).then_inc(scored.sem, 1)

                def outputs(h):
                    pe.wait_ge(decayed.sem, decayed.at(TT * (h + 1)))
                    if h >= 2:
                        pe.wait_ge(taken.sem, taken.at(h - 1))
                    for i in range(TT):
                        for j in range(i + 1):
                            last = nc.tensor.matmul(ps[4 + h % 2][:, i * P:(i + 1) * P],
                                                    probs[:, h % 2, j, (i - j) * P:(i - j + 1) * P],
                                                    v[:, j, h * P:(h + 1) * P], start=(j == 0), stop=(j == i))
                    last.then_inc(summed.sem, 1)

                scores(0)
                for h in range(1, NH):
                    scores(h)
                    outputs(h - 1)
                outputs(NH - 1)

            @block.vector
            def _(dve):
                for h in range(NH):
                    if h >= 2:
                        dve.wait_ge(summed.sem, summed.at(h - 1))
                    for j in range(TT):
                        n = T - j * P
                        dve.wait_ge(scored.sem, scored.at(TT * h + j + 1))
                        nc.vector.tensor_tensor(probs[:, h % 2, j, 0:n], ps[j][:, 0:n], decay[:, h, 0:n],
                                                ALU.mult).then_inc(decayed.sem, 1)

            @block.scalar
            def _(act):
                for h in range(NH):
                    act.wait_ge(summed.sem, summed.at(h + 1))
                    nc.scalar.activation(mix[:, :, h, :], ps[4 + h % 2][:, :].rearrange("p (t d) -> p t d", t=TT),
                                         ACT.Copy).then_inc(taken.sem, 1)
        scored.base += 16
        decayed.base += 16
        summed.base += NH
        taken.base += NH


def log_gate_stage(S, name, tiles, factor):
    nc, ps = S.nc, S.ps
    made, own, logs, low, out = (S.sig("g_" + x) for x in ("made", "own", "logs", "low", "out"))
    n_act = 0
    with ExitStack() as st:
        y = S.sb(name + "_y", [P, len(tiles), T], F32, st)
        e = S.sb(name + "_e", [P, len(tiles), T], F32, st)
        with nc.Block(name) as block:
            @block.tensor
            def _(pe):
                for n, (lhsT, rhs, bias, dst) in enumerate(tiles):
                    rows = dst.shape[0]
                    nc.tensor.matmul(ps[n][0:rows, :], lhsT, rhs, start=True, stop=True).then_inc(made.sem, 1)

            @block.scalar
            def _(act):
                nonlocal n_act
                o = Count(own)
                for n, (lhsT, rhs, bias, dst) in enumerate(tiles):
                    r = dst.shape[0]
                    act.wait_ge(made.sem, made.at(n + 1))
                    nc.scalar.activation(y[0:r, n, :], ps[n][0:r, :], ACT.Identity, bias=bias).then_inc(low.sem, 1)
                    act.wait_ge(low.sem, low.at(n + 1))
                    nc.scalar.activation(e[0:r, n, :], y[0:r, n, :], ACT.Abs).then_inc(own.sem, o.up())
                    act.wait_ge(own.sem, o.value())
                    nc.scalar.activation(e[0:r, n, :], e[0:r, n, :], ACT.Exp, scale=-1.0).then_inc(own.sem, o.up())
                    act.wait_ge(own.sem, o.value())
                    nc.scalar.activation(e[0:r, n, :], e[0:r, n, :], ACT.Ln, bias=1.0).then_inc(logs.sem, 1)
                n_act = o.n

            @block.vector
            def _(dve):
                for n, (lhsT, rhs, bias, dst) in enumerate(tiles):
                    r = dst.shape[0]
                    dve.wait_ge(logs.sem, logs.at(n + 1))
                    nc.vector.scalar_tensor_tensor(dst, y[0:r, n, :], 0.0, e[0:r, n, :], ALU.min,
                                                   ALU.subtract).then_inc(out.sem, 1)
                    dve.wait_ge(out.sem, out.at(2 * n + 1))
                    nc.vector.tensor_scalar(dst, dst, factor, None, ALU.mult).then_inc(out.sem, 1)
        made.base += len(tiles)
        own.base += n_act
        low.base += len(tiles)
        logs.base += len(tiles)
        out.base += 2 * len(tiles)


def gated_stage(S, name, n_packs, heads, q, k, logf, v, mix, head0):
    nc, ps = S.nc, S.ps
    W = P // heads
    L = LEVELS
    sig = S.sig
    g_own, diffs, decays, queries = sig("q_own"), sig("q_diffs"), sig("q_decays"), sig("q_queries")
    keys, keys_k = sig("q_keys"), sig("q_keys_k")
    scored = [sig("q_scored0"), sig("q_scored1")]
    picked = [sig("q_picked0"), sig("q_picked1")]
    turned, turned_sb, updates, states, outs, taken, absed = (
        sig(x) for x in ("q_turned", "q_turned_sb", "q_updates", "q_states", "q_outs", "q_taken", "q_absed"))
    restart = S.const("restart")
    masks = S.const("levels").bitcast(U32).rearrange("p (l i) -> p l i", l=L + 1)
    ident = S.const("ident")
    with ExitStack() as st:
        g = S.sb(name + "_g", [P, T], F32, st)
        diff = S.sb(name + "_diff", [P, L + 2, T], F32, st)
        qE = S.sb(name + "_qe", [P, 2, T], F32, st)
        kE = S.sb(name + "_ke", [P, 2, T], F32, st)
        qd = S.sb(name + "_qd", [P, T], F32, st)
        kd = S.sb(name + "_kd", [P, T], F32, st)
        kdt = S.sb(name + "_kdt", [P, TT, P], F32, st)
        sT = S.sb(name + "_st", [P, heads, TT, P], F32, st)
        state = S.sb(name + "_state", [P, 3, P], F32, st)

        def loop(eng, body):
            if n_packs <= 2:
                for p in range(n_packs):
                    body(p)
            else:
                with eng.Fori(0, n_packs) as p:
                    body(p)

        with nc.Block(name) as block:
            @block.vector
            def _(dve):
                nc.vector.memset(sT[:, :, :, :], 0.0).then_inc(g_own.sem, 1)

                def body(p):
                    dve.wait_ge(keys.sem, keys.at((L + 1) * p))
                    dve.wait_ge(keys_k.sem, keys_k.at(p))
                    nc.vector.tensor_tensor_scan(g[:, :], restart, logf(p), 0.0, ALU.mult, ALU.add).then_inc(g_own.sem, 1)
                    dve.wait_ge(g_own.sem, g_own.at(p + 2))
                    for l in range(L):
                        b = 64 >> l
                        gv = g[:, :].rearrange("p (n w) -> p n w", w=2 * b)
                        dv = diff[:, l, :].rearrange("p (n w) -> p n w", w=2 * b)
                        nc.vector.tensor_tensor(dv, gv, gv[:, :, b - 1:b].broadcast_to([P, T // (2 * b), 2 * b]),
                                                ALU.subtract).then_inc(diffs.sem, 1)
                    gv = g[:, :].rearrange("p (n w) -> p n w", w=P)
                    dv = diff[:, L, :].rearrange("p (n w) -> p n w", w=P)
                    nc.vector.tensor_tensor(dv, gv, gv[:, :, P - 1:P].broadcast_to([P, TT, P]),
                                            ALU.subtract).then_inc(diffs.sem, 1)
                    dve.wait_ge(outs.sem, outs.at(heads * p))

                    def query(l):
                        dve.wait_ge(scored[l % 2].sem, scored[l % 2].at(_half(p, L + 1, l)))
                        if l < L:
                            dve.wait_ge(decays.sem, decays.at(p * (L + 2) + l + 1))
                            nc.vector.tensor_tensor(qE[:, l % 2, :], q(p), diff[:, l, :], ALU.mult).then_inc(queries.sem, 1)
                        else:
                            settle(dve, S.sig("passed_dve"))
                            nc.vector.tensor_copy(qE[:, l % 2, :], q(p)).then_inc(queries.sem, 1)

                    def pick(l):
                        dve.wait_ge(scored[l % 2].sem, scored[l % 2].at(_half(p, L + 1, l) + 1))
                        settle(dve, S.sig("passed_dve"))
                        for hd in range(heads):
                            ins = nc.vector.copy_predicated(
                                sT[:, hd, :, :], masks[:, l:l + 1, :].broadcast_to([P, TT, P]),
                                ps[2 * (l % 2) + hd][:, :].rearrange("p (c i) -> p c i", c=TT))
                            if hd == heads - 1:
                                ins.then_inc(picked[l % 2].sem, 1)

                    for l in range(L + 1):
                        query(l)
                        if l:
                            if l > 1:
                                dve.wait_ge(picked[l % 2].sem, picked[l % 2].at(_half(p, L + 1, l - 2) + 1))
                            pick(l - 1)
                    dve.wait_ge(picked[(L - 1) % 2].sem, picked[(L - 1) % 2].at(_half(p, L + 1, L - 1) + 1))
                    pick(L)
                    dve.wait_ge(decays.sem, decays.at(p * (L + 2) + L + 1))
                    nc.vector.tensor_tensor(qd[:, :], q(p), diff[:, L + 1, :], ALU.mult).then_inc(queries.sem, 1)
                    dve.wait_ge(updates.sem, updates.at(p + 1))
                    nc.vector.tensor_copy(state[:, 0, :], ps[5][:, 0:P]).then_inc(states.sem, 1)
                    for c in (1, 2):
                        dve.wait_ge(states.sem, states.at(3 * p + c))
                        nc.vector.scalar_tensor_tensor(state[:, c, :], state[:, c - 1, :],
                                                       diff[:, L + 1, c * P + P - 1:c * P + P],
                                                       ps[5][:, c * P:(c + 1) * P], ALU.mult,
                                                       ALU.add).then_inc(states.sem, 1)
                loop(dve, body)

            @block.scalar
            def _(act):
                def body(p):
                    for l in range(L):
                        act.wait_ge(diffs.sem, diffs.at(p * (L + 1) + l + 1))
                        nc.scalar.activation(diff[:, l, :], diff[:, l, :], ACT.Abs).then_inc(absed.sem, 1)
                        act.wait_ge(absed.sem, absed.at(p * L + l + 1))
                        nc.scalar.activation(diff[:, l, :], diff[:, l, :], ACT.Exp, scale=-1.0).then_inc(decays.sem, 1)
                    nc.scalar.activation(diff[:, L + 1, :], g[:, :], ACT.Exp).then_inc(decays.sem, 1)
                    act.wait_ge(diffs.sem, diffs.at((p + 1) * (L + 1)))
                    nc.scalar.activation(diff[:, L, :], diff[:, L, :], ACT.Exp, scale=-1.0).then_inc(decays.sem, 1)
                    act.wait_ge(turned.sem, turned.at(p + 1))
                    nc.scalar.activation(kdt[:, :, :], ps[4][:, :].rearrange("p (c d) -> p c d", c=TT),
                                         ACT.Copy).then_inc(turned_sb.sem, 1)
                    for hd in range(heads):
                        act.wait_ge(outs.sem, outs.at(heads * p + hd + 1))
                        nc.scalar.activation(mix(p * heads + hd), ps[6 + hd][:, :].rearrange("p (c d) -> p c d", c=TT),
                                             ACT.Copy).then_inc(taken.sem, 1)
                loop(act, body)

            @block.gpsimd
            def _(pool):
                def body(p):
                    for l in range(L + 1):
                        pool.wait_ge(scored[l % 2].sem, scored[l % 2].at(_half(p, L + 1, l)))
                        if l < L:
                            pool.wait_ge(decays.sem, decays.at(p * (L + 2) + l + 1))
                            settle(pool, S.sig("passed_pool"))
                            nc.gpsimd.tensor_tensor(kE[:, l % 2, :], k(p), diff[:, l, :], ALU.mult).then_inc(keys.sem, 1)
                        else:
                            settle(pool, S.sig("passed_pool"))
                            nc.gpsimd.tensor_copy(kE[:, l % 2, :], k(p)).then_inc(keys.sem, 1)
                    pool.wait_ge(decays.sem, decays.at((p + 1) * (L + 2)))
                    pool.wait_ge(turned.sem, turned.at(p))
                    settle(pool, S.sig("passed_pool"))
                    nc.gpsimd.tensor_tensor(kd[:, :], k(p), diff[:, L, :], ALU.mult).then_inc(keys_k.sem, 1)
                loop(pool, body)

            @block.tensor
            def _(pe):
                def body(p):
                    for l in range(L + 1):
                        pe.wait_ge(queries.sem, queries.at(p * (L + 2) + l + 1))
                        pe.wait_ge(keys.sem, keys.at(p * (L + 1) + l + 1))
                        pe.wait_ge(picked[l % 2].sem, picked[l % 2].at(_half(p, L + 1, l)))
                        for hd in range(heads):
                            r = slice(hd * W, (hd + 1) * W)
                            for c in range(TT):
                                cc = slice(c * P, (c + 1) * P)
                                last = nc.tensor.matmul(ps[2 * (l % 2) + hd][:, cc], kE[r, l % 2, cc], qE[r, l % 2, cc],
                                                        start=True, stop=True)
                        last.then_inc(scored[l % 2].sem, 1)
                    pe.wait_ge(keys_k.sem, keys_k.at(p + 1))
                    pe.wait_ge(turned_sb.sem, turned_sb.at(p))
                    for c in range(TT):
                        last = nc.tensor.transpose(ps[4][:, c * P:(c + 1) * P], kd[:, c * P:(c + 1) * P], ident)
                    last.then_inc(turned.sem, 1)
                    pe.wait_ge(turned_sb.sem, turned_sb.at(p + 1))
                    pe.wait_ge(states.sem, states.at(3 * p))
                    for c in range(3):
                        for hd in range(heads):
                            last = nc.tensor.matmul(ps[5][hd * W:(hd + 1) * W, c * P:(c + 1) * P],
                                                    kdt[:, c, hd * W:(hd + 1) * W], v(p * heads + hd, c),
                                                    start=True, stop=True)
                    last.then_inc(updates.sem, 1)
                    pe.wait_ge(picked[0].sem, picked[0].at((L + 1) // 2 * (p + 1)))
                    pe.wait_ge(picked[1].sem, picked[1].at((L + 1) // 2 * (p + 1)))
                    pe.wait_ge(queries.sem, queries.at((p + 1) * (L + 2)))
                    pe.wait_ge(states.sem, states.at(3 * (p + 1)))
                    pe.wait_ge(taken.sem, taken.at(heads * p))
                    for hd in range(heads):
                        r = slice(hd * W, (hd + 1) * W)
                        for c in range(TT):
                            cc = slice(c * P, (c + 1) * P)
                            last = nc.tensor.matmul(ps[6 + hd][:, cc], sT[:, hd, c, :], v(p * heads + hd, c),
                                                    start=True, stop=(c == 0))
                            if c:
                                last = nc.tensor.matmul(ps[6 + hd][:, cc], qd[r, cc], state[r, c - 1, :],
                                                        start=False, stop=True)
                        last.then_inc(outs.sem, 1)
                loop(pe, body)
        for s, n in ((g_own, 1 + n_packs), (diffs, (L + 1) * n_packs), (decays, (L + 2) * n_packs),
                     (queries, (L + 2) * n_packs), (keys, (L + 1) * n_packs), (keys_k, n_packs),
                     (scored[0], (L + 1) // 2 * n_packs), (scored[1], (L + 1) // 2 * n_packs),
                     (picked[0], (L + 1) // 2 * n_packs), (picked[1], (L + 1) // 2 * n_packs),
                     (turned, n_packs), (turned_sb, n_packs), (updates, n_packs), (states, 3 * n_packs),
                     (outs, heads * n_packs), (taken, heads * n_packs), (absed, L * n_packs)):
            s.base += n


def _half(p, per_pack, l):
    return p * (per_pack // 2) + l // 2


def head_norm_stage(S, name, mix, width, gain_row, gate):
    nc, ps, xT = S.nc, S.ps, S.xT
    NH = D // width
    squares, own, inverse, roots, ready, gained, turned, taken, got = (
        S.sig("m_" + x) for x in ("squares", "own", "inverse", "roots", "ready", "gained", "turned", "taken", "got"))
    n_own = 0
    with ExitStack() as st:
        sq = S.sb(name + "_sq", [P, 2, D], F32, st)
        gains = S.sb(name + "_gains", [P, D], F32, st)
        ss = S.sb(name + "_ss", [P, TT, NH], F32, st)
        r = S.sb(name + "_r", [P, TT, NH], F32, st)
        with nc.Block(name) as block:
            @block.sync
            def _(sp):
                for at, src in gain_row:
                    n = src.shape[0]
                    sp.dma_start(gains[:, at:at + n], src.partition_broadcast(P)).then_inc(got.sem, 16)

            @block.gpsimd
            def _(pool):
                pool.wait_ge(got.sem, got.at(16 * len(gain_row)))
                for t in range(TT):
                    m = gate[:, t, :] if gate is not None else None
                    if m is not None:
                        nc.gpsimd.tensor_tensor(m, m, gains[:, :], ALU.mult).then_inc(gained.sem, 1)

            @block.scalar
            def _(act):
                for t in range(TT):
                    if t >= 2:
                        act.wait_ge(own.sem, own.at(t - 1))
                    nc.scalar.activation(sq[:, t % 2, :], mix[:, t, :], ACT.Square).then_inc(squares.sem, 1)
                act.wait_ge(inverse.sem, inverse.at(1))
                nc.scalar.activation(r[:, :, :], ss[:, :, :], ACT.Sqrt).then_inc(roots.sem, 1)
                for t in range(TT):
                    for half in range(2):
                        act.wait_ge(turned.sem, turned.at(2 * t + half + 1))
                        nc.scalar.activation(xT[:, 4 * half:4 * half + 4, t * P:(t + 1) * P],
                                             ps[2 * t + half][:, :].rearrange("p (k c) -> p k c", k=4),
                                             ACT.Copy).then_inc(taken.sem, 1)

            @block.vector
            def _(dve):
                nonlocal n_own
                o = Count(own)
                for t in range(TT):
                    dve.wait_ge(squares.sem, squares.at(t + 1))
                    nc.vector.tensor_reduce(ss[:, t, :], sq[:, t % 2, :].rearrange("p (h w) -> p h w", h=NH),
                                                   AX.X, ALU.add).then_inc(own.sem, o.up())
                dve.wait_ge(own.sem, o.value())
                nc.vector.tensor_scalar(ss[:, :, :], ss[:, :, :], 1.0 / width, EPS, ALU.mult, ALU.add).then_inc(own.sem, o.up())
                dve.wait_ge(own.sem, o.value())
                nc.vector.reciprocal(ss[:, :, :], ss[:, :, :]).then_inc(inverse.sem, 1)
                dve.wait_ge(roots.sem, roots.at(1))
                for t in range(TT):
                    m = mix[:, t, :].rearrange("p (h w) -> p h w", h=NH)
                    nc.vector.tensor_tensor(m, m, r[:, t, :].unsqueeze(2).broadcast_to([P, NH, width]), ALU.mult).then_inc(own.sem, o.up())
                    dve.wait_ge(own.sem, o.value())
                    if gate is not None:
                        dve.wait_ge(gained.sem, gained.at(t + 1))
                        by = gate[:, t, :]
                    else:
                        dve.wait_ge(got.sem, got.at(16 * len(gain_row)))
                        by = gains[:, :]
                    nc.vector.tensor_tensor(mix[:, t, :], mix[:, t, :], by, ALU.mult).then_inc(ready.sem, 1)
                n_own = o.n

            @block.tensor
            def _(pe):
                for t in range(TT):
                    pe.wait_ge(ready.sem, ready.at(t + 1))
                    for half in range(2):
                        for kk in range(4):
                            c = 4 * half + kk
                            last = nc.tensor.transpose(ps[2 * t + half][:, kk * P:(kk + 1) * P],
                                                       mix[:, t, c * P:(c + 1) * P], S.const("ident"))
                        last.then_inc(turned.sem, 1)
        for s, n in ((squares, TT), (own, n_own), (inverse, 1), (roots, 1), (ready, TT), (turned, 8), (taken, 8),
                     (gained, TT * (gate is not None)), (got, 16 * len(gain_row))):
            s.base += n


def row_parts(rows):
    return [(r0, min(P, rows - r0)) for r0 in range(0, rows, P)]


def swiglu_stage(S, name, letter, rows, hidden, units, weights, x_of, gather, emit):
    nc, ps = S.nc, S.ps
    n_groups = hidden // GROUP
    per = ((n_groups + 1) // 2, n_groups // 2)
    subs = row_parts(rows)
    per_unit = 2 * len(subs)
    sig = lambda x: S.sig(letter + x)
    loaded = [sig("loaded0"), sig("loaded1")]
    hidden_ready = [sig("hidden0"), sig("hidden1")]
    gate_up, gated = [sig("gate_up0"), sig("gate_up1")], [sig("gated0"), sig("gated1")]
    freed = [sig("freed0"), sig("freed1")]
    y_ready, y_taken, y_turned, emitted, zeros_ready = (
        sig(x) for x in ("y_ready", "y_taken", "y_turned", "emitted", "zeros"))
    with ExitStack() as st:
        wg = S.sb(name + "_wg", [P, 2, KD, GROUP], F32, st)
        wu = S.sb(name + "_wu", [P, 2, KD, GROUP], F32, st)
        wd = S.sb(name + "_wd", [P, 2, 2, D], F32, st)
        gated_sb = S.sb(name + "_gs", [P, 2, rows], F32, st)
        hid = S.sb(name + "_hid", [P, 2, rows], F32, st)
        yT = S.sb(name + "_yt", [P, KD, rows], F32, st)
        zero = S.sb(name + "_zero", [P, BANK], BF16, st)

        def groups(eng, u, body):
            with eng.Fori(0, n_groups // 2) as i:
                for b in range(2):
                    body(i, b)
            if n_groups % 2:
                body(n_groups // 2, 0)

        with nc.Block(name) as block:
            @block.sync
            def _(sp):
                with sp.Fori(0, units(sp)) as u:
                    g, up, dn = weights(sp, u)

                    def body(i, b):
                        sp.wait_ge(freed[b].sem, freed[b].at(u * per[b] + i))
                        f = (i * 2 + b) * GROUP
                        gv = g[:, bass.ds(f, GROUP)].rearrange("(k p) f -> p k f", p=P)
                        uv = up[:, bass.ds(f, GROUP)].rearrange("(k p) f -> p k f", p=P)
                        dv = dn[bass.ds(f, GROUP), :].rearrange("(j p) d -> p j d", p=P)
                        sp.dma_start(wg[:, b, :, :], gv).then_inc(loaded[b].sem, 16)
                        sp.dma_start(wu[:, b, :, :], uv).then_inc(loaded[b].sem, 16)
                        sp.dma_start(wd[:, b, :, :], dv).then_inc(loaded[b].sem, 16)
                    groups(sp, u, body)

            @block.tensor
            def _(pe):
                pe.wait_ge(zeros_ready.sem, zeros_ready.at(1))
                with pe.Fori(0, units(pe)) as u:
                    if gather is not None:
                        gather.turn(pe, u)
                    pe.wait_ge(y_taken.sem, y_taken.at(u))
                    for b in range(4):
                        nc.tensor.matmul(ps[b][:, :], zero[:, 0:P], zero[:, :], start=True, stop=False,
                                         skip_group_check=True)
                    if gather is None:
                        pe.wait_ge(emitted.sem, emitted.at(per_unit * u))
                    else:
                        pe.wait_ge(gather.x_ready.sem, gather.x_ready.at(per_unit * (u + 1)))

                    settle(pe, S.sig("passed_pe"))

                    def body(i, b):
                        pe.wait_ge(loaded[b].sem, loaded[b].at((u * per[b] + i + 1) * 48))
                        n = u * n_groups + i * 2 + b
                        for j in range(2):
                            pe.wait_ge(hidden_ready[j].sem, hidden_ready[j].at(n))
                            for w, bank in ((wg, 4 + j), (wu, 6 + j)):
                                for k in range(KD):
                                    last = nc.tensor.matmul(ps[bank][:, 0:rows], w[:, b, k, j * P:(j + 1) * P], x_of(k, u),
                                                            start=(k == 0), stop=(k == KD - 1))
                            last.then_inc(gate_up[j].sem, 1)
                        for j in range(2):
                            pe.wait_ge(hidden_ready[j].sem, hidden_ready[j].at(n + 1))
                            for d in range(KD):
                                at = (d % 2) * rows
                                last = nc.tensor.matmul(ps[d // 2][:, at:at + rows], wd[:, b, j, d * P:(d + 1) * P],
                                                        hid[:, j, :], start=False, stop=False, skip_group_check=True)
                        last.then_inc(freed[b].sem, 1)
                    groups(pe, u, body)
                    nc.tensor.matmul(ps[3][0:32, 0:2], zero[:, 0:32], zero[:, 0:2], start=False, stop=True,
                                     skip_group_check=True).then_inc(y_ready.sem, 1)
                    pe.wait_ge(y_taken.sem, y_taken.at(u + 1))
                    pe.wait_ge(hidden_ready[0].sem, hidden_ready[0].at((u + 1) * n_groups))
                    pe.wait_ge(hidden_ready[1].sem, hidden_ready[1].at((u + 1) * n_groups))
                    for s, (r0, n) in enumerate(subs):
                        for half in range(2):
                            for kk in range(4):
                                last = nc.tensor.transpose(ps[4 + 2 * s + half][0:n, kk * P:(kk + 1) * P],
                                                           yT[:, 4 * half + kk, r0:r0 + n], S.const("ident"))
                            last.then_inc(y_turned.sem, 1)

            @block.scalar
            def _(act):
                with act.Fori(0, units(act)) as u:
                    def body(i, b):
                        n = u * n_groups + i * 2 + b
                        for j in range(2):
                            act.wait_ge(gate_up[j].sem, gate_up[j].at(n + 1))
                            act.wait_ge(hidden_ready[j].sem, hidden_ready[j].at(n))
                            nc.scalar.activation(gated_sb[:, j, :], ps[4 + j][:, 0:rows], ACT.Silu).then_inc(gated[j].sem, 1)
                    groups(act, u, body)
                    if gather is not None:
                        gather.store(act, u)

            @block.vector
            def _(dve):
                nc.vector.memset(zero[:, :], 0.0).then_inc(zeros_ready.sem, 1)
                with dve.Fori(0, units(dve)) as u:
                    if gather is not None:
                        gather.place(dve, u)

                    def body(i, b):
                        n = u * n_groups + i * 2 + b
                        for j in range(2):
                            dve.wait_ge(gated[j].sem, gated[j].at(n + 1))
                            nc.vector.tensor_tensor(hid[:, j, :], gated_sb[:, j, :], ps[6 + j][:, 0:rows],
                                                    ALU.mult).then_inc(hidden_ready[j].sem, 1)
                    groups(dve, u, body)
                    dve.wait_ge(y_ready.sem, y_ready.at(u + 1))
                    dve.wait_ge(y_turned.sem, y_turned.at(per_unit * u))
                    for b in range(4):
                        ins = nc.vector.tensor_copy(yT[:, 2 * b:2 * b + 2, :],
                                                    ps[b][:, 0:2 * rows].rearrange("p (d r) -> p d r", d=2))
                    ins.then_inc(y_taken.sem, 1)
                    if gather is not None:
                        gather.before_emit(dve, u)
                    for s, (r0, n) in enumerate(subs):
                        for half in range(2):
                            dve.wait_ge(y_turned.sem, y_turned.at(per_unit * u + 2 * s + half + 1))
                            emit(u, s, half, ps[4 + 2 * s + half][0:n, :]).then_inc(emitted.sem, 1)

            if gather is not None:
                @block.gpsimd
                def _(pool):
                    with pool.Fori(0, units(pool)) as u:
                        gather.fetch(pool, u)


def ffn_swiglu(S):
    a, rows = S.a, T // 2

    def emit(u, s, half, src):
        dst = S.h[:, bass.ds(u * 2 + s, 1), half * 512:(half + 1) * 512].rearrange("p o c -> p (o c)")
        return S.nc.vector.tensor_tensor(dst, dst, src, ALU.add)

    swiglu_stage(S, "ffn", "s_", rows, D_FF, lambda eng: 2,
                 lambda eng, u: (a["ffn_w_gate"][0], a["ffn_w_up"][0], a["ffn_w_down"][0]),
                 lambda k, u: S.xT[:, k, bass.ds(u * rows, rows)], None, emit)
    n = D_FF // GROUP
    for b, per in ((0, (n + 1) // 2), (1, n // 2)):
        S.sig(f"s_loaded{b}").base += 48 * 2 * per
        S.sig(f"s_freed{b}").base += 2 * per
    for j in range(2):
        for x in ("s_hidden", "s_gate_up", "s_gated"):
            S.sig(f"{x}{j}").base += 2 * n
    for x, c in (("y_ready", 2), ("y_taken", 2), ("y_turned", 8), ("emitted", 8), ("zeros", 1)):
        S.sig("s_" + x).base += c


def hgrn_gate_stage(S, z, logf, keys):
    nc, a = S.nc, S.a
    got, own, lb_exp, sig_f, sig_k, made, logs, kept = (
        S.sig("h_" + x) for x in ("got", "own", "exp", "sig_f", "sig_k", "made", "logs", "kept"))
    n_own = 0
    with ExitStack() as st:
        lg = S.sb("lb_logits", [P, 2, KD], F32, st)
        e = S.sb("lb_e", [P, 2, KD], F32, st)
        m = S.sb("lb_m", [P, KD], F32, st)
        lb = S.sb("lb_v", [P, KD], F32, st)
        rest = S.sb("lb_rest", [P, KD], F32, st)
        with nc.Block("hgrn_gates") as block:
            @block.sync
            def _(sp):
                with nc.allow_non_contiguous_dma(reason="8 KB of logits"):
                    for l in range(2):
                        sp.dma_start(lg[:, l, :], a["hgrn_lb_logits"][l].rearrange("(k p) -> p k", p=P)).then_inc(got.sem, 16)

            @block.vector
            def _(dve):
                nonlocal n_own
                o = Count(own)
                dve.wait_ge(got.sem, got.at(32))
                nc.vector.tensor_tensor(m[:, :], lg[:, 0, :], lg[:, 1, :], ALU.max).then_inc(own.sem, o.up())
                dve.wait_ge(own.sem, o.value())
                nc.vector.tensor_tensor(e[:, :, :], lg[:, :, :], m[:, :].unsqueeze(1).broadcast_to([P, 2, KD]),
                                               ALU.subtract).then_inc(own.sem, o.up())
                dve.wait_ge(own.sem, o.value())
                dve.wait_ge(lb_exp.sem, lb_exp.at(1))
                nc.vector.tensor_tensor(m[:, :], e[:, 0, :], e[:, 1, :], ALU.add).then_inc(own.sem, o.up())
                dve.wait_ge(own.sem, o.value())
                nc.vector.reciprocal(m[:, :], m[:, :]).then_inc(own.sem, o.up())
                dve.wait_ge(own.sem, o.value())
                nc.vector.tensor_tensor(lb[:, :], e[:, 1, :], m[:, :], ALU.mult).then_inc(own.sem, o.up())
                dve.wait_ge(own.sem, o.value())
                nc.vector.tensor_scalar(rest[:, :], lb[:, :], -1.0, 1.0, ALU.mult, ALU.add).then_inc(own.sem, o.up())
                dve.wait_ge(own.sem, o.value())
                for k in range(KD):
                    dve.wait_ge(sig_f.sem, sig_f.at(k + 1))
                    nc.vector.tensor_scalar(logf[:, k, :], logf[:, k, :], rest[:, k:k + 1], lb[:, k:k + 1],
                                                   ALU.mult, ALU.add).then_inc(own.sem, o.up())
                    dve.wait_ge(own.sem, o.value())
                    nc.vector.tensor_scalar(logf[:, k, :], logf[:, k, :], 2.0e-38, None, ALU.max).then_inc(made.sem, 1)
                    dve.wait_ge(sig_k.sem, sig_k.at(k + 1))
                    nc.vector.tensor_scalar(keys[:, k, :], keys[:, k, :], rest[:, k:k + 1], None, ALU.mult).then_inc(kept.sem, 1)
                n_own = o.n

            @block.scalar
            def _(act):
                act.wait_ge(own.sem, own.at(2))
                nc.scalar.activation(e[:, :, :], e[:, :, :], ACT.Exp).then_inc(lb_exp.sem, 1)
                for k in range(KD):
                    nc.scalar.activation(keys[:, k, :], z[:, k, :], ACT.Sigmoid, scale=-1.0).then_inc(sig_k.sem, 1)
                    if z is logf:
                        act.wait_ge(sig_k.sem, sig_k.at(k + 1))
                    nc.scalar.activation(logf[:, k, :], z[:, k, :], ACT.Sigmoid).then_inc(sig_f.sem, 1)
                for k in range(KD):
                    act.wait_ge(made.sem, made.at(k + 1))
                    nc.scalar.activation(logf[:, k, :], logf[:, k, :], ACT.Ln).then_inc(logs.sem, 1)
        for s, n in ((got, 32), (own, n_own), (lb_exp, 1), (sig_f, KD), (sig_k, KD), (made, KD), (logs, KD), (kept, KD)):
            s.base += n


def mixer1(S):
    a = S.a
    norm_stage(S, "norm2", S.gains[:, 2, :])
    w = a["c_w_in"][0]
    with ExitStack() as st:
        mix = S.sb("mix1", [P, TT, D], F32, st)
        gate = S.sb("gate1", [P, TT, D], F32, st)
        heads = mix[:, :, :].rearrange("p t (h d) -> p t h d", h=8)
        with ExitStack() as st2:
            v = S.sb("v1", [P, TT, D], F32, st2)
            q = S.sb("q1", [P, KD, T], F32, st2)
            z = S.sb("z1", [P, KD, T], F32, st2)
            keys = S.sb("k1", [P, KD, T], F32, st2)
            project_stage(S, "proj1", [
                (w[:, c * 512:(c + 1) * 512], "T", "silu", lambda m, c=c: q[:, 4 * c + m, :]) for c in range(2)] + [
                (w[:, (2 + c) * 512:(3 + c) * 512], "T", "copy", lambda m, c=c: z[:, 4 * c + m, :]) for c in range(2)] + [
                (w[:, (4 + c) * 512:(5 + c) * 512], "tok", "copy", lambda t, c=c: v[:, t, c * 512:(c + 1) * 512]) for c in range(2)] + [
                (w[:, (6 + c) * 512:(7 + c) * 512], "tok", "silu", lambda t, c=c: gate[:, t, c * 512:(c + 1) * 512]) for c in range(2)])
            hgrn_gate_stage(S, z, z, keys)
            scale_stage(S, q[:, :, :], P ** -0.5)
            row = lambda x, p: x[:, bass.ds(p, 1), :].rearrange("p o t -> p (o t)")
            gated_stage(S, "hgrn", 8, 1, lambda p: row(q, p), lambda p: row(keys, p), lambda p: row(z, p),
                        lambda hd, c: v[:, c, bass.ds(hd * P, P)],
                        lambda hd: mix[:, :, bass.ds(hd * P, P)], 0)
        head_norm_stage(S, "headnorm1", mix, 128, [(i * P, a["hgrn_norm_g"][0]) for i in range(8)], gate)
        add_projection(S, "out1", a["c_w_out"][0])


def scale_stage(S, x, by):
    nc = S.nc
    done = S.sig("scaled")
    with nc.Block(f"scale{done.base}") as block:
        @block.vector
        def _(dve):
            nc.vector.tensor_scalar(x, x, by, None, ALU.mult).then_inc(done.sem, 1)
    done.base += 1


def route_stage(S, R):
    nc, a, ps, xT = S.nc, S.a, S.ps, S.xT
    S_ = S.sig
    got, logits, own, gates_in, gates_e, chosen, placed, zeroed, ids, blanked = (
        S_("o_" + x) for x in ("got", "logits", "own", "gates_in", "gates_e", "chosen", "placed", "zeroed", "ids", "blanked"))
    cleared, scattered = S_("o_cleared", pool_dma=True), S_("o_scattered", pool_dma=True)
    n_own = 0
    with ExitStack() as st:
        wr = S.sb("router_w", [P, KD, N_EXP], F32, st)
        lg = S.sb("router_lg", [P, TT, N_EXP], F32, st)
        top = S.sb("router_top", [P, TT, 8], F32, st)
        top_i = S.sb("router_ti", [P, TT, 8], U32, st)
        top_f = S.sb("router_tf", [P, TT, 8], F32, st)
        hot = S.sb("router_hot", [P, TT, 2, N_EXP], F32, st)
        both = S.sb("router_both", [P, TT, N_EXP], F32, st)
        e2 = S.sb("router_e2", [P, TT, 1], F32, st)
        total = S.sb("router_total", [P, TT, 1], F32, st)
        count = S.sb("router_count", [P, N_EXP], F32, st)
        need = S.sb("router_need", [P, 2, N_EXP], F32, st)
        large = S.sb("router_large", [P, N_EXP], F32, st)
        begin = S.sb("router_begin", [P, 2, N_EXP], F32, st)
        more = S.sb("router_more", [P, N_EXP], F32, st)
        upto = S.sb("router_upto", [P, 2, N_EXP], F32, st)
        first = S.sb("router_first", [P, N_EXP], F32, st)
        pos = S.sb("router_pos", [P, TT, N_EXP], F32, st)
        prod = S.sb("router_prod", [P, TT, 2, N_EXP], F32, st)
        row = S.sb("router_row", [P, TT, 2], F32, st)
        past = S.sb("router_past", [P, 2, 16, N_EXP], F32, st)
        owner = S.sb("router_owner", [P, 2, 16], F32, st)
        token_i = S.sb("router_token", [P, TT], I32, st)
        zero_rows = S.sb("router_zero", [1, ROWS_MAX], I32, st)
        blank = S.sb("router_blank", [P, D], F32, st)
        with nc.Block("route") as block:
            @block.sync
            def _(sp):
                with nc.allow_non_contiguous_dma(reason="32 KB of router weights"):
                    sp.dma_start(wr[:, :, :], a["moe_router"][0].rearrange("(k p) e -> p k e", p=P)).then_inc(got.sem, 16)

            @block.tensor
            def _(pe):
                pe.wait_ge(got.sem, got.at(16))
                for t in range(TT):
                    for k in range(KD):
                        last = nc.tensor.matmul(ps[t][:, 0:N_EXP], xT[:, k, t * P:(t + 1) * P], wr[:, k, :],
                                                start=(k == 0), stop=(k == KD - 1))
                    last.then_inc(logits.sem, 1)
                pe.wait_ge(chosen.sem, chosen.at(1))
                for t in range(TT):
                    for u in range(t + 1):
                        nc.tensor.matmul(ps[4 + t % 2][:, t * 8:t * 8 + 8], S.const("before") if u == t else S.const("ones"),
                                         both[:, u, :], start=(u == 0), stop=(u == t))
                for u in range(TT):
                    last = nc.tensor.matmul(ps[6][:, 0:8], S.const("ones"), both[:, u, :], start=(u == 0), stop=(u == TT - 1))
                last.then_inc(placed.sem, 1)

            @block.scalar
            def _(act):
                act.wait_ge(zeroed.sem, zeroed.at(2))
                act.dma_start(R.y.rearrange("(a p) d -> p a d", p=P),
                              blank[:, :].unsqueeze(1).broadcast_to([P, ROWS_MAX // P, D])).then_inc(blanked.sem, 16)
                act.wait_ge(gates_in.sem, gates_in.at(1))
                nc.scalar.activation(e2[:, :, :], e2[:, :, :], ACT.Exp).then_inc(gates_e.sem, 1)
                act.wait_ge(blanked.sem, blanked.at(16))

            @block.vector
            def _(dve):
                nonlocal n_own
                o = Count(own)
                iota8 = S.const("iota16")[:, 0:8]
                for t in range(TT):
                    dve.wait_ge(logits.sem, logits.at(t + 1))
                    nc.vector.tensor_copy(lg[:, t, :], ps[t][:, 0:N_EXP]).then_inc(own.sem, o.up())
                dve.wait_ge(own.sem, o.value())
                for t in range(TT):
                    nc.vector.max(top[:, t, :], lg[:, t, :]).then_inc(own.sem, o.up())
                dve.wait_ge(own.sem, o.value())
                for t in range(TT):
                    nc.vector.max_index(top_i[:, t, :], top[:, t, :], lg[:, t, :]).then_inc(own.sem, o.up())
                nc.vector.tensor_tensor(e2[:, :, :], top[:, :, 1:2], top[:, :, 0:1], ALU.subtract).then_inc(gates_in.sem, 1)
                dve.wait_ge(own.sem, o.value())
                nc.vector.tensor_copy(top_f[:, :, :], top_i[:, :, :]).then_inc(own.sem, o.up())
                dve.wait_ge(own.sem, o.value())
                for c in range(2):
                    nc.vector.tensor_tensor(hot[:, :, c, :], iota8.unsqueeze(1).broadcast_to([P, TT, 8]),
                                                   top_f[:, :, c:c + 1].broadcast_to([P, TT, 8]), ALU.is_equal).then_inc(own.sem, o.up())
                dve.wait_ge(own.sem, o.value())
                nc.vector.tensor_tensor(both[:, :, :], hot[:, :, 0, :], hot[:, :, 1, :], ALU.add).then_inc(chosen.sem, 1)
                dve.wait_ge(gates_e.sem, gates_e.at(1))
                nc.vector.tensor_scalar(total[:, :, :], e2[:, :, :], 1.0, None, ALU.add).then_inc(own.sem, o.up())
                dve.wait_ge(own.sem, o.value())
                nc.vector.reciprocal(R.gates[:, :, 0:1], total[:, :, :]).then_inc(own.sem, o.up())
                dve.wait_ge(own.sem, o.value())
                nc.vector.tensor_tensor(R.gates[:, :, 1:2], R.gates[:, :, 0:1], e2[:, :, :], ALU.mult).then_inc(own.sem, o.up())
                dve.wait_ge(placed.sem, placed.at(1))
                for t in range(TT):
                    nc.vector.tensor_copy(pos[:, t, :], ps[4 + t % 2][:, t * 8:t * 8 + 8]).then_inc(own.sem, o.up())
                nc.vector.tensor_copy(count[:, :], ps[6][:, 0:8]).then_inc(own.sem, o.up())
                dve.wait_ge(own.sem, o.value())
                nc.vector.tensor_scalar(need[:, 0, :], count[:, :], 0.0, None, ALU.is_gt).then_inc(own.sem, o.up())
                nc.vector.tensor_scalar(large[:, :], count[:, :], float(UNIT_ROWS[0]), None, ALU.is_gt).then_inc(own.sem, o.up())
                nc.vector.tensor_scalar(need[:, 1, :], count[:, :], float(UNIT_ROWS[0]), None, ALU.is_gt).then_inc(own.sem, o.up())
                dve.wait_ge(own.sem, o.value())
                nc.vector.tensor_tensor(need[:, 0, :], need[:, 0, :], large[:, :], ALU.subtract).then_inc(own.sem, o.up())
                for m in range(1, (T + UNIT_ROWS[1] - 1) // UNIT_ROWS[1]):
                    nc.vector.tensor_scalar(more[:, :], count[:, :], float(m * UNIT_ROWS[1]), None, ALU.is_gt).then_inc(own.sem, o.up())
                    dve.wait_ge(own.sem, o.value())
                    nc.vector.tensor_tensor(need[:, 1, :], need[:, 1, :], more[:, :], ALU.add).then_inc(own.sem, o.up())
                    dve.wait_ge(own.sem, o.value())
                for c in range(2):
                    nc.vector.tensor_tensor_scan(upto[:, c, :], S.const("ones")[:, 0:8], need[:, c, :], 0.0, ALU.mult,
                                                 ALU.add).then_inc(own.sem, o.up())
                dve.wait_ge(own.sem, o.value())
                nc.vector.tensor_tensor(begin[:, :, :], upto[:, :, :], need[:, :, :], ALU.subtract).then_inc(own.sem, o.up())
                dve.wait_ge(own.sem, o.value())
                for c in range(2):
                    nc.vector.tensor_scalar(begin[:, c, :], begin[:, c, :], float(UNIT_ROWS[c]), float(FIRST_ROW[c]), ALU.mult,
                                            ALU.add).then_inc(own.sem, o.up())
                dve.wait_ge(own.sem, o.value())
                nc.vector.tensor_tensor(begin[:, 0, :], begin[:, 0, :], need[:, 0, :], ALU.mult).then_inc(own.sem, o.up())
                nc.vector.tensor_tensor(begin[:, 1, :], begin[:, 1, :], large[:, :], ALU.mult).then_inc(own.sem, o.up())
                dve.wait_ge(own.sem, o.value())
                nc.vector.tensor_tensor(first[:, :], begin[:, 0, :], begin[:, 1, :], ALU.add).then_inc(own.sem, o.up())
                dve.wait_ge(own.sem, o.value())
                nc.vector.tensor_tensor(pos[:, :, :], pos[:, :, :], first[:, :].unsqueeze(1).broadcast_to([P, TT, 8]),
                                               ALU.add).then_inc(own.sem, o.up())
                dve.wait_ge(own.sem, o.value())
                for c in range(2):
                    nc.vector.tensor_tensor(prod[:, :, c, :], hot[:, :, c, :], pos[:, :, :], ALU.mult).then_inc(own.sem, o.up())
                dve.wait_ge(own.sem, o.value())
                nc.vector.tensor_reduce(row[:, :, :], prod[:, :, :, :], AX.X, ALU.add).then_inc(own.sem, o.up())
                dve.wait_ge(own.sem, o.value())
                nc.vector.tensor_copy(R.row[:, :, :], row[:, :, :]).then_inc(ids.sem, 1)
                nc.vector.tensor_copy(token_i[:, :], S.const("token")).then_inc(ids.sem, 1)
                for c in range(2):
                    nc.vector.tensor_tensor(past[:, c, :, :], S.const("iota16").unsqueeze(2).broadcast_to([P, 16, 8]),
                                            upto[:, c, :].unsqueeze(1).broadcast_to([P, 16, 8]), ALU.is_ge).then_inc(own.sem, o.up())
                dve.wait_ge(own.sem, o.value())
                nc.vector.tensor_reduce(owner[:, :, :], past[:, :, :, :], AX.X, ALU.add).then_inc(own.sem, o.up())
                nc.vector.tensor_scalar(upto[:, :, :], upto[:, :, :], 1.0, None, ALU.max).then_inc(own.sem, o.up())
                dve.wait_ge(own.sem, o.value())
                nc.vector.tensor_scalar(owner[:, :, :], owner[:, :, :], float(N_EXP - 1), None, ALU.min).then_inc(own.sem, o.up())
                dve.wait_ge(own.sem, o.value())
                nc.vector.tensor_copy(R.expert[:, :, :], owner[:, :, :]).then_inc(own.sem, o.up())
                nc.vector.tensor_copy(R.units[:, :], upto[:, :, N_EXP - 1]).then_inc(own.sem, o.up())
                n_own = o.n

            @block.gpsimd
            def _(pool):
                nc.gpsimd.memset(zero_rows[:, :], 0).then_inc(zeroed.sem, 1)
                nc.gpsimd.memset(blank[:, :], 0.0).then_inc(zeroed.sem, 1)
                pool.wait_ge(zeroed.sem, zeroed.at(2))
                pool.dma_start(R.token_of_row.rearrange("r o -> o r"), zero_rows[:, :]).then_inc(cleared.sem, 16)
                pool.wait_ge(cleared.sem, cleared.at(16))
                pool.wait_ge(ids.sem, ids.at(2))
                for t in range(TT):
                    for c in range(2):
                        pool.indirect_dma_start(
                            out=R.token_of_row, out_offset=bass.IndirectOffsetOnAxis(ap=R.row[:, t, c:c + 1], axis=0),
                            in_=token_i[:, t:t + 1], in_offset=None).then_inc(scattered.sem, 16)
                pool.wait_ge(scattered.sem, scattered.at(16 * 2 * TT))
        for s, n in ((got, 16), (logits, TT), (own, n_own), (gates_in, 1), (gates_e, 1), (chosen, 1), (placed, 1),
                     (zeroed, 2), (cleared, 16), (blanked, 16), (scattered, 32 * TT), (ids, 2)):
            s.base += n


class ExpertRows:

    def __init__(self, S, R, size, st):
        self.S, self.R = S, R
        self.rows, self.row0 = UNIT_ROWS[size], FIRST_ROW[size]
        self.xg = S.sb(f"rows{size}_x", [P, 2, D], F32, st)
        self.xu = S.sb(f"rows{size}_xt", [P, KD, self.rows], F32, st)
        self.yrow = S.sb(f"rows{size}_y", [P, 2, D], F32, st)
        self.index = S.sb(f"rows{size}_index", [P, 2], I32, st)
        self.subs = row_parts(self.rows)
        self.indexed, self.gathered = (S.sig(f"e{size}_{x}", pool_dma=True) for x in ("indexed", "gathered"))
        self.turned, self.stored, self.x_ready = (S.sig(f"e{size}_{x}") for x in ("turned", "stored", "x_ready"))
        self.emitted = S.sig(f"s{size}_emitted")

    def fetch(self, pool, u):
        S, nc, R = self.S, self.S.nc, self.R
        pool.wait_ge(self.turned.sem, self.turned.at(2 * len(self.subs) * u))
        settle(pool, S.sig("passed_pool"))
        for s, (r0, n) in enumerate(self.subs):
            pool.dma_start(self.index[0:n, s:s + 1], R.token_of_row[bass.ds(u * self.rows + self.row0 + r0, n), :]).then_inc(self.indexed.sem, 16)
        pool.wait_ge(self.indexed.sem, self.indexed.at(16 * len(self.subs) * (u + 1)))
        settle(pool, S.sig("passed_pool"))
        for s, (r0, n) in enumerate(self.subs):
            pool.indirect_dma_start(out=self.xg[0:n, s, :], out_offset=None, in_=R.xn,
                                    in_offset=bass.IndirectOffsetOnAxis(ap=self.index[0:n, s:s + 1], axis=0),
                                    ).then_inc(self.gathered.sem, 16)

    def turn(self, pe, u):
        S, nc = self.S, self.S.nc
        pe.wait_ge(self.gathered.sem, self.gathered.at(16 * len(self.subs) * (u + 1)))
        pe.wait_ge(self.emitted.sem, self.emitted.at(2 * len(self.subs) * u))
        settle(pe, S.sig("passed_pe"))
        for s, (r0, n) in enumerate(self.subs):
            for half in range(2):
                for kk in range(4):
                    c = (4 * half + kk) * P
                    last = nc.tensor.transpose(S.ps[4 + 2 * s + half][:, kk * P:kk * P + n], self.xg[0:n, s, c:c + P],
                                               S.const("ident")[0:n, 0:n])
                last.then_inc(self.turned.sem, 1)

    def place(self, dve, u):
        S, nc = self.S, self.S.nc
        for s, (r0, n) in enumerate(self.subs):
            for half in range(2):
                dve.wait_ge(self.turned.sem, self.turned.at(2 * len(self.subs) * u + 2 * s + half + 1))
                src = S.ps[4 + 2 * s + half][:, :].rearrange("p (k r) -> p k r", k=4)[:, :, 0:n]
                g = S.gains[:, 3, 4 * half:4 * half + 4].unsqueeze(2).broadcast_to([P, 4, n])
                nc.vector.tensor_tensor(self.xu[:, 4 * half:4 * half + 4, r0:r0 + n], src, g,
                                        ALU.mult).then_inc(self.x_ready.sem, 1)

    def before_emit(self, dve, u):
        dve.wait_ge(self.stored.sem, self.stored.at(16 * len(self.subs) * u))

    def emit(self, u, s, half, src):
        n = self.subs[s][1]
        return self.S.nc.vector.tensor_copy(self.yrow[0:n, s, half * 512:(half + 1) * 512], src)

    def store(self, act, u):
        for s, (r0, n) in enumerate(self.subs):
            act.wait_ge(self.emitted.sem, self.emitted.at(2 * len(self.subs) * u + 2 * s + 2))
            act.dma_start(self.R.y[bass.ds(u * self.rows + self.row0 + r0, n), :], self.yrow[0:n, s, :]).then_inc(self.stored.sem, 16)
        act.wait_ge(self.stored.sem, self.stored.at(16 * len(self.subs) * (u + 1)))


class Routing:
    pass


def expert_values(eng, tile, lo, hi):
    return eng.value_load(tile, min_val=lo, max_val=hi)


def moe1(S):
    nc, a = S.nc, S.a
    with ExitStack() as st:
        R = Routing()
        R.gates = S.sb("gates", [P, TT, 2], F32, st)
        R.row = S.sb("row_of", [P, TT, 2], I32, st)
        R.expert = S.sb("expert_of", [P, 2, 16], I32, st)
        R.units = S.sb("n_units", [P, 2], I32, st)
        R.xn = nc.dram_tensor("xn_rows", (T, D), F32, kind="Internal").ap()
        R.y = nc.dram_tensor("y_rows", (ROWS_MAX, D), F32, kind="Internal").ap()
        R.token_of_row = nc.dram_tensor("token_of_row", (ROWS_MAX, 1), I32, kind="Internal").ap()
        norm_stage(S, "norm3", S.gains[:, 3, :], xn_dram=R.xn)
        route_stage(S, R)
        for size in range(2):
            with ExitStack() as st2:
                rows = ExpertRows(S, R, size, st2)

                def weights(eng, u, size=size):
                    e = expert_values(eng, R.expert[0:1, size, bass.ds(u, 1)], 0, N_EXP - 1)
                    one = lambda w: w[0][bass.ds(e, 1)].rearrange("o a b -> (o a) b")
                    return one(a["moe_w_gate"]), one(a["moe_w_up"]), one(a["moe_w_down"])

                swiglu_stage(S, f"experts{size}", f"s{size}_", UNIT_ROWS[size], E_FF,
                             lambda eng, size=size: expert_values(eng, R.units[0:1, size:size + 1], 1, UNITS_MAX[size]), weights,
                             lambda k, u, rows=rows: rows.xu[:, k, :], rows, rows.emit)
        combine_stage(S, R)


def combine_stage(S, R):
    nc = S.nc
    got, own = S.sig("c_got", pool_dma=True), S.sig("c_own")
    with ExitStack() as st:
        yg = S.sb("combine_y", [P, TT, 2, D], F32, st)
        with nc.Block("combine") as block:
            @block.gpsimd
            def _(pool):
                for t in range(TT):
                    for c in range(2):
                        pool.indirect_dma_start(out=yg[:, t, c, :], out_offset=None, in_=R.y,
                                                in_offset=bass.IndirectOffsetOnAxis(ap=R.row[:, t, c:c + 1], axis=0),
                                                ).then_inc(got.sem, 16)

            @block.vector
            def _(dve):
                o = Count(own)
                dve.wait_ge(got.sem, got.at(16 * 2 * TT))
                for c in range(2):
                    for t in range(TT):
                        nc.vector.scalar_tensor_tensor(S.h[:, t, :], yg[:, t, c, :], R.gates[:, t, c:c + 1],
                                                              S.h[:, t, :], ALU.mult, ALU.add).then_inc(own.sem, o.up())
                    dve.wait_ge(own.sem, o.value())
        got.base += 32 * TT
        own.base += 8


def row_norm_stage(S, name, gain):
    nc, h = S.nc, S.h
    got, squares, own, inverse, roots, ready = (S.sig("w_" + x) for x in ("got", "squares", "own", "inverse", "roots", "ready"))
    with ExitStack() as st:
        junk = S.sb(name + "_sq", [P, TT, D], F32, st)
        g = S.sb(name + "_g", [P, D], F32, st)
        ss = S.sb(name + "_ss", [P, TT], F32, st)
        r = S.sb(name + "_r", [P, TT], F32, st)
        with nc.Block(name) as block:
            @block.sync
            def _(sp):
                sp.dma_start(g[:, :], gain.partition_broadcast(P)).then_inc(got.sem, 16)

            @block.scalar
            def _(act):
                for t in range(TT):
                    nc.scalar.activation(junk[:, t, :], h[:, t, :], ACT.Square, accum_out=ss[:, t:t + 1]).then_inc(squares.sem, 1)
                act.wait_ge(inverse.sem, inverse.at(1))
                nc.scalar.activation(r[:, :], ss[:, :], ACT.Sqrt).then_inc(roots.sem, 1)

            @block.vector
            def _(dve):
                o = Count(own)
                dve.wait_ge(squares.sem, squares.at(TT))
                nc.vector.tensor_scalar(ss[:, :], ss[:, :], 1.0 / D, EPS, ALU.mult, ALU.add).then_inc(own.sem, o.up())
                dve.wait_ge(own.sem, o.value())
                nc.vector.reciprocal(ss[:, :], ss[:, :]).then_inc(inverse.sem, 1)
                dve.wait_ge(roots.sem, roots.at(1))
                dve.wait_ge(got.sem, got.at(16))
                for t in range(TT):
                    nc.vector.scalar_tensor_tensor(h[:, t, :], h[:, t, :], r[:, t:t + 1], g[:, :], ALU.mult,
                                                   ALU.mult).then_inc(ready.sem, 1)
        for s, n in ((got, 16), (squares, TT), (own, 1), (inverse, 1), (roots, 1), (ready, TT)):
            s.base += n


def ada_stage(S, M):
    nc, a, ps = S.nc, S.a, S.ps
    NW, NC = 3, 6 * D // 512
    got, c_ready, summed, turned, own, rows_made, biased = (
        S.sig("d_" + x) for x in ("got", "c", "summed", "turned", "own", "rows", "biased"))
    row_summed, row_out = S.sig("d_row_summed"), S.sig("d_row_out")
    loaded = [S.sig(f"d_loaded{b}") for b in range(NW)]
    n_own = 0
    with ExitStack() as st:
        wring = S.sb("ada_w", [P, NW, KD, 512], F32, st)
        small = S.sb("ada_small", [6 * KD + KD, P], F32, st)
        cT = S.sb("ada_c", [P, KD], F32, st)
        row = S.sb("ada_row", [1, 2, 512], F32, st)
        with nc.Block("ada") as block:
            @block.sync
            def _(sp):
                sp.dma_start(small[0:48, :], a["b_ada_2"][0].rearrange("(m p) -> m p", p=P)).then_inc(got.sem, 16)
                sp.dma_start(small[48:56, :], a["c_2"][0].rearrange("(m p) -> m p", p=P)).then_inc(got.sem, 16)
                for c in range(NC):
                    if c >= NW:
                        sp.wait_ge(row_summed.sem, row_summed.at(c - NW + 1))
                    sp.dma_start(wring[:, c % NW, :, :], a["w_ada_2"][0][:, c * 512:(c + 1) * 512].rearrange(
                        "(k p) n -> p k n", p=P)).then_inc(loaded[c % NW].sem, 16)

            @block.tensor
            def _(pe):
                pe.wait_ge(got.sem, got.at(32))
                nc.tensor.transpose(ps[1][:, 0:56], small[:, :], S.const("ident")[0:56, 0:56]).then_inc(turned.sem, 1)
                pe.wait_ge(c_ready.sem, c_ready.at(1))

                def turn_row(c):
                    pe.wait_ge(row_out.sem, row_out.at(c + 1))
                    for m in range(4):
                        last = nc.tensor.matmul(ps[0][:, 4 * c + m:4 * c + m + 1], row[:, c % 2, m * P:(m + 1) * P],
                                                S.const("ones")[0:1, 0:1], start=True, stop=True)
                    last.then_inc(summed.sem, 1)

                for c in range(NC):
                    pe.wait_ge(loaded[c % NW].sem, loaded[c % NW].at(16 * (c // NW + 1)))
                    if c >= 2:
                        pe.wait_ge(row_out.sem, row_out.at(c - 1))
                    for k in range(KD):
                        last = nc.tensor.matmul(ps[6 + c % 2][0:1, :], cT[:, k:k + 1], wring[:, c % NW, k, :],
                                                start=(k == 0), stop=(k == KD - 1))
                    last.then_inc(row_summed.sem, 1)
                    if c:
                        turn_row(c - 1)
                turn_row(NC - 1)
                pe.wait_ge(own.sem, own.at(1))
                for g, part in enumerate((2, 5)):
                    for m in range(KD):
                        col = M.col[:, part * KD + m:part * KD + m + 1].broadcast_to([P, P])
                        last = nc.tensor.matmul(ps[2 + 2 * g + m // 4][:, (m % 4) * P:(m % 4 + 1) * P], col,
                                                S.const("ident"), start=True, stop=True)
                last.then_inc(rows_made.sem, 1)

            @block.scalar
            def _(act):
                act.wait_ge(turned.sem, turned.at(1))
                nc.scalar.activation(cT[:, :], ps[1][:, 48:56], ACT.Silu).then_inc(c_ready.sem, 1)
                for c in range(NC):
                    act.wait_ge(row_summed.sem, row_summed.at(c + 1))
                    if c >= 2:
                        act.wait_ge(summed.sem, summed.at(c - 1))
                    nc.scalar.activation(row[:, c % 2, :], ps[6 + c % 2][0:1, :], ACT.Copy).then_inc(row_out.sem, 1)

            @block.vector
            def _(dve):
                nonlocal n_own
                o = Count(own)
                dve.wait_ge(summed.sem, summed.at(NC))
                dve.wait_ge(turned.sem, turned.at(1))
                nc.vector.tensor_copy(M.bias[:, :], ps[1][:, 0:48]).then_inc(biased.sem, 1)
                dve.wait_ge(biased.sem, biased.at(1))
                nc.vector.tensor_tensor(M.col[:, :], ps[0][:, 0:48], M.bias[:, :], ALU.add).then_inc(own.sem, o.up())
                dve.wait_ge(own.sem, o.value())
                for gain, part, g in ((M.gain1, 1, 4), (M.gain2, 4, 5)):
                    nc.vector.scalar_tensor_tensor(gain[:, :], M.col[:, part * KD:(part + 1) * KD], 1.0,
                                                          S.gains[:, g, :], ALU.add, ALU.mult).then_inc(own.sem, o.up())
                dve.wait_ge(rows_made.sem, rows_made.at(1))
                for g in range(2):
                    for half in range(2):
                        nc.vector.tensor_copy(M.rows[:, g, half * 512:(half + 1) * 512], ps[2 + 2 * g + half][:, :]).then_inc(own.sem, o.up())
                n_own = o.n
        for s, n in ((got, 32), (c_ready, 1), (summed, NC), (turned, 1), (own, n_own), (rows_made, 1), (biased, 1),
                     (row_summed, NC), (row_out, NC),
                     *((loaded[b], 16 * (NC // NW)) for b in range(NW))):
            s.base += n


def latent_stage(S, lat, latT, qa, q_lat, w_uk_T, gain):
    nc, a, ps = S.nc, S.a, S.ps
    got, squares, inverse, roots, own, normed, turned, copied, made, cleared = (
        S.sig("l_" + x) for x in ("got", "squares", "inverse", "roots", "own", "normed", "turned", "copied", "made", "cleared"))
    with ExitStack() as st:
        uk = S.sb("w_uk_sb", [P, 8, 64], F32, st)
        g = S.sb("g_kv_row", [P, P], F32, st)
        sq = S.sb("lat_sq", [P, TT, P], F32, st)
        ss = S.sb("lat_ss", [P, TT], F32, st)
        r = S.sb("lat_r", [P, TT], F32, st)
        n_own = 0
        with nc.Block("latent") as block:
            @block.gpsimd
            def _(pool):
                nc.gpsimd.memset(uk[:, :, 0:16], 0.0).then_inc(cleared.sem, 1)

            @block.sync
            def _(sp):
                sp.dma_start(uk[:, :, 16:64], a["w_uk_2"][0]).then_inc(got.sem, 16)
                sp.dma_start(g[:, :], a["g_kv_2"][0].partition_broadcast(P)).then_inc(got.sem, 16)

            @block.scalar
            def _(act):
                for t in range(TT):
                    nc.scalar.activation(sq[:, t, :], lat[:, t, :], ACT.Square, accum_out=ss[:, t:t + 1]).then_inc(squares.sem, 1)
                act.wait_ge(inverse.sem, inverse.at(1))
                nc.scalar.activation(r[:, :], ss[:, :], ACT.Sqrt).then_inc(roots.sem, 1)
                for h in range(8):
                    act.wait_ge(made.sem, made.at(h + 1))
                    nc.scalar.activation(q_lat[:, h, :], ps[h][:, :], ACT.Copy).then_inc(copied.sem, 1)

            @block.vector
            def _(dve):
                nonlocal n_own
                o = Count(own)
                dve.wait_ge(squares.sem, squares.at(TT))
                nc.vector.tensor_scalar(ss[:, :], ss[:, :], 1.0 / P, EPS, ALU.mult, ALU.add).then_inc(own.sem, o.up())
                dve.wait_ge(own.sem, o.value())
                nc.vector.reciprocal(ss[:, :], ss[:, :]).then_inc(inverse.sem, 1)
                dve.wait_ge(roots.sem, roots.at(1))
                dve.wait_ge(got.sem, got.at(32))
                for t in range(TT):
                    nc.vector.scalar_tensor_tensor(lat[:, t, :], lat[:, t, :], r[:, t:t + 1], g[:, :], ALU.mult,
                                                   ALU.mult).then_inc(normed.sem, 1)
                dve.wait_ge(turned.sem, turned.at(1))
                nc.vector.tensor_copy(w_uk_T[:, :, :], ps[0][:, :].rearrange("p (m r) -> p m r", m=4)).then_inc(own.sem, o.up())
                dve.wait_ge(turned.sem, turned.at(2))
                nc.vector.tensor_copy(latT[:, :], ps[1][:, :]).then_inc(own.sem, o.up())
                n_own = o.n

            @block.tensor
            def _(pe):
                pe.wait_ge(got.sem, got.at(32))
                pe.wait_ge(cleared.sem, cleared.at(1))
                for m in range(4):
                    last = nc.tensor.transpose(ps[0][:, m * P:(m + 1) * P], uk[:, 2 * m:2 * m + 2, :].rearrange("p h n -> p (h n)"),
                                               S.const("ident"))
                last.then_inc(turned.sem, 1)
                pe.wait_ge(normed.sem, normed.at(TT))
                for t in range(TT):
                    last = nc.tensor.transpose(ps[1][:, t * P:(t + 1) * P], lat[:, t, :], S.const("ident"))
                last.then_inc(turned.sem, 1)
                pe.wait_ge(own.sem, own.at(3))
                for h in range(8):
                    b = 64 * (h % 2)
                    nc.tensor.matmul(ps[h][:, :], w_uk_T[b:b + 64, h // 2, :], qa[b:b + 64, h // 2, :], start=True,
                                     stop=True).then_inc(made.sem, 1)
        for s, n in ((got, 32), (squares, TT), (inverse, 1), (roots, 1), (own, n_own), (normed, TT), (turned, 2), (copied, 8),
                     (made, 8), (cleared, 1)):
            s.base += n


def index_stage(S, iq, ik, iw, bias):
    nc, ps = S.nc, S.ps
    H = 8
    dots, relus, own, weighed = (S.sig("i_" + x) for x in ("dots", "relus", "own", "weighed"))
    n_own = 0
    with ExitStack() as st:
        work = S.sb("index_work", [P, TT - 1, T], F32, st)
        r = S.sb("index_relu", [P, 4, T], F32, st)
        best = S.sb("index_best", [P, TT - 1, 8], F32, st)
        w = S.sb("index_w", [P, TT, H], F32, st)
        with nc.Block("indexer") as block:
            @block.tensor
            def _(pe):
                for t in range(1, TT):
                    K = (t + 1) * P
                    for h in range(H):
                        n = (t - 1) * H + h
                        b = 32 * (h % 4)
                        if n >= 8:
                            pe.wait_ge(relus.sem, relus.at(n - 7))
                        nc.tensor.matmul(ps[n % 8][:, 0:K], iq[b:b + 32, h // 4, t * P:(t + 1) * P], ik[b:b + 32, 0:K],
                                         start=True, stop=True).then_inc(dots.sem, 1)

            @block.scalar
            def _(act):
                for t in range(1, TT):
                    for h in range(H):
                        n = (t - 1) * H + h
                        act.wait_ge(dots.sem, dots.at(n + 1))
                        if n >= 4:
                            act.wait_ge(weighed.sem, weighed.at(n - 3))
                        K = (t + 1) * P
                        nc.scalar.activation(r[:, n % 4, 0:K], ps[n % 8][:, 0:K], ACT.Relu, scale=32 ** -0.5).then_inc(relus.sem, 1)

            @block.vector
            def _(dve):
                nonlocal n_own
                o = Count(own)
                nc.vector.tensor_scalar(w[:, :, :], iw[:, :, :], 8 ** -0.5, None, ALU.mult).then_inc(own.sem, o.up())
                dve.wait_ge(own.sem, o.value())
                for t in range(1, TT):
                    K = (t + 1) * P
                    s = work[:, t - 1, 0:K]
                    for h in range(H):
                        n = (t - 1) * H + h
                        dve.wait_ge(relus.sem, relus.at(n + 1))
                        wt = w[:, t, h:h + 1]
                        if h == 0:
                            ins = nc.vector.tensor_scalar(s, r[:, n % 4, 0:K], wt, None, ALU.mult)
                        else:
                            dve.wait_ge(weighed.sem, weighed.at(n))
                            ins = nc.vector.scalar_tensor_tensor(s, r[:, n % 4, 0:K], wt, s, ALU.mult, ALU.add)
                        ins.then_inc(weighed.sem, 1)
                    dve.wait_ge(weighed.sem, weighed.at(H * t))
                    d = work[:, t - 1, t * P:K]
                    nc.vector.tensor_tensor(d, d, S.const("causal"), ALU.add).then_inc(own.sem, o.up())
                for i in range(DSA_TOPK // 8):
                    dve.wait_ge(own.sem, o.value())
                    for t in range(1, TT):
                        nc.vector.max(best[:, t - 1, :], work[:, t - 1, 0:(t + 1) * P]).then_inc(own.sem, o.up())
                    dve.wait_ge(own.sem, o.value())
                    for t in range(1, TT):
                        s = work[:, t - 1, 0:(t + 1) * P]
                        nc.vector.match_replace(s, best[:, t - 1, :], s, TAKEN).then_inc(own.sem, o.up())
                dve.wait_ge(own.sem, o.value())
                for t in range(1, TT):
                    K = (t + 1) * P
                    nc.vector.tensor_scalar(bias[:, t - 1, 0:K], work[:, t - 1, 0:K], -2.0e38, -NEG, ALU.is_le, ALU.mult).then_inc(own.sem, o.up())
                dve.wait_ge(own.sem, o.value())
                for t in range(1, TT):
                    K = (t + 1) * P
                    nc.vector.tensor_scalar(bias[:, t - 1, 0:K], bias[:, t - 1, 0:K], NEG, None, ALU.add).then_inc(own.sem, o.up())
                n_own = o.n


def attention_stage(S, A, mix):
    nc, ps = S.nc, S.ps
    items = [(t, h, kind) for t in range(TT) for h in range(8) for kind in "ab"]
    N = len(items)
    n_a = [sum(1 for x in items[:i] if x[2] == "a") for i in range(N + 1)]
    s_ = lambda x: S.sig("x_" + x)
    ready, logits, masked, scaled, exps, turned, copied, lat_made, lat_copied, made, inverse, taken, zeroed, cum_own = (
        s_(x) for x in ("ready", "logits", "masked", "scaled", "exps", "turned", "copied", "lat_made", "lat_copied", "made",
                        "inverse", "taken", "zeroed", "cum"))
    got = s_("got")
    ident = S.const("ident")
    with ExitStack() as st:
        cum = S.sb("cum", [8, T], F32, st)
        ncum = S.sb("ncum", [8, T], F32, st)
        past = S.sb("past_bias", [P, T], F32, st)
        uv = S.sb("w_uv_sb", [P, 8, 64], F32, st)
        lg = S.sb("logits_sb", [P, 3, T], F32, st)
        pT = S.sb("probs_t", [P, 2, T], F32, st)
        olT = S.sb("o_lat", [P, 2, P], F32, st)
        top = S.sb("row_max", [P, N], F32, st)
        rsum = S.sb("row_sum", [P, N], F32, st)
        rinv = S.sb("row_inv", [P, N], F32, st)

        def bias_of(t, kind):
            K = (t + 1) * P
            if kind == "b" or t == 0:
                return past[:, T - K:T]
            return A.bias[:, t - 1, 0:K]

        with nc.Block("attention") as block:
            @block.sync
            def _(sp):
                sp.dma_start(uv[:, :, :], A.w_uv).then_inc(got.sem, 16)

            @block.vector
            def _(dve):
                nc.vector.memset(past[:, 0:T - P], 0.0).then_inc(zeroed.sem, 1)
                nc.vector.tensor_copy(past[:, T - P:T], S.const("causal")).then_inc(zeroed.sem, 1)
                nc.vector.tensor_tensor_scan(cum[:, :], A.ones8, A.logf[:, :], 0.0, ALU.mult, ALU.add).then_inc(cum_own.sem, 1)
                dve.wait_ge(cum_own.sem, cum_own.at(1))
                nc.vector.tensor_scalar(ncum[:, :], cum[:, :], -1.0, None, ALU.mult).then_inc(cum_own.sem, 1)
                dve.wait_ge(zeroed.sem, zeroed.at(2))
                for i in range(N + 4):
                    if i < N:
                        t, h, kind = items[i]
                        K = (t + 1) * P
                        dve.wait_ge(logits.sem, logits.at(i + 1))
                        if i >= 3:
                            dve.wait_ge(turned.sem, turned.at(i - 2))
                        nc.vector.tensor_tensor_reduce(out=lg[:, i % 3, 0:K], in0=ps[i % 3][:, 0:K], in1=bias_of(t, kind),
                                                       scale=1.0, scalar=-3.0e38, op0=ALU.add, op1=ALU.max,
                                                       accum_out=top[:, i:i + 1]).then_inc(masked.sem, 1)
                        dve.wait_ge(masked.sem, masked.at(i + 1))
                        nc.vector.tensor_scalar(top[:, i:i + 1], top[:, i:i + 1], -0.125 if kind == "a" else -1.0, None,
                                                ALU.mult).then_inc(scaled.sem, 1)
                    j = i - 2
                    if 0 <= j < N:
                        t, h, kind = items[j]
                        K = (t + 1) * P
                        dve.wait_ge(turned.sem, turned.at(j + 1))
                        if j >= 2:
                            if items[j - 2][2] == "a":
                                dve.wait_ge(lat_made.sem, lat_made.at(n_a[j - 1]))
                            else:
                                dve.wait_ge(made.sem, made.at(j - 1))
                        nc.vector.tensor_copy(pT[:, j % 2, 0:K], ps[3 + j % 2][:, 0:K]).then_inc(copied.sem, 1)
                        dve.wait_ge(exps.sem, exps.at(j + 1))
                        nc.vector.reciprocal(rinv[:, j:j + 1], rsum[:, j:j + 1]).then_inc(inverse.sem, 1)
                    j = i - 4
                    if 0 <= j < N:
                        t, h, kind = items[j]
                        dve.wait_ge(made.sem, made.at(j + 1))
                        dve.wait_ge(inverse.sem, inverse.at(j + 1))
                        at = (0 if kind == "a" else 512) + h * 64
                        nc.vector.tensor_scalar(mix[:, t, at:at + 64], ps[6 + j % 2][:, 0:64], rinv[:, j:j + 1], None,
                                                ALU.mult).then_inc(taken.sem, 1)

            @block.scalar
            def _(act):
                for i in range(N + 3):
                    if i < N:
                        t, h, kind = items[i]
                        K = (t + 1) * P
                        act.wait_ge(scaled.sem, scaled.at(i + 1))
                        nc.scalar.activation(lg[:, i % 3, 0:K], lg[:, i % 3, 0:K], ACT.Exp, bias=top[:, i:i + 1],
                                             scale=0.125 if kind == "a" else 1.0,
                                             accum_out=rsum[:, i:i + 1]).then_inc(exps.sem, 1)
                    j = i - 3
                    if 0 <= j < N and items[j][2] == "a":
                        act.wait_ge(lat_made.sem, lat_made.at(n_a[j] + 1))
                        if n_a[j] >= 2:
                            act.wait_ge(made.sem, made.at([x for x in range(N) if items[x][2] == "a"][n_a[j] - 2] + 1))
                        nc.scalar.activation(olT[:, n_a[j] % 2, :], ps[5][:, 0:P], ACT.Copy).then_inc(lat_copied.sem, 1)

            @block.tensor
            def _(pe):
                pe.wait_ge(got.sem, got.at(16))
                pe.wait_ge(cum_own.sem, cum_own.at(2))
                for i in range(N + 4):
                    if i < N:
                        t, h, kind = items[i]
                        K = (t + 1) * P
                        q = slice(t * P, (t + 1) * P)
                        b = 64 * (h % 2)
                        if i >= 3:
                            pe.wait_ge(masked.sem, masked.at(i - 2))
                        out = ps[i % 3][:, 0:K]
                        if kind == "a":
                            nc.tensor.matmul(out, A.q_lat[:, h, q], A.latT[:, 0:K], start=True, stop=False)
                            last = nc.tensor.matmul(out, A.qa[b:b + 16, h // 2, q], A.kr[b:b + 16, 0:K], start=False, stop=True)
                        else:
                            nc.tensor.matmul(out, A.qb[b:b + 64, h // 2, q], A.kb[b:b + 64, h // 2, 0:K], start=True, stop=False)
                            nc.tensor.matmul(out, cum[:, q], ident[0:8, h:h + 1].broadcast_to([8, K]), start=False, stop=False)
                            last = nc.tensor.matmul(out, ident[0:8, h:h + 1].broadcast_to([8, P]), ncum[:, 0:K], start=False,
                                                    stop=True)
                        last.then_inc(logits.sem, 1)
                    j = i - 2
                    if 0 <= j < N:
                        pe.wait_ge(exps.sem, exps.at(j + 1))
                        if j >= 2:
                            pe.wait_ge(copied.sem, copied.at(j - 1))
                        for kt in range(items[j][0] + 1):
                            last = nc.tensor.transpose(ps[3 + j % 2][:, kt * P:(kt + 1) * P], lg[:, j % 3, kt * P:(kt + 1) * P], ident)
                        last.then_inc(turned.sem, 1)
                    j = i - 3
                    if 0 <= j < N:
                        t, h, kind = items[j]
                        pe.wait_ge(copied.sem, copied.at(j + 1))
                        if kind == "a":
                            if n_a[j] >= 1:
                                pe.wait_ge(lat_copied.sem, lat_copied.at(n_a[j]))
                            for kt in range(t + 1):
                                last = nc.tensor.matmul(ps[5][:, 0:P], A.lat[:, kt, :], pT[:, j % 2, kt * P:(kt + 1) * P],
                                                        start=(kt == 0), stop=(kt == t))
                            last.then_inc(lat_made.sem, 1)
                    j = i - 4
                    if 0 <= j < N and items[j][2] == "a":
                        t, h, kind = items[j]
                        pe.wait_ge(lat_copied.sem, lat_copied.at(n_a[j] + 1))
                        if j >= 2:
                            pe.wait_ge(taken.sem, taken.at(j - 1))
                        nc.tensor.matmul(ps[6 + j % 2][:, 0:64], olT[:, n_a[j] % 2, :], uv[:, h, :], start=True,
                                         stop=True).then_inc(made.sem, 1)
                    j = i - 3
                    if 0 <= j < N and items[j][2] == "b":
                        t, h, kind = items[j]
                        if j >= 2:
                            pe.wait_ge(taken.sem, taken.at(j - 1))
                        for kt in range(t + 1):
                            last = nc.tensor.matmul(ps[6 + j % 2][:, 0:64], pT[:, j % 2, kt * P:(kt + 1) * P],
                                                    A.v[:, kt, h * 64:(h + 1) * 64], start=(kt == 0), stop=(kt == t))
                        last.then_inc(made.sem, 1)


def attention2(S, M):
    nc, a = S.nc, S.a
    w = a["w_in_2"][0]
    norm_stage(S, "norm4", M.gain1[:, :], shift=M.col[:, 0:KD])
    A = Routing()
    with ExitStack() as st:
        mix = S.sb("mix2", [P, TT, D], F32, st)
        with ExitStack() as st2:
            A.qa = S.sb("qa2", [P, 4, T], F32, st2)
            A.qb = S.sb("qb2", [P, 4, T], F32, st2)
            A.kb = S.sb("kb2", [P, 4, T], F32, st2)
            A.v = S.sb("vb2", [P, TT, 512], F32, st2)
            A.lat = S.sb("lat2", [P, TT, P], F32, st2)
            A.latT = S.sb("lat2T", [P, T], F32, st2)
            A.kr = S.sb("kr2", [P, T], F32, st2)
            A.q_lat = S.sb("q_lat", [P, 8, T], F32, st2)
            A.bias = S.sb("dsa_bias", [P, TT - 1, T], F32, st2)
            A.logf = S.sb("logf2", [8, T], F32, st2)
            A.ones8 = S.const("ones")[0:8, 0:1].broadcast_to([8, T])
            A.w_uv = a["w_uv_2"][0]
            iq = S.sb("iq2", [P, 2, T], F32, st2)
            ik = S.sb("ik2", [P, T], F32, st2)
            iw = S.sb("iw2", [P, TT, 8], F32, st2)
            f = S.sb("f2", [8, T], F32, st2)
            project_stage(S, "proj2", [
                (w[:, 0:512], "T", "copy", lambda m: A.qa[:, m, :]),
                (w[:, 512:640], "tok", "copy", lambda t: A.lat[:, t, :]),
                ([w[:, 640:704], w[:, 640:704]], "T", "copy", lambda m: A.kr[:, :]),
                (w[:, 656:912], "T", "copy", lambda m: iq[:, m, :]),
                ([w[:, 912:944]] * 4, "T", "copy", lambda m: ik[:, :]),
                (w[:, 944:952], "tok", "copy", lambda t: iw[:, t, :]),
                (w[:, 2488:2496], "T", "copy", lambda m: f[:, :]),
                (w[:, 952:1464], "T", 64 ** -0.5, lambda m: A.qb[:, m, :]),
                (w[:, 1464:1976], "T", "copy", lambda m: A.kb[:, m, :]),
                (w[:, 1976:2488], "tok", "copy", lambda t: A.v[:, t, :])])
            with ExitStack() as st3:
                ca, sa, ci, si = (S.sb(x, [P, T], F32, st3) for x in ("cos_a", "sin_a", "cos_i", "sin_i"))
                angle_stage(S, "angles2", a["positions_2"][0], [S.const("freq")[:, 1:2], S.const("freq")[:, 2:3]],
                            [(ca[:, :], sa[:, :]), (ci[:, :], si[:, :])])
                rotate_stage(S, "rotary2", [(A.qa[:, m, :], S.const("swap_a"), ca, sa) for m in range(4)]
                             + [(A.kr[:, :], S.const("swap_a"), ca, sa)]
                             + [(iq[:, m, :], S.const("swap_i"), ci, si) for m in range(2)]
                             + [(ik[:, :], S.const("swap_i"), ci, si)])
            with ExitStack() as st3:
                ukT = S.sb("w_uk_T", [P, 4, P], F32, st3)
                bf = S.sb("b_forget", [8, 1], F32, st3)
                load_stage(S, "load_bf", [(bf[:, :], a["b_forget_2"][0].rearrange("(h o) -> h o", o=1))])
                latent_stage(S, A.lat, A.latT, A.qa, A.q_lat, ukT, None)
                log_gate_stage(S, "log_forget", [(S.const("ident")[0:8, 0:8], f[:, :], bf[:, :], A.logf[:, :])], 1.0)
            index_stage(S, iq, ik, iw, A.bias)
            attention_stage(S, A, mix)
        head_norm_stage(S, "headnorm2", mix, 512, [(0, a["g_out_a_2"][0]), (512, a["g_out_b_2"][0])], None)
        w_out = a["w_out_2"][0]
        project_stage(S, "out2", [(w_out[:, c * 512:(c + 1) * 512], "tok", M.rows[:, 0, c * 512:(c + 1) * 512],
                                   lambda t, c=c: S.h[:, t, c * 512:(c + 1) * 512]) for c in range(2)])


def modulation(S, stack):
    M = Routing()
    M.col = S.sb("mod_col", [P, 48], F32, stack)
    M.bias = S.sb("mod_bias", [P, 48], F32, stack)
    M.gain1 = S.sb("mod_gain1", [P, KD], F32, stack)
    M.gain2 = S.sb("mod_gain2", [P, KD], F32, stack)
    M.rows = S.sb("mod_rows", [P, 2, D], F32, stack)
    ada_stage(S, M)
    return M


def peer_stage(S, G, qT, keysT, h2, M):
    nc, a, ps, h = S.nc, S.a, S.ps, S.h
    NK, H, B, Q = PEER_K, PEER_HEADS, 16, 4
    NQ = B // Q
    NG = PICKS // B
    scored, copied, own, exps_in, exps, chosen = (S.sig("u_" + x) for x in ("scored", "copied", "own", "exps_in", "exps", "chosen"))
    staged, dots_out, acted, diags, w_staged, fin, cleared, starts = (
        S.sig("y_" + x) for x in ("staged", "dots_out", "acted", "diags", "w_staged", "fin", "cleared", "starts"))
    arrived = [S.sig(f"y_arrived{q}", pool_dma=True) for q in range(NQ)]
    dotted = [S.sig(f"y_dotted{q}") for q in range(NQ)]
    added = [S.sig(f"y_added{q}") for q in range(NQ)]
    weighed = [S.sig(f"y_weighed{q}") for q in range(NQ)]
    iota = S.const("iota16")
    tables = (a["peer_u_2"][0], a["peer_v_2"][0])
    with ExitStack() as st:
        s = S.sb("peer_s", [P, H, 2, P], F32, st)
        v = S.sb("peer_v16", [P, H, 2, NK], F32, st)
        vi = S.sb("peer_i16", [P, H, 2, NK], U32, st)
        vf = S.sb("peer_f16", [P, H, 2, NK], F32, st)
        cand = S.sb("peer_cand", [P, H, NK, NK], F32, st)
        best = S.sb("peer_best", [P, H, NK], F32, st)
        at = S.sb("peer_at", [P, H, NK], U32, st)
        half = S.sb("peer_half", [P, 2, H, NK], U32, st)
        half_f = S.sb("peer_halff", [P, 2, H, NK], F32, st)
        hit = S.sb("peer_hit", [P, H, NK, NK], F32, st)
        key = S.sb("peer_key", [P, 2, H, NK], F32, st)
        total = S.sb("peer_total", [P, H, 1], F32, st)
        ring = S.sb("peer_ring", [P, B, D], F32, st)
        index = S.sb("peer_index", [P, B], I32, st)
        dots = S.sb("peer_dots", [P, B], F32, st)
        act_all = S.sb("peer_act", [P, PICKS], F32, st)
        wgt = S.sb("peer_wgt", [P, PICKS], F32, st)
        diag = S.sb("peer_diag", [P, B // 2, P], F32, st)
        acc = S.sb("peer_acc", [P, D], F32, st)
        zero = S.sb("peer_zero", [P, BANK], BF16, st)
        with nc.Block("peer") as block:
            @block.gpsimd
            def _(pool):
                for t in range(TT):
                    pool.wait_ge(chosen.sem, chosen.at(t + 1))
                    for phase in range(2):
                        with pool.Fori(0, NG) as i:
                            for q in range(NQ):
                                if phase == 0:
                                    pool.wait_ge(dotted[q].sem, dotted[q].at((NG * t + i) * Q))
                                    pool.wait_ge(added[q].sem, added[q].at(NG * t * Q // 2))
                                    pool.wait_ge(weighed[q].sem, weighed[q].at(NG * t * Q // 2))
                                else:
                                    pool.wait_ge(dotted[q].sem, dotted[q].at(NG * (t + 1) * Q))
                                    pool.wait_ge(added[q].sem, added[q].at((NG * t + i) * (Q // 2)))
                                    pool.wait_ge(weighed[q].sem, weighed[q].at((NG * t + i) * (Q // 2)))
                                settle(pool, S.sig("passed_pool"))
                                sl = slice(q * Q, (q + 1) * Q)
                                nc.gpsimd.tensor_copy(index[:, sl], G.expert[:, t, bass.ds(i * B + q * Q, Q)]).then_inc(staged.sem, 1)
                                pool.wait_ge(staged.sem, staged.at((NG * (2 * t + phase) + i) * NQ + q + 1))
                                settle(pool, S.sig("passed_pool"))
                                for b in range(q * Q, (q + 1) * Q):
                                    pool.indirect_dma_start(out=ring[:, b, :], out_offset=None, in_=tables[phase],
                                                            in_offset=bass.IndirectOffsetOnAxis(ap=index[:, b:b + 1], axis=0),
                                                            ).then_inc(arrived[q].sem, 16)

            @block.tensor
            def _(pe):
                def scores(t):
                    if t:
                        pe.wait_ge(copied.sem, copied.at(4 * t))
                    for hd in range(H):
                        for side in range(2):
                            b = 64 * side
                            nc.tensor.matmul(ps[4 + 2 * side + hd // 4][:, (hd % 4) * P:(hd % 4 + 1) * P],
                                             qT[b:b + 64, hd, t * P:(t + 1) * P], keysT[b:b + 64, :], start=True,
                                             stop=True).then_inc(scored.sem, 1)

                scores(0)
                pe.wait_ge(cleared.sem, cleared.at(1))
                for t in range(TT):
                    if t + 1 < TT:
                        scores(t + 1)
                    pe.wait_ge(fin.sem, fin.at(4 * t))
                    for hf in range(2):
                        nc.tensor.matmul(ps[hf][:, :], zero[:, 0:P], zero[:, :], start=True, stop=False, skip_group_check=True)
                    with pe.Fori(0, NG) as i:
                        n = NG * t + i
                        for q in range(NQ):
                            pe.wait_ge(arrived[q].sem, arrived[q].at(16 * Q * (n + NG * (t + 1) + 1)))
                            for b in range(q * Q + 1, (q + 1) * Q, 2):
                                pe.wait_ge(diags.sem, diags.at((B // 2) * n + b // 2 + 1))
                                for hf in range(2):
                                    last = nc.tensor.matmul(ps[hf][:, :], diag[:, b // 2, :], ring[:, b, hf * 512:(hf + 1) * 512],
                                                            start=False, stop=(b == B - 1), skip_group_check=True)
                                last.then_inc(added[q].sem, 1)

            @block.scalar
            def _(act):
                def take_scores(t):
                    for hh in range(2):
                        act.wait_ge(scored.sem, scored.at(2 * (t * H + 4 * hh + 4)))
                        if t:
                            act.wait_ge(exps_in.sem, exps_in.at(t))
                        for side in range(2):
                            nc.scalar.activation(s[:, 4 * hh:4 * hh + 4, side, :],
                                                 ps[4 + 2 * side + hh][:, :].rearrange("p (h n) -> p h n", h=4),
                                                 ACT.Copy).then_inc(copied.sem, 1)

                def softmax_exp(t):
                    act.wait_ge(exps_in.sem, exps_in.at(t + 1))
                    g = G.gate[:, t, :]
                    nc.scalar.activation(g, g, ACT.Exp).then_inc(exps.sem, 1)

                take_scores(0)
                softmax_exp(0)
                for t in range(TT):
                    if t + 1 < TT:
                        take_scores(t + 1)
                    act.wait_ge(dots_out.sem, dots_out.at(NG * (t + 1)))
                    nc.scalar.activation(act_all[:, :], act_all[:, :], ACT.Gelu).then_inc(acted.sem, 1)
                    act.wait_ge(w_staged.sem, w_staged.at(t + 1))
                    with act.Fori(0, NG) as i:
                        n = NG * t + i
                        for q in range(NQ):
                            act.wait_ge(added[q].sem, added[q].at((Q // 2) * n))
                            for b in range(q * Q + 1, (q + 1) * Q, 2):
                                nc.scalar.activation(diag[:, b // 2, :], S.const("ident"), ACT.Copy,
                                                     scale=wgt[:, bass.ds(i * B + b, 1)]).then_inc(diags.sem, 1)
                    if t + 1 < TT:
                        softmax_exp(t + 1)

            @block.vector
            def _(dve):
                o = Count(own)

                def choose(t):
                    dve.wait_ge(copied.sem, copied.at(4 * (t + 1)))
                    rows = [(hd, side) for hd in range(H) for side in range(2)]
                    for r in range(2):
                        sl = slice(8 * r, 8 * r + 8)
                        for hd, side in rows:
                            nc.vector.max(v[:, hd, side, sl], s[:, hd, side, :]).then_inc(own.sem, o.up())
                        dve.wait_ge(own.sem, o.value())
                        for hd, side in rows:
                            nc.vector.max_index(vi[:, hd, side, sl], v[:, hd, side, sl], s[:, hd, side, :]).then_inc(own.sem, o.up())
                        dve.wait_ge(own.sem, o.value())
                        yield
                        if r == 0:
                            for hd, side in rows:
                                x = s[:, hd, side, :]
                                nc.vector.match_replace(x, v[:, hd, side, sl], x, TAKEN).then_inc(own.sem, o.up())
                            dve.wait_ge(own.sem, o.value())
                    nc.vector.tensor_copy(vf[:, :, :, :], vi[:, :, :, :]).then_inc(own.sem, o.up())
                    nc.vector.tensor_tensor(cand[:, :, :, :], v[:, :, 0, :].unsqueeze(3).broadcast_to([P, H, NK, NK]),
                                            v[:, :, 1, :].unsqueeze(2).broadcast_to([P, H, NK, NK]), ALU.add).then_inc(own.sem, o.up())
                    dve.wait_ge(own.sem, o.value())
                    for r in range(2):
                        sl = slice(8 * r, 8 * r + 8)
                        for hd in range(H):
                            nc.vector.max(best[:, hd, sl], cand[:, hd, :, :].rearrange("p a b -> p (a b)")).then_inc(own.sem, o.up())
                        dve.wait_ge(own.sem, o.value())
                        for hd in range(H):
                            nc.vector.max_index(at[:, hd, sl], best[:, hd, sl],
                                                cand[:, hd, :, :].rearrange("p a b -> p (a b)")).then_inc(own.sem, o.up())
                        dve.wait_ge(own.sem, o.value())
                        if r == 0:
                            for hd in range(H):
                                x = cand[:, hd, :, :].rearrange("p a b -> p (a b)")
                                nc.vector.match_replace(x, best[:, hd, sl], x, TAKEN).then_inc(own.sem, o.up())
                            dve.wait_ge(own.sem, o.value())
                        yield
                    g = G.gate[:, t, :].rearrange("p (h k) -> p h k", h=H)
                    nc.vector.tensor_tensor(g, best[:, :, :], best[:, :, 0:1].broadcast_to([P, H, NK]),
                                            ALU.subtract).then_inc(exps_in.sem, 1)
                    nc.vector.tensor_scalar(half[:, 0, :, :], at[:, :, :], 4, None, ALU.logical_shift_right).then_inc(own.sem, o.up())
                    nc.vector.tensor_scalar(half[:, 1, :, :], at[:, :, :], 15, None, ALU.bitwise_and).then_inc(own.sem, o.up())
                    dve.wait_ge(own.sem, o.value())
                    nc.vector.tensor_copy(half_f[:, :, :, :], half[:, :, :, :]).then_inc(own.sem, o.up())
                    dve.wait_ge(own.sem, o.value())
                    for side in range(2):
                        nc.vector.tensor_tensor(hit[:, :, :, :], half_f[:, side, :, :].unsqueeze(3).broadcast_to([P, H, NK, NK]),
                                                iota.unsqueeze(1).unsqueeze(1).broadcast_to([P, H, NK, NK]),
                                                ALU.is_equal).then_inc(own.sem, o.up())
                        dve.wait_ge(own.sem, o.value())
                        nc.vector.tensor_tensor(hit[:, :, :, :], hit[:, :, :, :],
                                                vf[:, :, side, :].unsqueeze(2).broadcast_to([P, H, NK, NK]),
                                                ALU.mult).then_inc(own.sem, o.up())
                        dve.wait_ge(own.sem, o.value())
                        nc.vector.tensor_reduce(key[:, side, :, :], hit[:, :, :, :], AX.X, ALU.add).then_inc(own.sem, o.up())
                        dve.wait_ge(own.sem, o.value())
                        yield
                    nc.vector.scalar_tensor_tensor(key[:, 0, :, :], key[:, 0, :, :], float(P), key[:, 1, :, :], ALU.mult,
                                                   ALU.add).then_inc(own.sem, o.up())
                    dve.wait_ge(own.sem, o.value())
                    nc.vector.tensor_copy(G.expert[:, t, :].rearrange("p (h k) -> p h k", h=H), key[:, 0, :, :]).then_inc(chosen.sem, 1)
                    yield

                def gates(t):
                    g = G.gate[:, t, :].rearrange("p (h k) -> p h k", h=H)
                    dve.wait_ge(exps.sem, exps.at(t + 1))
                    nc.vector.tensor_reduce(total[:, :, :], g, AX.X, ALU.add).then_inc(own.sem, o.up())
                    dve.wait_ge(own.sem, o.value())
                    nc.vector.reciprocal(total[:, :, :], total[:, :, :]).then_inc(own.sem, o.up())
                    dve.wait_ge(own.sem, o.value())
                    nc.vector.tensor_tensor(g, g, total[:, :, :].broadcast_to([P, H, NK]), ALU.mult).then_inc(own.sem, o.up())
                    dve.wait_ge(own.sem, o.value())

                nc.vector.memset(zero[:, :], 0.0).then_inc(cleared.sem, 1)
                for piece in choose(0):
                    pass
                gates(0)
                for t in range(TT):
                    with dve.Fori(0, NG) as i:
                        n = NG * t + i
                        dve.wait_ge(dots_out.sem, dots_out.at(n))
                        for q in range(NQ):
                            dve.wait_ge(arrived[q].sem, arrived[q].at(16 * Q * (n + NG * t + 1)))
                            for b in range(q * Q, (q + 1) * Q):
                                nc.vector.scalar_tensor_tensor(ring[:, b, :], ring[:, b, :], 1.0, h2[:, t, :], ALU.mult, ALU.mult,
                                                               accum_out=dots[:, b:b + 1]).then_inc(dotted[q].sem, 1)
                        for q in range(NQ):
                            dve.wait_ge(dotted[q].sem, dotted[q].at(Q * (n + 1)))
                        settle(dve, S.sig("passed_dve"))
                        nc.vector.tensor_copy(act_all[:, bass.ds(i * B, B)], dots[:, :]).then_inc(dots_out.sem, 1)
                    dve.wait_ge(acted.sem, acted.at(t + 1))
                    if t:
                        dve.wait_ge(diags.sem, diags.at(PICKS // 2 * t))
                    nc.vector.tensor_tensor(wgt[:, :], act_all[:, :], G.gate[:, t, :], ALU.mult).then_inc(w_staged.sem, 1)
                    nc.vector.memset(acc[:, :], 0.0).then_inc(starts.sem, 1)
                    dve.wait_ge(w_staged.sem, w_staged.at(t + 1))
                    dve.wait_ge(starts.sem, starts.at(t + 1))
                    next_choice = choose(t + 1) if t + 1 < TT else iter(())
                    for i in range(NG):
                        n = NG * t + i
                        for q in range(NQ):
                            dve.wait_ge(arrived[q].sem, arrived[q].at(16 * Q * (n + NG * (t + 1) + 1)))
                            for b in range(q * Q, (q + 1) * Q, 2):
                                if b % Q:
                                    dve.wait_ge(weighed[q].sem, weighed[q].at((Q // 2) * n + 1))
                                elif q or i:
                                    m = n if q else n - 1
                                    dve.wait_ge(weighed[q - 1].sem, weighed[q - 1].at((Q // 2) * (m + 1)))
                                nc.vector.scalar_tensor_tensor(acc[:, :], ring[:, b, :], wgt[:, i * B + b:i * B + b + 1], acc[:, :],
                                                               ALU.mult, ALU.add).then_inc(weighed[q].sem, 1)
                        next(next_choice, None)
                    for q in range(NQ):
                        dve.wait_ge(added[q].sem, added[q].at((Q // 2) * NG * (t + 1)))
                    dve.wait_ge(weighed[NQ - 1].sem, weighed[NQ - 1].at((Q // 2) * NG * (t + 1)))
                    for hf in range(2):
                        sl = slice(hf * 512, (hf + 1) * 512)
                        nc.vector.tensor_tensor(acc[:, sl], acc[:, sl], ps[hf][:, :], ALU.add).then_inc(fin.sem, 1)
                    dve.wait_ge(fin.sem, fin.at(4 * t + 2))
                    nc.vector.tensor_tensor(acc[:, :], acc[:, :], M.rows[:, 1, :], ALU.mult).then_inc(fin.sem, 1)
                    dve.wait_ge(fin.sem, fin.at(4 * t + 3))
                    nc.vector.tensor_tensor(h[:, t, :], h[:, t, :], acc[:, :], ALU.add).then_inc(fin.sem, 1)
                    dve.wait_ge(fin.sem, fin.at(4 * t + 4))
                    if t + 1 < TT:
                        gates(t + 1)


def rows_stage(S, name, dst):
    nc, ps, xT = S.nc, S.ps, S.xT
    turned, copied = S.sig("b_turned"), S.sig("b_copied")
    with nc.Block(name) as block:
        @block.tensor
        def _(pe):
            for t in range(TT):
                for half in range(2):
                    for kk in range(4):
                        last = nc.tensor.transpose(ps[2 * t + half][:, kk * P:(kk + 1) * P],
                                                   xT[:, 4 * half + kk, t * P:(t + 1) * P], S.const("ident"))
                    last.then_inc(turned.sem, 1)

        @block.vector
        def _(dve):
            for t in range(TT):
                for half in range(2):
                    dve.wait_ge(turned.sem, turned.at(2 * t + half + 1))
                    nc.vector.tensor_copy(dst[:, t, half * 512:(half + 1) * 512], ps[2 * t + half][:, :]).then_inc(copied.sem, 1)
    turned.base += 8
    copied.base += 8


def keys_stage(S, keysT):
    nc, a, ps = S.nc, S.a, S.ps
    got, turned, copied = S.sig("k_got"), S.sig("k_turned"), S.sig("k_copied")
    with ExitStack() as st:
        keys = S.sb("peer_keys", [P, P], F32, st)
        with nc.Block("peer_keys") as block:
            @block.sync
            def _(sp):
                sp.dma_start(keys[:, 0:64], a["peer_keys1_2"][0]).then_inc(got.sem, 16)
                sp.dma_start(keys[:, 64:128], a["peer_keys2_2"][0]).then_inc(got.sem, 16)

            @block.tensor
            def _(pe):
                pe.wait_ge(got.sem, got.at(32))
                nc.tensor.transpose(ps[0][:, 0:P], keys[:, :], S.const("ident")).then_inc(turned.sem, 1)

            @block.vector
            def _(dve):
                dve.wait_ge(turned.sem, turned.at(1))
                nc.vector.tensor_copy(keysT[:, :], ps[0][:, 0:P]).then_inc(copied.sem, 1)


def peer(S, M):
    w = S.a["w_peer_q_2"][0]
    norm_stage(S, "norm5", M.gain2[:, :], shift=M.col[:, 3 * KD:4 * KD])
    G = Routing()
    with ExitStack() as st:
        h2 = S.sb("h2_rows", [P, TT, D], F32, st)
        G.expert = S.sb("peer_expert", [P, TT, PICKS], I32, st)
        G.gate = S.sb("peer_gate", [P, TT, PICKS], F32, st)
        rows_stage(S, "h2_rows_back", h2)
        with ExitStack() as st2:
            qT = S.sb("peer_q", [P, KD, T], F32, st2)
            keysT = S.sb("peer_kt", [P, P], F32, st2)
            keys_stage(S, keysT)
            project_stage(S, "proj3", [(w[:, c * 512:(c + 1) * 512], "T", "copy", lambda m, c=c: qT[:, 4 * c + m, :])
                                       for c in range(2)])
            peer_stage(S, G, qT, keysT, h2, M)


def start_stage(S):
    nc, a = S.nc, S.a
    got = S.sig("start")
    with nc.Block("start") as block:
        @block.sync
        def _(sp):
            sp.dma_start(S.h[:, :, :], a["x"][0].rearrange("(t p) d -> p t d", p=P)).then_inc(got.sem, 16)
            with nc.allow_non_contiguous_dma(reason="gains by feature, a few KB"):
                for i, v in enumerate((a["norm_mix_g"][0], a["norm_ffn_g"][0], a["norm_mix_g"][1], a["norm_ffn_g"][1],
                                       a["g_mix_2"][0], a["g_ffn_2"][0])):
                    sp.dma_start(S.gains[:, i, :], v.rearrange("(k p) -> p k", p=P)).then_inc(got.sem, 16)
            sp.wait_ge(got.sem, got.at(16 * 8))

        @block.scalar
        def _(act):
            act.dma_start(S.consts[:, :], a["consts"]).then_inc(got.sem, 16)
    got.base += 16 * 8


def store_stage(S, dst, src):
    nc = S.nc
    done = S.sig("stored")
    with nc.Block(f"store{done.base}") as block:
        @block.sync
        def _(sp):
            sp.dma_start(dst, src).then_inc(done.sem, 16)
            sp.wait_ge(done.sem, done.at(16))
    done.base += 16


def mixer0(S):
    nc, a = S.nc, S.a
    norm_stage(S, "norm0", S.gains[:, 0, :])
    w = a["ab_w_in"][0]
    with ExitStack() as st:
        mix = S.sb("mix0", [P, TT, D], F32, st)
        gate = S.sb("gate0", [P, TT, D], F32, st)
        heads = mix[:, :, :].rearrange("p t (h d) -> p t h d", h=8)
        va = S.sb("va", [P, TT, 512], F32, st)
        vb = S.sb("vb", [P, TT, 512], F32, st)
        with ExitStack() as st2:
            qa = S.sb("qa", [P, 4, T], F32, st2)
            ka = S.sb("ka", [P, 4, T], F32, st2)
            qkb = S.sb("qkb", [P, 4, T], F32, st2)
            ba = S.sb("ba", [16, T], F32, st2)
            project_stage(S, "proj0", [
                (w[:, 0:512], "T", "copy", lambda m: qa[:, m, :]),
                (w[:, 512:1024], "T", P ** -0.5, lambda m: ka[:, m, :]),
                (w[:, 3584:3600], "T", "copy", lambda m: ba[:, :]),
                (w[:, 2048:2304], "T", 64 ** -0.5, lambda m: qkb[:, m, :]),
                (w[:, 2304:2560], "T", "copy", lambda m: qkb[:, 2 + m, :]),
                (w[:, 1024:1536], "tok", "copy", lambda t: va[:, t, :]),
                (w[:, 2560:3072], "tok", "copy", lambda t: vb[:, t, :]),
                (w[:, 1536:2048], "tok", "silu", lambda t: gate[:, t, 0:512]),
                (w[:, 3072:3584], "tok", "silu", lambda t: gate[:, t, 512:1024])])
            with ExitStack() as st3:
                cos = S.sb("cos_r", [P, T], F32, st3)
                sin = S.sb("sin_r", [P, T], F32, st3)
                angle_stage(S, "angles0", a["positions"][0], [S.const("freq")[:, 0:1]], [(cos[:, :], sin[:, :])])
                rotate_stage(S, "rotary0", [(x[:, m, :], S.const("swap_ret"), cos, sin) for x in (qa, ka) for m in range(4)])
                retention_stage(S, qa, ka, va, heads)
            with ExitStack() as st3:
                logf = S.sb("logf0", [P, 2, T], F32, st3)
                wa = S.sb("wa", [16, 256], F32, st3)
                bias = S.sb("ba2", [P, 2], F32, st3)
                load_stage(S, "load_gla", [(wa[:, :], a["gla_w_a2"][0]),
                                           (bias[:, :], a["gla_b_a2"][0].rearrange("(k p) -> p k", p=P))])
                log_gate_stage(S, "log_alpha", [(wa[:, m * P:(m + 1) * P], ba[:, :], bias[:, m:m + 1], logf[:, m, :])
                                                for m in range(2)], 1.0 / 16.0)
                gated_stage(S, "gla", 2, 2, lambda p: qkb[:, p, :], lambda p: qkb[:, 2 + p, :],
                            lambda p: logf[:, p, :], lambda hd, c: vb[:, c, hd * P:(hd + 1) * P],
                            lambda hd: heads[:, :, 4 + hd, :], 4)
        head_norm_stage(S, "headnorm0", mix, 128,
                        [(i * P, a["ret_norm_g"][0] if i < 4 else a["gla_norm_g"][0]) for i in range(8)], gate)
        add_projection(S, "out0", a["ab_w_out"][0])


def load_stage(S, name, pairs):
    nc = S.nc
    got = S.sig("loads")
    with nc.Block(name) as block:
        @block.sync
        def _(sp):
            with nc.allow_non_contiguous_dma(reason="a few KB of vectors"):
                for dst, src in pairs:
                    sp.dma_start(dst, src).then_inc(got.sem, 16)
            sp.wait_ge(got.sem, got.at(16 * len(pairs)))
    got.base += 16 * len(pairs)


def add_projection(S, name, w):
    project_stage(S, name, [(w[:, c * 512:(c + 1) * 512], "tok", "add", lambda t, c=c: S.h[:, t, c * 512:(c + 1) * 512])
                            for c in range(2)])


def run_stages(S, out):
    S.gains = S.sb("gains", [P, 6, KD])
    start_stage(S)
    mixer0(S)
    norm_stage(S, "norm1", S.gains[:, 1, :])
    ffn_swiglu(S)
    mixer1(S)
    for prefix in ("t_", "h_", "q_", "s_"):
        S.retire(prefix)
    moe1(S)
    row_norm_stage(S, "final1", S.a["final_norm_g"])
    M = modulation(S, S.stack)
    attention2(S, M)
    for prefix in ("d_", "l_"):
        S.retire(prefix)
    peer(S, M)
    row_norm_stage(S, "final2", S.a["g_final_2"])
    store_stage(S, out[0].rearrange("(t p) d -> p t d", p=P), S.h[:, :, :])


def program(nc, a, out):
    with ExitStack() as stack:
        S = Stages(nc, stack)
        S.where, n_const = const_layout()
        S.consts = S.sb("consts", [P, n_const])
        S.h = S.sb("h", [P, TT, D])
        S.xT = S.sb("xT", [P, KD, T])
        S.ps = [stack.enter_context(nc.psum_tensor(f"bank{b}", [P, BANK], F32)) for b in range(8)]
        S.a = a
        for name in SIGNALS:
            S.signals[name] = Signal(nc, stack, name, False)
        nc.all_engine_barrier()
        run_stages(S, out)


_INS = ['x', 'positions', 'norm_mix_g', 'norm_ffn_g', 'final_norm_g', 'ab_w_in', 'gla_w_a2', 'gla_b_a2',
        'ret_norm_g', 'gla_norm_g', 'ab_w_out', 'ffn_w_gate', 'ffn_w_up', 'ffn_w_down', 'hgrn_lb_logits',
        'c_w_in', 'hgrn_norm_g', 'c_w_out', 'moe_router', 'moe_w_gate', 'moe_w_up', 'moe_w_down', 'c_2',
        'positions_2', 'w_ada_2', 'b_ada_2', 'g_mix_2', 'w_in_2', 'g_kv_2', 'w_uk_2', 'w_uv_2', 'b_forget_2',
        'g_out_a_2', 'g_out_b_2', 'w_out_2', 'g_ffn_2', 'w_peer_q_2', 'peer_keys1_2', 'peer_keys2_2',
        'peer_u_2', 'peer_v_2', 'g_final_2']


def kernel(**inputs):
    import numpy as _np
    import concourse.bacc as _bacc
    from concourse import mybir as _mybir
    from concourse.bass_utils import run_bass_kernel_spmd as _run

    nc = _bacc.Bacc("TRN2", target_bir_lowering=False, num_devices=1)
    arrays, args = {}, {}
    for name in _INS:
        a = _np.ascontiguousarray(inputs[name])
        arrays[f"in_{name}_dram"] = a
        args[name] = nc.dram_tensor(f"in_{name}_dram", a.shape, _mybir.dt.from_np(a.dtype), kind="ExternalInput").ap()
    consts = const_values()
    arrays["in_consts_dram"] = consts
    args["consts"] = nc.dram_tensor("in_consts_dram", consts.shape, _mybir.dt.from_np(consts.dtype), kind="ExternalInput").ap()
    out = nc.dram_tensor("out_0_dram", (1, T, D), _mybir.dt.from_np(_np.dtype("float32")), kind="ExternalOutput").ap()
    program(nc, args, out)
    r = _run(nc, [arrays], core_ids=[0])
    return r.results[0]["out_0_dram"]
```
